# Optimizing a Trainium2 kernel written in Bass

```python
import math
import jax, jax.numpy as jnp
from jax import lax
import numpy as np

D_MODEL = 1024
BATCH = 1
SEQ = 256
DEPTH = 2

CHUNK = 64
N_A_LAYERS = DEPTH // 2
N_B_LAYERS = DEPTH - N_A_LAYERS

RWKV_HEAD = 64
RWKV_HEADS = D_MODEL // RWKV_HEAD
DECAY_LORA = 64
A_LORA = 64
GATE_LORA = 160
LNX_EPS = 64e-5

DA_HEAD_DIM = 64
DA_HEADS = D_MODEL // (2 * DA_HEAD_DIM)
DA_V_DIM = 2 * DA_HEAD_DIM
ROPE_DIM = DA_HEAD_DIM // 4
ROPE_THETA = 500000.0
Q_BLOCK = 128
SUBLN_EPS = 1e-5

D_FF = ((8 * D_MODEL + 3 * 256 - 1) // (3 * 256)) * 256

NORM_EPS = 1e-6


def rms_norm(x, g, eps=NORM_EPS):
    xf = x.astype(jnp.float32)
    y = xf * lax.rsqrt(jnp.mean(xf * xf, axis=-1, keepdims=True) + eps)
    return (y * g.astype(jnp.float32)).astype(x.dtype)

def swiglu_ffn(h, w_gu, w_down):
    gate, up = jnp.split(h @ w_gu, 2, axis=-1)
    return (jax.nn.silu(gate) * up) @ w_down

def partial_rope(x, pos):
    half = ROPE_DIM // 2
    inv = jnp.power(ROPE_THETA, -jnp.arange(0, ROPE_DIM, 2, dtype=jnp.float32) / ROPE_DIM)
    ang = pos[:, None] * inv[None, :]
    cos = jnp.cos(ang)[None, :, None, :]
    sin = jnp.sin(ang)[None, :, None, :]
    xf = x.astype(jnp.float32)
    x1 = xf[..., :half]
    x2 = xf[..., half:ROPE_DIM]
    out = jnp.concatenate([x1 * cos - x2 * sin, x2 * cos + x1 * sin, xf[..., ROPE_DIM:]], axis=-1)
    return out.astype(x.dtype)

def rwkv7_time_mix(h, mu, w_r, w_k, w_v, w_o, w0, w1, w2, a0, a1, a2, g1, g2,
                   k_k, k_a, r_k, lnx_w, lnx_b):
    B, S, D = h.shape
    H, N = RWKV_HEADS, RWKV_HEAD
    h_prev = jnp.pad(h, ((0, 0), (1, 0), (0, 0)))[:, :-1]
    hh = h_prev - h
    xr = h + hh * mu[0]
    xw = h + hh * mu[1]
    xk = h + hh * mu[2]
    xv = h + hh * mu[3]
    xa = h + hh * mu[4]
    xg = h + hh * mu[5]

    r = xr @ w_r
    w = -jax.nn.softplus(-(w0 + jnp.tanh(xw @ w1) @ w2)) - 0.5
    k = xk @ w_k
    v = xv @ w_v
    a = jax.nn.sigmoid(a0 + (xa @ a1) @ a2)
    g = jax.nn.sigmoid(xg @ g1) @ g2

    kk = (k * k_k).astype(jnp.float32).reshape(B, S, H, N)
    kk = kk / jnp.maximum(jnp.sqrt(jnp.sum(kk * kk, axis=-1, keepdims=True)), 1e-12)
    k = k * (1.0 + (a - 1.0) * k_a)

    def heads(t):
        return t.astype(jnp.float32).reshape(B, S, H, N)

    r_h, k_h, v_h, a_h = heads(r), heads(k), heads(v), heads(a)
    decay = jnp.exp(-jnp.exp(heads(w)))
    a_vec = -kk
    b_vec = kk * a_h

    def time_major(t):
        return t.transpose(1, 0, 2, 3)

    def step(state, inp):
        r_t, w_t, k_t, v_t, a_t, b_t = inp
        sa = jnp.einsum('bhvk,bhk->bhv', state, a_t)
        state = (state * w_t[:, :, None, :]
                 + sa[..., None] * b_t[:, :, None, :]
                 + v_t[..., None] * k_t[:, :, None, :])
        y_t = jnp.einsum('bhvk,bhk->bhv', state, r_t)
        return state, y_t

    state0 = jnp.zeros((B, H, N, N), jnp.float32)
    _, y = lax.scan(step, state0, (time_major(r_h), time_major(decay), time_major(k_h),
                                   time_major(v_h), time_major(a_vec), time_major(b_vec)))
    y = y.transpose(1, 0, 2, 3)

    mean = jnp.mean(y, axis=-1, keepdims=True)
    var = jnp.mean(jnp.square(y - mean), axis=-1, keepdims=True)
    y = ((y - mean) * lax.rsqrt(var + LNX_EPS)).reshape(B, S, D)
    y = y * lnx_w.astype(jnp.float32) + lnx_b.astype(jnp.float32)
    bonus = jnp.sum(r_h * k_h * r_k.astype(jnp.float32), axis=-1, keepdims=True) * v_h
    y = y + bonus.reshape(B, S, D)
    return (y * g.astype(jnp.float32)).astype(h.dtype) @ w_o

def shared_kv(x, kv_g, kv_w, k_norm_g, pos):
    B, S, _ = x.shape
    hkv = rms_norm(x, kv_g)
    k, v = jnp.split(hkv @ kv_w, 2, axis=-1)
    k = k.reshape(B, S, 2 * DA_HEADS, DA_HEAD_DIM)
    k = partial_rope(rms_norm(k, k_norm_g), pos)
    v = v.reshape(B, S, DA_HEADS, DA_V_DIM)
    return k, v

def diff_attention(h, k, v, pos, w_q, q_norm_g, lam_q1, lam_k1, lam_q2, lam_k2,
                   subln_g, w_o, lam_init):
    B, S, D = h.shape
    H = DA_HEADS
    q = (h @ w_q).reshape(B, S, 2 * H, DA_HEAD_DIM)
    q = partial_rope(rms_norm(q, q_norm_g), pos)
    f32 = jnp.float32
    lam = (jnp.exp(jnp.sum(lam_q1.astype(f32) * lam_k1.astype(f32)))
           - jnp.exp(jnp.sum(lam_q2.astype(f32) * lam_k2.astype(f32))) + lam_init)
    scale = DA_HEAD_DIM ** -0.5
    k_chunk = jnp.arange(S) // CHUNK
    n_blocks = S // Q_BLOCK

    def block(i):
        start = i * Q_BLOCK
        q_blk = lax.dynamic_slice_in_dim(q, start, Q_BLOCK, axis=1)
        s = jnp.einsum('bqhd,bkhd->bhqk', q_blk, k).astype(f32) * scale
        q_chunk = (start + jnp.arange(Q_BLOCK)) // CHUNK
        allowed = k_chunk[None, :] <= q_chunk[:, None]
        s = jnp.where(allowed[None, None], s, -jnp.inf)
        p = jax.nn.softmax(s, axis=-1).reshape(B, H, 2, Q_BLOCK, S)
        p = p[:, :, 0] - lam * p[:, :, 1]
        return jnp.einsum('bhqk,bkhe->bqhe', p.astype(v.dtype), v)

    o = lax.map(block, jnp.arange(n_blocks))
    o = o.transpose(1, 0, 2, 3, 4).reshape(B, S, H, DA_V_DIM)
    o = rms_norm(o, subln_g, eps=SUBLN_EPS) * (1.0 - lam_init)
    return o.reshape(B, S, D) @ w_o

def first_inputs(seed: int = 0) -> dict:
    key = jax.random.key(seed)
    ks = iter(jax.random.split(key, 48))
    D, F, NA, NB = D_MODEL, D_FF, N_A_LAYERS, N_B_LAYERS
    nrm = lambda shape, s: jax.random.normal(next(ks), shape, jnp.float32) * s
    gain = lambda shape: 1.0 + 0.02 * jax.random.normal(next(ks), shape, jnp.float32)
    inp = {}
    inp["x"] = nrm((BATCH, SEQ, D), 1.0)
    inp["g_mix"] = gain((DEPTH, D))
    inp["g_ffn"] = gain((DEPTH, D))
    inp["rw_mu"] = jax.random.uniform(next(ks), (NA, 6, D), jnp.float32)
    inp["rw_w_r"] = nrm((NA, D, D), D ** -0.5)
    inp["rw_w_k"] = nrm((NA, D, D), D ** -0.5)
    inp["rw_w_v"] = nrm((NA, D, D), D ** -0.5)
    inp["rw_w_o"] = nrm((NA, D, D), D ** -0.5)
    inp["rw_w0"] = jax.random.uniform(next(ks), (NA, D), jnp.float32, -6.0, -1.0)
    inp["rw_w1"] = nrm((NA, D, DECAY_LORA), D ** -0.5)
    inp["rw_w2"] = nrm((NA, DECAY_LORA, D), 0.5 * DECAY_LORA ** -0.5)
    inp["rw_a0"] = nrm((NA, D), 0.1)
    inp["rw_a1"] = nrm((NA, D, A_LORA), D ** -0.5)
    inp["rw_a2"] = nrm((NA, A_LORA, D), A_LORA ** -0.5)
    inp["rw_g1"] = nrm((NA, D, GATE_LORA), D ** -0.5)
    inp["rw_g2"] = nrm((NA, GATE_LORA, D), GATE_LORA ** -0.5)
    inp["rw_k_k"] = 0.85 + nrm((NA, D), 0.05)
    inp["rw_k_a"] = 1.0 + nrm((NA, D), 0.05)
    inp["rw_r_k"] = nrm((NA, RWKV_HEADS, RWKV_HEAD), 0.1)
    inp["rw_lnx_w"] = gain((NA, D))
    inp["rw_lnx_b"] = nrm((NA, D), 0.02)
    inp["kv_g"] = gain((D,))
    inp["kv_w"] = nrm((D, 2 * D), D ** -0.5)
    inp["k_norm_g"] = gain((DA_HEAD_DIM,))
    inp["da_w_q"] = nrm((NB, D, D), D ** -0.5)
    inp["da_q_norm_g"] = gain((NB, DA_HEAD_DIM))
    inp["da_lam_q1"] = nrm((NB, DA_HEAD_DIM), 0.1)
    inp["da_lam_k1"] = nrm((NB, DA_HEAD_DIM), 0.1)
    inp["da_lam_q2"] = nrm((NB, DA_HEAD_DIM), 0.1)
    inp["da_lam_k2"] = nrm((NB, DA_HEAD_DIM), 0.1)
    inp["da_subln_g"] = gain((NB, DA_V_DIM))
    inp["da_w_o"] = nrm((NB, D, D), D ** -0.5)
    inp["ffn_w_gu"] = nrm((DEPTH, D, 2 * F), D ** -0.5)
    inp["ffn_w_down"] = nrm((DEPTH, F, D), F ** -0.5)
    return inp

def first_block(x, g_mix, g_ffn, rw_mu, rw_w_r, rw_w_k, rw_w_v, rw_w_o, rw_w0, rw_w1, rw_w2,
              rw_a0, rw_a1, rw_a2, rw_g1, rw_g2, rw_k_k, rw_k_a, rw_r_k, rw_lnx_w, rw_lnx_b,
              kv_g, kv_w, k_norm_g, da_w_q, da_q_norm_g, da_lam_q1, da_lam_k1, da_lam_q2,
              da_lam_k2, da_subln_g, da_w_o, ffn_w_gu, ffn_w_down):
    S = x.shape[1]
    pos = jnp.arange(S, dtype=jnp.float32)
    k_sh, v_sh = None, None
    for layer in range(DEPTH):
        if layer < N_A_LAYERS:
            i = layer
            h = rms_norm(x, g_mix[layer])
            x = x + rwkv7_time_mix(h, rw_mu[i], rw_w_r[i], rw_w_k[i], rw_w_v[i], rw_w_o[i],
                                   rw_w0[i], rw_w1[i], rw_w2[i], rw_a0[i], rw_a1[i], rw_a2[i],
                                   rw_g1[i], rw_g2[i], rw_k_k[i], rw_k_a[i], rw_r_k[i],
                                   rw_lnx_w[i], rw_lnx_b[i])
        else:
            j = layer - N_A_LAYERS
            if j == 0:
                k_sh, v_sh = shared_kv(x, kv_g, kv_w, k_norm_g, pos)
            lam_init = 0.8 - 0.6 * math.exp(-0.3 * layer)
            h = rms_norm(x, g_mix[layer])
            x = x + diff_attention(h, k_sh, v_sh, pos, da_w_q[j], da_q_norm_g[j],
                                   da_lam_q1[j], da_lam_k1[j], da_lam_q2[j], da_lam_k2[j],
                                   da_subln_g[j], da_w_o[j], lam_init)
        h = rms_norm(x, g_ffn[layer])
        x = x + swiglu_ffn(h, ffn_w_gu[layer], ffn_w_down[layer])
    return x


DEPTH_2 = 1

GRID_W = 64
CTX_LEN = 256
HG_DIM = 128
HG_WIDTH = D_MODEL // 2
HG_HEADS = HG_WIDTH // HG_DIM
MLP_WIDTH = D_MODEL - HG_WIDTH
MLP_HEADS = 4
MLP_DIM = MLP_WIDTH // MLP_HEADS
MLP_CHUNK = 128
SCAN_CHUNK = 32
MIX_WIDTH = HG_WIDTH + MLP_WIDTH
PROJ_WIDTH = 5 * HG_WIDTH + 2 * MLP_WIDTH
D_FF_2 = 2816
CONV_W = 3
EPS = 1e-6


def rmsnorm(x, gain):
    xf = x.astype(jnp.float32)
    y = xf * lax.rsqrt(jnp.mean(xf * xf, axis=-1, keepdims=True) + EPS)
    return (y * gain.astype(jnp.float32)).astype(x.dtype)

def layernorm(x, gain, bias):
    xf = x.astype(jnp.float32)
    mu = jnp.mean(xf, axis=-1, keepdims=True)
    var = jnp.mean(jnp.square(xf - mu), axis=-1, keepdims=True)
    y = (xf - mu) * lax.rsqrt(var + EPS) * gain.astype(jnp.float32) + bias.astype(jnp.float32)
    return y.astype(x.dtype)

def modulate(h, shift, scale):
    return h * (1.0 + scale) + shift

def split_heads(a, n_heads):
    b, t, w = a.shape
    return a.reshape(b, t, n_heads, w // n_heads).transpose(0, 2, 1, 3)

def merge_heads(a):
    b, h, t, d = a.shape
    return a.transpose(0, 2, 1, 3).reshape(b, t, h * d)

def flip_t(a):
    return jnp.flip(a, axis=2)

def lower_bounds(logits):
    cum = jnp.cumsum(jax.nn.softmax(logits.astype(jnp.float32), axis=0), axis=0)
    return cum - cum[0:1]

def forget_gate(f_logit, lb, first):
    f = f_logit.astype(jnp.float32)
    if first:
        return jax.nn.log_sigmoid(f), jax.nn.sigmoid(-f)
    gate = lb + (1.0 - lb) * jax.nn.sigmoid(f)
    return jnp.log(gate), 1.0 - gate

def hgrn2_gates(p, lb_f, lb_b, first):
    w = HG_WIDTH
    logf_f, k_f = forget_gate(p[..., :w], lb_f, first)
    logf_b, k_b = forget_gate(p[..., w:2 * w], lb_b, first)
    v = p[..., 2 * w:3 * w].astype(jnp.float32)
    return tuple(split_heads(a, HG_HEADS) for a in (logf_f, k_f, logf_b, k_b, v))

def advance_state(h, k, v, b):
    b_last = b[:, :, -1:, :]
    return (jnp.exp(b_last)[:, :, 0, :, None] * h
            + jnp.einsum('bhsk,bhsv->bhkv', k * jnp.exp(b_last - b), v))

def chunk_gla(q, k, v, log_f, h0):
    b_, h_, t, _ = q.shape
    n = t // SCAN_CHUNK

    def to_chunks(a):
        return jnp.moveaxis(a.reshape(b_, h_, n, SCAN_CHUNK, a.shape[-1]), 2, 0)

    mask = jnp.tril(jnp.ones((SCAN_CHUNK, SCAN_CHUNK), dtype=bool))[:, :, None]

    def step(h, blk):
        qc, kc, vc, gc = blk
        b = jnp.cumsum(gc, axis=2)
        o_inter = jnp.einsum('bhtk,bhkv->bhtv', qc * jnp.exp(b), h)
        diff = b[:, :, :, None, :] - b[:, :, None, :, :]
        decay = jnp.where(mask, jnp.exp(jnp.where(mask, diff, 0.0)), 0.0)
        scores = jnp.einsum('bhtk,bhsk,bhtsk->bhts', qc, kc, decay)
        o = o_inter + jnp.einsum('bhts,bhsv->bhtv', scores, vc)
        return advance_state(h, kc, vc, b), o

    h_end, o = lax.scan(step, h0, (to_chunks(q), to_chunks(k), to_chunks(v), to_chunks(log_f)))
    o = jnp.moveaxis(o, 0, 2).reshape(b_, h_, t, v.shape[-1])
    return o, h_end

def chunk_sgu(u, v, ln_g, ln_b, w_s, b_s):
    bsz, t, _ = u.shape
    n = t // MLP_CHUNK
    u = jax.nn.gelu(u, approximate=False).reshape(bsz, n, MLP_CHUNK, MLP_HEADS, MLP_DIM)
    v = jax.nn.gelu(v, approximate=False).reshape(bsz, n, MLP_CHUNK, MLP_HEADS, MLP_DIM)
    v = layernorm(v, ln_g.reshape(MLP_HEADS, MLP_DIM), ln_b.reshape(MLP_HEADS, MLP_DIM))
    z = jnp.einsum('hpq,bnqhc->bnphc', w_s.astype(v.dtype), v) + jnp.transpose(b_s)[None, None, :, :, None]
    return (u * z).reshape(bsz, t, MLP_WIDTH)

def token_mixers(p, lb_f, lb_b, first, h0_f, h0_b, hg_gain, sgu_g, sgu_b, w_s, b_s):
    w = HG_WIDTH
    logf_f, k_f, logf_b, k_b, v = hgrn2_gates(p, lb_f, lb_b, first)
    q = split_heads(jax.nn.silu(p[..., 3 * w:4 * w].astype(jnp.float32)), HG_HEADS) * (HG_DIM ** -0.5)
    o_f, h_f = chunk_gla(q, k_f, v, logf_f, h0_f)
    o_b, h_b = chunk_gla(flip_t(q), flip_t(k_b), flip_t(v), flip_t(logf_b), h0_b)
    o = rmsnorm(o_f + flip_t(o_b), hg_gain.reshape(HG_HEADS, 1, HG_DIM))
    o_hg = merge_heads(o).astype(p.dtype) * jax.nn.silu(p[..., 4 * w:5 * w])
    o_mlp = chunk_sgu(p[..., 5 * w:5 * w + MLP_WIDTH], p[..., 5 * w + MLP_WIDTH:], sgu_g, sgu_b, w_s, b_s)
    return jnp.concatenate([o_hg, o_mlp], axis=-1), h_f, h_b

def conv_ffn(h, w_up, taps, conv_b, w_down, rows):
    a, g = jnp.split(h @ w_up, 2, axis=-1)
    bsz, t, f = g.shape
    if rows is None:
        g2, tp = g.reshape(bsz, 1, t, f), taps[1:2]
    else:
        g2, tp = g.reshape(bsz, rows, GRID_W, f), taps
    gc = lax.conv_general_dilated(g2, tp[:, :, None, :].astype(g.dtype), (1, 1), 'SAME',
                                  dimension_numbers=('NHWC', 'HWIO', 'NHWC'), feature_group_count=f)
    gc = gc.reshape(bsz, t, f) + conv_b
    return (a * jax.nn.gelu(gc, approximate=False)) @ w_down

def second_inputs(seed: int = 0) -> dict:
    key = jax.random.key(seed)
    ks = jax.random.split(key, 22)
    nrm = jax.random.normal
    L, D, F = DEPTH_2, D_MODEL, D_FF_2
    return {
        "x": nrm(ks[0], (BATCH, SEQ, D), jnp.float32),
        "c": nrm(ks[1], (BATCH, D), jnp.float32),
        "ctx": nrm(ks[2], (BATCH, CTX_LEN, D), jnp.float32),
        "c_ctx": nrm(ks[3], (D,), jnp.float32),
        "w_ada": nrm(ks[4], (L, D, 6 * D), jnp.float32) * (0.5 * D ** -0.5),
        "b_ada": nrm(ks[5], (L, 6 * D), jnp.float32) * 0.02,
        "norm_mix": 1.0 + 0.1 * nrm(ks[6], (L, D), jnp.float32),
        "norm_ffn": 1.0 + 0.1 * nrm(ks[7], (L, D), jnp.float32),
        "w_in": nrm(ks[8], (L, D, PROJ_WIDTH), jnp.float32) * D ** -0.5,
        "lb_logits_fwd": nrm(ks[9], (L, HG_WIDTH), jnp.float32),
        "lb_logits_bwd": nrm(ks[10], (L, HG_WIDTH), jnp.float32),
        "hg_norm": 1.0 + 0.1 * nrm(ks[11], (L, HG_WIDTH), jnp.float32),
        "sgu_norm_g": 1.0 + 0.1 * nrm(ks[12], (L, MLP_WIDTH), jnp.float32),
        "sgu_norm_b": 0.02 * nrm(ks[13], (L, MLP_WIDTH), jnp.float32),
        "w_spatial": nrm(ks[14], (L, MLP_HEADS, MLP_CHUNK, MLP_CHUNK), jnp.float32) * MLP_CHUNK ** -0.5,
        "b_spatial": 1.0 + 0.1 * nrm(ks[15], (L, MLP_HEADS, MLP_CHUNK), jnp.float32),
        "w_out": nrm(ks[16], (L, MIX_WIDTH, D), jnp.float32) * MIX_WIDTH ** -0.5,
        "w_up": nrm(ks[17], (L, D, 2 * F), jnp.float32) * D ** -0.5,
        "conv_w": nrm(ks[18], (L, CONV_W, CONV_W, F), jnp.float32) / CONV_W,
        "conv_b": 0.02 * nrm(ks[19], (L, F), jnp.float32),
        "w_down": nrm(ks[20], (L, F, D), jnp.float32) * F ** -0.5,
        "norm_final": 1.0 + 0.1 * nrm(ks[21], (D,), jnp.float32),
    }

def second_block(x, c, ctx, c_ctx, w_ada, b_ada, norm_mix, norm_ffn, w_in, lb_logits_fwd, lb_logits_bwd,
              hg_norm, sgu_norm_g, sgu_norm_b, w_spatial, b_spatial, w_out, w_up, conv_w, conv_b, w_down,
              norm_final):
    w = HG_WIDTH
    rows = x.shape[1] // GRID_W
    bsz = x.shape[0]
    lb_f_all = lower_bounds(lb_logits_fwd)
    lb_b_all = lower_bounds(lb_logits_bwd)
    ada = jnp.einsum('bd,lde->lbe', jax.nn.silu(c), w_ada) + b_ada[:, None, :]
    ada_c = jnp.einsum('d,lde->le', jax.nn.silu(c_ctx), w_ada) + b_ada
    h0 = jnp.zeros((bsz, HG_HEADS, HG_DIM, HG_DIM), jnp.float32)
    xc = ctx
    for l in range(DEPTH_2):
        first, last = l == 0, l == DEPTH_2 - 1
        sh1, sc1, g1, sh2, sc2, g2 = (m[:, None, :] for m in jnp.split(ada[l], 6, axis=-1))
        csh1, csc1, cg1, csh2, csc2, cg2 = jnp.split(ada_c[l], 6, axis=-1)
        lb_f, lb_b = lb_f_all[l], lb_b_all[l]
        mix_args = (hg_norm[l], sgu_norm_g[l], sgu_norm_b[l], w_spatial[l], b_spatial[l])

        hc = modulate(rmsnorm(xc, norm_mix[l]), csh1, csc1)
        if last:
            logf_f, k_f, logf_b, k_b, vc = hgrn2_gates(hc @ w_in[l][:, :3 * w], lb_f, lb_b, first)
            hf_c = advance_state(h0, k_f, vc, jnp.cumsum(logf_f, axis=2))
            hb_c = advance_state(h0, flip_t(k_b), flip_t(vc), jnp.cumsum(flip_t(logf_b), axis=2))
        else:
            oc, hf_c, hb_c = token_mixers(hc @ w_in[l], lb_f, lb_b, first, h0, h0, *mix_args)

        h = modulate(rmsnorm(x, norm_mix[l]), sh1, sc1)
        o, _, _ = token_mixers(h @ w_in[l], lb_f, lb_b, first, hf_c, hb_c, *mix_args)
        x = x + g1 * (o @ w_out[l])
        h2 = modulate(rmsnorm(x, norm_ffn[l]), sh2, sc2)
        x = x + g2 * conv_ffn(h2, w_up[l], conv_w[l], conv_b[l], w_down[l], rows)

        if not last:
            xc = xc + cg1 * (oc @ w_out[l])
            hc2 = modulate(rmsnorm(xc, norm_ffn[l]), csh2, csc2)
            xc = xc + cg2 * conv_ffn(hc2, w_up[l], conv_w[l], conv_b[l], w_down[l], None)
    return rmsnorm(x, norm_final)


def setup_inputs(seed=0):
    out = dict(first_inputs(seed))
    for name, value in second_inputs(seed + 1).items():
        if name != "x":
            out[name + "_2"] = value
    return out


def reference(
    x, g_mix, g_ffn, rw_mu, rw_w_r, rw_w_k, rw_w_v, rw_w_o, rw_w0, rw_w1, rw_w2, rw_a0, rw_a1,
    rw_a2, rw_g1, rw_g2, rw_k_k, rw_k_a, rw_r_k, rw_lnx_w, rw_lnx_b, kv_g, kv_w, k_norm_g,
    da_w_q, da_q_norm_g, da_lam_q1, da_lam_k1, da_lam_q2, da_lam_k2, da_subln_g, da_w_o,
    ffn_w_gu, ffn_w_down, c_2, ctx_2, c_ctx_2, w_ada_2, b_ada_2, norm_mix_2, norm_ffn_2, w_in_2,
    lb_logits_fwd_2, lb_logits_bwd_2, hg_norm_2, sgu_norm_g_2, sgu_norm_b_2, w_spatial_2,
    b_spatial_2, w_out_2, w_up_2, conv_w_2, conv_b_2, w_down_2, norm_final_2,
):
    x = first_block(
        x, g_mix, g_ffn, rw_mu, rw_w_r, rw_w_k, rw_w_v, rw_w_o, rw_w0, rw_w1, rw_w2, rw_a0,
        rw_a1, rw_a2, rw_g1, rw_g2, rw_k_k, rw_k_a, rw_r_k, rw_lnx_w, rw_lnx_b, kv_g, kv_w,
        k_norm_g, da_w_q, da_q_norm_g, da_lam_q1, da_lam_k1, da_lam_q2, da_lam_k2, da_subln_g,
        da_w_o, ffn_w_gu, ffn_w_down,
    )
    return second_block(
        x, c_2, ctx_2, c_ctx_2, w_ada_2, b_ada_2, norm_mix_2, norm_ffn_2, w_in_2,
        lb_logits_fwd_2, lb_logits_bwd_2, hg_norm_2, sgu_norm_g_2, sgu_norm_b_2, w_spatial_2,
        b_spatial_2, w_out_2, w_up_2, conv_w_2, conv_b_2, w_down_2, norm_final_2,
    )


_drawn_inputs = setup_inputs


def setup_inputs(seed=0):
    import zlib

    import numpy as np

    out = dict(_drawn_inputs(seed))
    spreads = {}
    factors = {'rw_w1': 3.411,
     'rw_w2': 3.428,
     'rw_lnx_w': 4.044,
     'kv_g': 3.62,
     'k_norm_g': 5.536,
     'da_q_norm_g': 5.339,
     'da_lam_q2': 3.422,
     'da_subln_g': 5.789,
     'ctx_2': 8.0,
     'c_ctx_2': 8.0,
     'b_ada_2': 3.47,
     'norm_mix_2': 2.689,
     'norm_ffn_2': 2.844,
     'hg_norm_2': 6.037,
     'sgu_norm_g_2': 4.995,
     'sgu_norm_b_2': 8.0,
     'b_spatial_2': 5.621,
     'conv_b_2': 8.0}
    for name, (base, spread) in spreads.items():
        noise = np.random.default_rng([zlib.crc32(name.encode()), seed]).standard_normal(out[name].shape)
        drawn = base * np.exp(spread * noise) if base else spread * noise
        out[name] = __import__('jax').numpy.asarray(drawn.astype(out[name].dtype))
    for name, factor in factors.items():
        out[name] = (out[name] * factor).astype(out[name].dtype)
    return out
```

```python
import concourse.bass as bass
from concourse import mybir
from contextlib import ExitStack
import math
import numpy as np

F32 = mybir.dt.float32
I32 = mybir.dt.int32
ALU = mybir.AluOpType
ACT = mybir.ActivationFunctionType
AXX = mybir.AxisListType.X

P = 128
D = 1024
KT = D // P
S = 256
TT = S // P
CH = 64
FF = 2816
FT = FF // P
LEV = 7
NG = KT
HG = 4
DECAY_SCALE = math.exp(-0.5)
LAM_INIT = 0.8 - 0.6 * math.exp(-0.3 * 1)
NORM_EPS = 1e-6
LNX_EPS = 64e-5
SUBLN_EPS = 1e-5
RING = 4
CHUNK = KT * 512
NBANK = 8

COLS = [("g_mix0", 8), ("g_mix1", 8), ("g_ffn0", 8), ("g_ffn1", 8), ("mu", 48), ("w0", 8), ("a0", 8),
        ("k_k", 8), ("k_a", 8), ("r_k", 8), ("lnx_w", 8), ("lnx_b", 8), ("kv_g", 8), ("norm_mix", 8),
        ("norm_ffn", 8), ("norm_final", 8), ("k_norm", 1), ("q_norm", 1), ("subln", 1), ("hg_norm", 4),
        ("conv_b", FT), ("conv_w", 9 * FT), ("b_ada", 48), ("c", 16)]
CONS = [("ident", P), ("right_left", LEV * P), ("left_right", LEV * P), ("score_mask", 4 * P), ("head_sum", P),
        ("ones", P), ("rope_swap", P), ("cos", S), ("sin", S), ("chunk_mask", 3 * P)]
ROWS = [("sgu_g", 512), ("sgu_b", 512), ("b_spatial", 512), ("lam", 256)]


def offsets(table):
    at, out = 0, {}
    for name, n in table:
        out[name] = (at, n)
        at += n
    return out, at


COL_AT, NCOL = offsets(COLS)
CON_AT, NCON = offsets(CONS)
ROW_AT, NROW = offsets(ROWS)

W_LORA1, W_LORA2, W_K, W_R, W_V, W_O = 0, 1, 2, 4, 6, 8
W_GU0 = 10
W_KV_K, W_KV_V, W_Q, W_AO = W_GU0 + 11, W_GU0 + 13, W_GU0 + 15, W_GU0 + 17
W_GU1 = W_AO + 2
W_ADA = W_GU1 + 11
W_IN = W_ADA + 12
W_OUT = W_IN + 7
W_UP = W_OUT + 2
N_WIDE = W_UP + 11
CHUNKS = ([("wide", i) for i in range(W_KV_K)] + [("down", i) for i in range(8)]
          + [("wide", i) for i in range(W_KV_K, W_ADA)] + [("down", 8 + i) for i in range(8)]
          + [("wide", i) for i in range(W_ADA, N_WIDE)] + [("down", 16 + i) for i in range(8)])
CHUNK_NO = {c: n for n, c in enumerate(CHUNKS)}


def build(nc, wide, down, x_t, ctx_t, cols, cons, rows, w_sp, out):
    with ExitStack() as ctx:
        def sb(name, shape, dt=F32):
            return ctx.enter_context(nc.sbuf_tensor(name, shape, dt))

        sems = {}

        def sem(name):
            if name not in sems:
                sems[name] = ctx.enter_context(nc.semaphore(name))
            return sems[name]

        ring = sb("ring", [P, RING, CHUNK])
        resid = sb("resid", [P, KT, S])
        col = sb("col", [P, NCOL])
        con = sb("con", [P, NCON])
        buf = [sb(f"buf{i}", [P, KT, S]) for i in range(12)]
        rstd = sb("rstd", [P, S])
        tiny = sb("tiny", [P, 640])
        work = sb("work", [P, 2, 4, 512])
        banks = [ctx.enter_context(nc.psum_tensor(f"bank{i}", [P, 512], F32)) for i in range(NBANK)]

        def pcol(name, i=0, n=1):
            return col[:, COL_AT[name][0] + i:COL_AT[name][0] + i + n]

        def const(name, i=0, n=P):
            return con[:, CON_AT[name][0] + i:CON_AT[name][0] + i + n]

        def flat(t):
            return t[:, :, :].rearrange("p a b -> p (a b)")

        def prow(name):
            if name == "lam":
                return tiny[:, 384:640]
            at = ROW_AT[name][0]
            return work[:, 1, 1 + at // 512, :]

        ident = const("ident")

        jobs = {}
        uses = [0] * NBANK
        order = []

        def place(key):
            b = len(order) % NBANK
            jobs[key] = (b, uses[b])
            uses[b] += 1
            order.append(key)

        released = {}

        def frees(which, i, key):
            released[CHUNK_NO[(which, i)]] = key

        def plan_proj(name, base):
            for c in range(2):
                for j in range(2):
                    place((name, 2 * c + j))
                frees("wide", base + c, (name, 2 * c + 1))

        def plan_ffn(n, base):
            for f in range(FT):
                place(("gu", n, f))
                if f % 2:
                    frees("wide", base + f // 2, ("gu", n, f))
            for cb in range(KT):
                place(("dn", n, cb))
                frees("down", 8 * n + cb, ("dn", n, cb))

        place(("norm", 0))
        for i in range(4):
            place(("l1", i))
        frees("wide", W_LORA1, ("l1", 3))
        for cb in range(KT):
            place(("l2", cb))
        for j in range(4):
            place(("l2g", j))
        frees("wide", W_LORA2, ("l2g", 3))
        plan_proj("k", W_K)
        plan_proj("r", W_R)
        plan_proj("v", W_V)
        for n in ("kksum", "bonus"):
            for j in range(4):
                place((n, j))
        for j in range(4):
            place(("vt", j))
        for n in ("bt", "kt"):
            for j in range(2):
                place((n, j))
        PAIRS = [(0, 1), (2, 3), (4, 5), (6, 7)]
        for pair in PAIRS:
            for g in pair:
                for j in range(4):
                    place(("sc", g, j))
            for g in pair:
                place(("nt", g))
            for l in range(1, LEV):
                for what in ("y", "dxt") + (("dx",) if l < LEV - 1 else ()):
                    for g in pair:
                        place((what, g, l))
            for what in ("q0", "sa0", "st", "q1", "sa1", "yt"):
                for g in pair:
                    place((what, g))
        for n in ("ymean", "yvar"):
            for j in range(4):
                place((n, j))
        plan_proj("o", W_O)
        place(("norm", 1))
        plan_ffn(0, W_GU0)
        place(("norm", 2))
        plan_proj("ak", W_KV_K)
        plan_proj("av", W_KV_V)
        plan_proj("aq", W_Q)
        for n in ("aksum", "akrot", "aqsum", "aqrot"):
            for j in range(4):
                place((n, j))
        for h in range(8):
            place(("s", h, 0))
            place(("s", h, 1))
            if h >= 1:
                place(("pt", h - 1))
                place(("ao", h - 1))
        place(("pt", 7))
        place(("ao", 7))
        for j in range(4):
            place(("aosum", j))
        plan_proj("awo", W_AO)
        place(("norm", 3))
        plan_ffn(1, W_GU1)
        place(("ada", 0))
        for c in range(12):
            frees("wide", W_ADA + c, ("ada", c + 1))
        place(("norm", 4))
        place(("norm", 5))
        for d in range(3):
            for t in range(TT):
                place(("ctx", d, t))
            for j in range(2):
                place(("in", d, j))
            frees("wide", W_IN + d, ("in", d, 1))
        for d in range(3, 7):
            for j in range(2):
                place(("in", d, j))
            frees("wide", W_IN + d, ("in", d, 1))
        for d in range(2):
            for t in range(TT):
                place(("csum", d, t))
        for d in range(2):
            place(("cstate", d))
        for t in range(TT):
            place(("diag", t))
        for l in range(LEV):
            for d in range(2):
                for t in range(TT):
                    place(("lv", l, d, t))
        for d in range(2):
            place(("cross", d))
        for j in range(2):
            place(("go", j))
        for j in range(2):
            place(("gsum", j))
        for j in range(2):
            place(("z", j))
        plan_proj("mo", W_OUT)
        place(("norm", 6))
        plan_ffn(2, W_UP)
        place(("norm", 7))

        full = [sem(f"bank_full{b}") for b in range(NBANK)]
        free = [sem(f"bank_free{b}") for b in range(NBANK)]
        slot_full = [sem(f"slot_full{r}") for r in range(RING)]

        def bank_of(key):
            return banks[jobs[key][0]]

        def wait_full(eng, key):
            b, use = jobs[key]
            eng.wait_ge(full[b], use + 1)

        def wait_freed(eng, key):
            b, use = jobs[key]
            eng.wait_ge(free[b], use + 1)


        class Lane:

            def __init__(self, eng, name):
                self.eng, self.sem, self.n = eng, sem(name), 0

            def go(self, ins):
                self.n += 1
                ins.then_inc(self.sem, 1)

            def step(self, ins):
                self.go(ins)
                self.eng.wait_ge(self.sem, self.n)

        def spread(ap, shape):
            return ap.unsqueeze(1).to_broadcast(shape)

        def halves(t, d, b):
            v = t[:, 4 * d:4 * d + 4, :].rearrange("p h (n r b) -> p (h n) r b", r=2, b=b)
            return v[:, :, 0, :], v[:, :, 1, :]

        def halves_all(t, b):
            v = t[:, :, :].rearrange("p h (n r b) -> p (h n) r b", r=2, b=b)
            return v[:, :, 0, :], v[:, :, 1, :]

        TAPS = [(i, j) for i in range(3) for j in range(3)]
        ROWS_X, GRID = S // 64, 64
        h_t, hh_t, mixed = buf[0], buf[1], [buf[2], buf[3]]
        k_t, r_t, a_t, w_t, g_t, v_tok = buf[4], buf[5], buf[6], buf[7], buf[8], buf[9]
        lora = buf[10]
        sq = buf[11]
        kk_t, b_t, cum_t, grow_t = buf[0], buf[1], buf[2], buf[3]
        bk_tok = flat(buf[3])
        v_t, y_t = buf[7], buf[2]
        v_tokf = v_tok[:, :, :].rearrange("p (t a) b -> p t (a b)", t=TT)
        scores = [buf[10][:, :, :].rearrange("p (j a) b -> p j (a b)", j=4),
                  buf[11][:, :, :].rearrange("p (j a) b -> p j (a b)", j=4)]
        last_mix = [("l1", 0), ("l1", 1), ("l1", 3), ("k", 3), ("r", 3), ("v", 3)]
        mix_of = [1, 4, 5, 2, 0, 3]
        hkv_t, hq_t, ak_t, aq_t = buf[0], buf[1], buf[2], buf[4]
        av_tok = buf[3][:, :, :].rearrange("p (t a) b -> p t (a b)", t=TT)
        turn_t, ao_t = buf[6], buf[9]
        prob = buf[7][:, :, :].rearrange("p (w i q) n -> p w i (q n)", w=2, i=2)
        Q_COLS = [slice(0, P), slice(P, 3 * P)]
        prob_t = buf[8][:, :, :].rearrange("p (w a) n -> p w (a n)", w=2)
        ffn_h = buf[0]
        act = lambda f: buf[1 + f // 8][:, f % 8, :]
        ctx_r, hc_t, hx_t = buf[11], buf[0], buf[1]
        f_x, k_x = buf[2], buf[3]
        q_x, u_x = buf[4][:, 0:4, :], buf[4][:, 4:8, :]
        gate_x = buf[5][:, 0:4, :]
        v_x = buf[5][:, 4:8, :].rearrange("p (t a) n -> p t (a n)", t=TT)
        vv_x = buf[6][:, 0:4, :].rearrange("p (t a) n -> p t (a n)", t=TT)
        v_c = buf[6][:, 4:8, :].rearrange("p (t a) n -> p t (a n)", t=TT)
        f_c = buf[7][:, :, :].rearrange("p (d t a) n -> p d t (a n)", d=2, t=TT)
        k_c = buf[8][:, :, :].rearrange("p (d t a) n -> p d t (a n)", d=2, t=TT)
        pre_t, suf_t, wgt_t, st_t = buf[9], buf[10], buf[11], buf[0]
        st_v = st_t[:, :, :].rearrange("p (t h) n -> p t h n", t=TT)
        qd_t = buf[1]
        mix_t = buf[8]
        state = work[:, 0, 0:2, :]
        wsp = work[:, 1, 0, :]
        o_t = buf[7][:, 0:4, :]
        o_sq = buf[7][:, 4:8, :]
        ada = tiny[:, 0:96].rearrange("p (e c) -> p e c", c=2)
        silu_c = tiny[:, 96:112].rearrange("p (k c) -> p k c", c=2)
        gain = tiny[:, 112:136]
        mid = tiny[:, 136:152]
        send = tiny[:, 152:160]
        one_minus_ka = tiny[:, 160:168]
        mx = tiny[:, 168:176].rearrange("p (w n) -> p w n", w=2)
        sums = tiny[:, 176:184].rearrange("p (w n) -> p w n", w=2)
        lam_t = tiny[:, 184:186]
        neg_lam = tiny[:, 186:187]
        sub_col = tiny[:, 187:188]
        one_col = tiny[:, 188:189]
        bn = tiny[:, 192:192 + 8 * 6].rearrange("p (a s) -> p a s", a=8)
        bna = tiny[:, 240:256].rearrange("p (a s) -> p a s", a=8)
        lam_tmp = tiny[:, 256:384].rearrange("p (a n) -> p a n", a=2)
        ISS = CH ** -0.5
        HG_SCALE = float(P) ** -0.5

        with nc.Block() as block:
            @block.sync
            def _(sp):
                sp.dma_start(con[:, :], cons).then_inc(sem("con_in"), 16)
                for n, (which, i) in enumerate(CHUNKS):
                    if n >= RING:
                        key = released[n - RING]
                        if key[0] == "ada" and key[1] < 12:
                            sp.wait_ge(sem("ada_used"), key[1])
                        else:
                            wait_full(sp, ("ada", 0) if key[0] == "ada" else key)
                    if which == "wide":
                        src, dst = wide[i], ring[:, n % RING, :]
                    else:
                        src, dst = down[i], ring[:, n % RING, 0:FT * P]
                    sp.dma_start(dst, src).then_inc(slot_full[n % RING], 16)
                for t in range(KT):
                    sp.wait_ge(sem("out_ready"), t + 1)
                    sp.dma_start(out[:, t, :], resid[:, t, :]).then_inc(sem("out_done"), 16)
                sp.wait_ge(sem("out_done"), 16 * KT)

            @block.tensor
            def _(pe):
                mm = nc.tensor.matmul

                def open_bank(key):
                    b, use = jobs[key]
                    if use > 0:
                        pe.wait_ge(free[b], use)
                    return banks[b]

                def close(ins, key):
                    ins.then_inc(full[jobs[key][0]], 1)

                def arrived(which, i):
                    n = CHUNK_NO[(which, i)]
                    pe.wait_ge(slot_full[n % RING], 16 * (n // RING + 1))
                    return ring[:, n % RING, :]

                def norm(n, sqb):
                    pe.wait_ge(sem("norm_sq"), n + 1)
                    bank = open_bank(("norm", n))
                    for kt in range(KT):
                        last = mm(bank[:, 0:S], const("ones"), sqb[:, kt, :], start=kt == 0, stop=kt == KT - 1)
                    close(last, ("norm", n))

                def columns(bank, w, c0, x, ready=None):
                    for kt in range(KT):
                        if ready is not None:
                            pe.wait_ge(ready[0], ready[1] + kt + 1)
                        last = mm(bank, w[:, kt, c0:c0 + P], x[:, kt, :], start=kt == 0, stop=kt == KT - 1)
                    return last

                def project(name, base, x, ready):
                    for c in range(2):
                        w = arrived("wide", base + c).rearrange("p (k n) -> p k n", k=KT)
                        for j in range(2):
                            bank = open_bank((name, 2 * c + j))
                            for half in range(2):
                                last = columns(bank[:, half * S:(half + 1) * S], w, (2 * j + half) * P, x, ready)
                                ready = None
                            close(last, (name, 2 * c + j))

                def tokens(key, w, x, t, ready=None):
                    bank = open_bank(key)
                    for kt in range(KT):
                        if ready is not None:
                            pe.wait_ge(ready[0], ready[1] + kt + 1)
                        last = mm(bank[:, :], x[:, kt, t * P:(t + 1) * P], w[:, kt, :], start=kt == 0, stop=kt == KT - 1)
                    close(last, key)

                def project_tokens(name, base, x, ready):
                    for c in range(2):
                        w = arrived("wide", base + c).rearrange("p (k n) -> p k n", k=KT)
                        for t in range(TT):
                            tokens((name, 2 * c + t), w, x, t, ready)
                            ready = None

                def sums_over(name, lhs, src, before):
                    for j in range(4):
                        before(j)
                        bank = open_bank((name, j))
                        close(mm(bank[:, :], lhs, flat(src)[:, 512 * j:512 * (j + 1)], start=True, stop=True), (name, j))

                def ffn(n, base, x):
                    for c in range(FT // 2):
                        w = arrived("wide", base + c).rearrange("p (k n) -> p k n", k=KT)
                        for i in range(2):
                            key = ("gu", n, 2 * c + i)
                            bank = open_bank(key)
                            ready = (sem(f"ffn_h{n}"), 0) if c == 0 and i == 0 else None
                            columns(bank[:, 0:S], w, i * P, x, ready)
                            close(columns(bank[:, S:2 * S], w, 2 * P + i * P, x), key)
                    for cb in range(KT):
                        w = arrived("down", 8 * n + cb)[:, 0:FT * P].rearrange("p (f n) -> p f n", n=P)
                        bank = open_bank(("dn", n, cb))
                        for f in range(FT):
                            if cb == 0:
                                pe.wait_ge(sem(f"act{n}"), f + 1)
                            last = mm(bank[:, 0:S], w[:, f, :], act(f), start=f == 0, stop=f == FT - 1)
                        close(last, ("dn", n, cb))

                pe.wait_ge(sem("con_in"), 16)
                norm(0, sq)
                w = arrived("wide", W_LORA1)[:, 0:KT * 288].rearrange("p (k n) -> p k n", n=288)
                for i, (c0, m, src) in enumerate([(0, 64, 0), (64, 64, 1), (128, 128, 2), (256, 32, 2)]):
                    bank = open_bank(("l1", i))
                    for kt in range(KT):
                        pe.wait_ge(sem("mix_ready"), 8 * src + kt + 1)
                        last = mm(bank[0:m, 0:S], w[:, kt, c0:c0 + m], mixed[src % 2][:, kt, :], start=kt == 0, stop=kt == KT - 1)
                    close(last, ("l1", i))
                w = arrived("wide", W_LORA2).rearrange("p (k n) -> p k n", k=4)
                wait_freed(pe, ("l1", 0))
                wait_freed(pe, ("l1", 1))
                for cb in range(KT):
                    bank = open_bank(("l2", cb))
                    mm(bank[:, 0:S], w[0:64, 0, cb * P:(cb + 1) * P], lora[0:64, 0, :], start=True, stop=True)
                    close(mm(bank[:, S:2 * S], w[0:64, 1, cb * P:(cb + 1) * P], lora[0:64, 1, :], start=True, stop=True), ("l2", cb))
                wait_freed(pe, ("l1", 2))
                wait_freed(pe, ("l1", 3))
                for j in range(4):
                    bank = open_bank(("l2g", j))
                    for half in range(2):
                        cb = 2 * j + half
                        mm(bank[:, half * S:(half + 1) * S], w[:, 2, cb * P:(cb + 1) * P], lora[:, 2, :], start=True, stop=False)
                        last = mm(bank[:, half * S:(half + 1) * S], w[0:32, 3, cb * P:(cb + 1) * P], lora[0:32, 3, :], start=False, stop=True)
                    close(last, ("l2g", j))
                project("k", W_K, mixed[1], (sem("mix_ready"), 24))
                project("r", W_R, mixed[0], (sem("mix_ready"), 32))
                project_tokens("v", W_V, mixed[1], (sem("mix_ready"), 40))
                sums_over("kksum", const("head_sum"), sq, lambda j: pe.wait_ge(sem("kk_sq"), 1))
                sums_over("bonus", const("head_sum"), a_t, lambda j: pe.wait_ge(sem("bonus_in"), 2 * j + 2))
                for j in range(4):
                    if j == 0:
                        for i in range(4):
                            wait_freed(pe, ("v", i))
                    bank = open_bank(("vt", j))
                    for half in range(2):
                        for t in range(TT):
                            last = nc.tensor.transpose(bank[:, half * S + t * P:half * S + (t + 1) * P],
                                                       v_tokf[:, t, (2 * j + half) * P:(2 * j + half + 1) * P], ident)
                    close(last, ("vt", j))
                for name, src in (("bt", b_t), ("kt", k_t)):
                    pe.wait_ge(sem("tilde_ready"), 2 if name == "bt" else 3)
                    for j in range(2):
                        bank = open_bank((name, j))
                        for i in range(4):
                            last = nc.tensor.transpose(bank[:, i * P:(i + 1) * P], src[:, 4 * j + i, 0:P], ident)
                        close(last, (name, j))
                pe.wait_ge(sem("tilde_ready"), 4)
                for n_pair, pair in enumerate(PAIRS):
                    for g in pair:
                        for c in range(2):
                            for hd in range(2):
                                key = ("sc", g, 2 * c + hd)
                                bank = open_bank(key)
                                part = slice(hd * CH, hd * CH + CH)
                                tok = slice(c * P, (c + 1) * P)
                                at_, bt_, kt_, rt_ = (z[part, g, tok] for z in (kk_t, b_t, k_t, r_t))
                                mm(bank[:, 0:P], at_, bt_, start=True, stop=True)
                                mm(bank[:, P:2 * P], bt_, rt_, start=True, stop=True)
                                mm(bank[:, 2 * P:3 * P], kt_, at_, start=True, stop=True)
                                close(mm(bank[:, 3 * P:4 * P], kt_, rt_, start=True, stop=True), key)
                    for g in pair:
                        nm = work[:, g % 2, 0, :]
                        pe.wait_ge(sem(f"nm_ready{g % 2}"), LEV * (g // 2) + 1)
                        bank = open_bank(("nt", g))
                        for j in range(4):
                            last = nc.tensor.transpose(bank[:, j * P:(j + 1) * P], nm[:, j * P:(j + 1) * P], ident)
                        close(last, ("nt", g))
                    for l in range(1, LEV):
                        for g in pair:
                            nm, x, xt, y = (work[:, g % 2, i, :] for i in range(4))
                            pe.wait_ge(sem(f"nm_ready{g % 2}"), LEV * (g // 2) + l + 1)
                            wait_freed(pe, ("nt", g) if l == 1 else ("dxt", g, l - 1))
                            bank = open_bank(("y", g, l))
                            for j in range(4):
                                s_ = slice(j * P, (j + 1) * P)
                                last = mm(bank[:, s_], nm[:, s_], xt[:, s_], start=True, stop=True)
                            close(last, ("y", g, l))
                        for g in pair:
                            nm, x, xt, y = (work[:, g % 2, i, :] for i in range(4))
                            wait_freed(pe, ("y", g, l))
                            if l == 1:
                                pe.wait_ge(sem("x_ready"), g + 1)
                            else:
                                wait_freed(pe, ("dx", g, l - 1))
                            bank = open_bank(("dxt", g, l))
                            for j in range(4):
                                s_ = slice(j * P, (j + 1) * P)
                                last = mm(bank[:, s_], x[:, s_], y[:, s_], start=True, stop=True)
                            close(last, ("dxt", g, l))
                        if l < LEV - 1:
                            for g in pair:
                                nm, x, xt, y = (work[:, g % 2, i, :] for i in range(4))
                                bank = open_bank(("dx", g, l))
                                for j in range(4):
                                    s_ = slice(j * P, (j + 1) * P)
                                    last = mm(bank[:, s_], y[:, s_], x[:, s_], start=True, stop=True)
                                close(last, ("dx", g, l))
                    for what in ("q0", "sa0", "st", "q1", "sa1", "yt"):
                        for g in pair:
                            key = (what, g)
                            sc = scores[g % 2]
                            xt = work[:, g % 2, 2, :]
                            q0, sa0, st, q1 = (work[:, g % 2, 0, i * P:(i + 1) * P] for i in range(4))
                            sa1 = work[:, g % 2, 3, 0:P]
                            if what == "sa0":
                                wait_freed(pe, ("q0", g))
                                wait_freed(pe, ("dxt", g, LEV - 1))
                            elif what != "q0":
                                wait_freed(pe, ({"st": "sa0", "q1": "st", "sa1": "q1", "yt": "sa1"}[what], g))
                            if what == "st" and g == 0:
                                for i in range(2):
                                    wait_freed(pe, ("bt", i))
                                    wait_freed(pe, ("kt", i))
                            bank = open_bank(key)
                            if what in ("q0", "q1"):
                                c = int(what[1])
                                if c:
                                    mm(bank[:, 0:P], kk_t[:, g, P:S], st, start=True, stop=False)
                                for hd in range(2):
                                    o = hd * CH
                                    last = mm(bank[:, o:o + CH], sc[:, 2 * c + hd, 2 * P:3 * P], v_tokf[:, c, g * P + o:g * P + o + CH],
                                              start=c == 0, stop=c == 0 or hd == 1)
                            elif what in ("sa0", "sa1"):
                                c = int(what[2])
                                for hd in range(2):
                                    o = hd * CH
                                    j = 2 * c + hd
                                    last = mm(bank[:, o:o + CH], xt[:, j * P:(j + 1) * P], (q0, q1)[c][:, o:o + CH], start=True, stop=True)
                            elif what == "st":
                                mm(bank[:, 0:P], bk_tok[:, g * P:(g + 1) * P], sa0, start=True, stop=False)
                                last = mm(bank[:, 0:P], bk_tok[:, D + g * P:D + (g + 1) * P], v_tokf[:, 0, g * P:(g + 1) * P], start=False, stop=True)
                            else:
                                for hd in range(2):
                                    o = hd * CH
                                    for c in range(2):
                                        dst = bank[o:o + CH, c * P:(c + 1) * P]
                                        mm(dst, (sa0, sa1)[c][:, o:o + CH], sc[:, 2 * c + hd, P:2 * P], start=True, stop=False)
                                        last = mm(dst, v_tokf[:, c, g * P + o:g * P + o + CH], sc[:, 2 * c + hd, 3 * P:4 * P],
                                                  start=False, stop=c == 0)
                                        if c:
                                            last = mm(dst, st[:, o:o + CH], r_t[:, g, P:S], start=False, stop=True)
                            close(last, key)
                for g in range(NG):
                    wait_freed(pe, ("yt", g))
                sums_over("ymean", const("head_sum"), y_t, lambda j: None)
                sums_over("yvar", const("head_sum"), sq, lambda j: pe.wait_ge(sem("y_sq"), 1))
                project("o", W_O, y_t, (sem("y_ready"), 0))
                norm(1, sq)
                ffn(0, W_GU0, ffn_h)
                norm(2, buf[5])
                project("ak", W_KV_K, hkv_t, (sem("hkv_ready"), 0))
                project_tokens("av", W_KV_V, hkv_t, None)
                project("aq", W_Q, hq_t, (sem("hq_ready"), 0))
                for i, name in enumerate(("ak", "aq")):
                    src = (ak_t, aq_t)[i]
                    sums_over(name + "sum", const("head_sum"), buf[5], lambda j: pe.wait_ge(sem("head_sq"), i + 1))
                    sums_over(name + "rot", const("rope_swap"), src, lambda j: pe.wait_ge(sem("head_normed"), i + 1))

                def values(h):
                    wait_freed(pe, ("s", h, 1))
                    pe.wait_ge(sem("prob_ready"), 2 * h + 2)
                    bank = open_bank(("pt", h))
                    p_ = prob[:, h % 2]
                    for i in range(3):
                        last = nc.tensor.transpose(bank[:, i * P:(i + 1) * P], p_[:, 0, i * P:(i + 1) * P], ident)
                    close(last, ("pt", h))
                    wait_freed(pe, ("pt", h))
                    bank = open_bank(("ao", h))
                    t_ = prob_t[:, h % 2, :]
                    mm(bank[:, 0:S], av_tok[:, 0, h * P:(h + 1) * P], t_[:, 0:S], start=True, stop=False)
                    close(mm(bank[:, P:S], av_tok[:, 1, h * P:(h + 1) * P], t_[:, S:S + P], start=False, stop=True), ("ao", h))

                for i in range(4):
                    wait_freed(pe, ("av", i))
                pe.wait_ge(sem("roped"), 2)
                for h in range(8):
                    for i in range(2):
                        bank = open_bank(("s", h, i))
                        o = i * CH
                        for qt in range(2):
                            last = mm(bank[:, Q_COLS[qt]], aq_t[o:o + CH, h, qt * P:(qt + 1) * P],
                                      ak_t[o:o + CH, h, 0:(qt + 1) * P], start=True, stop=True)
                        close(last, ("s", h, i))
                    if h >= 1:
                        values(h - 1)
                values(7)
                sums_over("aosum", const("ones"), buf[5], lambda j: pe.wait_ge(sem("ao_sq"), 1))
                project("awo", W_AO, ao_t, (sem("ao_ready"), 0))
                norm(3, buf[5])
                ffn(1, W_GU1, ffn_h)
                pe.wait_ge(sem("silu_c"), 1)
                bank = open_bank(("ada", 0))
                for c in range(12):
                    w = arrived("wide", W_ADA + c).rearrange("p (k n) -> p k n", k=KT)
                    for i in range(4):
                        e = 4 * c + i
                        for kt in range(KT):
                            last = mm(bank[:, 2 * e:2 * e + 2], w[:, kt, i * P:(i + 1) * P], silu_c[:, kt, :], start=kt == 0, stop=kt == KT - 1)
                    if c < 11:
                        last.then_inc(sem("ada_used"), 1)
                close(last, ("ada", 0))
                norm(4, buf[10])
                norm(5, buf[10])
                for d in range(7):
                    w = arrived("wide", W_IN + d).rearrange("p (k n) -> p k n", k=KT)
                    if d < 3:
                        for t in range(TT):
                            tokens(("ctx", d, t), w, hc_t, t, (sem("hc_ready"), 0) if d == 0 and t == 0 else None)
                    for j in range(2):
                        if d in (2, 6):
                            tokens(("in", d, j), w, hx_t, j)
                        else:
                            bank = open_bank(("in", d, j))
                            for half in range(2):
                                last = columns(bank[:, half * S:(half + 1) * S], w, (2 * j + half) * P, hx_t,
                                               (sem("hx_ready"), 0) if d == 0 and j == 0 and half == 0 else None)
                            close(last, ("in", d, j))
                pe.wait_ge(sem("ctx_log"), 1)
                for d in range(2):
                    tri = const("score_mask", (0, 2)[d] * P)
                    for t in range(TT):
                        bank = open_bank(("csum", d, t))
                        other = t == d
                        last = mm(bank[:, :], tri, f_c[:, d, t, :], start=True, stop=not other)
                        if other:
                            last = mm(bank[:, :], const("ones"), f_c[:, d, 1 - t, :], start=False, stop=True)
                        close(last, ("csum", d, t))
                pe.wait_ge(sem("ctx_k"), 1)
                for d in range(2):
                    bank = open_bank(("cstate", d))
                    for h in range(HG):
                        for t in range(TT):
                            last = mm(bank[:, h * P:(h + 1) * P], k_c[:, d, t, h * P:(h + 1) * P], v_c[:, t, h * P:(h + 1) * P],
                                      start=t == 0, stop=t == TT - 1)
                    close(last, ("cstate", d))
                pe.wait_ge(sem("diag_ready"), 1)
                for t in range(TT):
                    bank = open_bank(("diag", t))
                    tok = slice(t * P, (t + 1) * P)
                    for h in range(HG):
                        last = mm(bank[:, h * P:(h + 1) * P], qd_t[:, h, tok], q_x[:, h, tok], start=True, stop=True)
                    close(last, ("diag", t))
                for l in range(LEV):
                    pe.wait_ge(sem("wgt_ready"), l + 1)
                    for d in range(2):
                        for t in range(TT):
                            bank = open_bank(("lv", l, d, t))
                            tok = slice(t * P, (t + 1) * P)
                            for h in range(HG):
                                z = wgt_t[:, 4 * d + h, tok]
                                last = mm(bank[:, h * P:(h + 1) * P], z, z, start=True, stop=True)
                            close(last, ("lv", l, d, t))
                pe.wait_ge(sem("wgt_ready"), LEV + 1)
                for d in range(2):
                    bank = open_bank(("cross", d))
                    s_tok, t_tok = (slice(0, P), slice(P, S)) if d == 0 else (slice(P, S), slice(0, P))
                    for h in range(HG):
                        last = mm(bank[:, h * P:(h + 1) * P], wgt_t[:, 4 * d + h, s_tok], wgt_t[:, 4 * d + h, t_tok], start=True, stop=True)
                    close(last, ("cross", d))
                pe.wait_ge(sem("qd_ready"), 1)
                wait_freed(pe, ("cross", 0))
                wait_freed(pe, ("cross", 1))
                for j in range(2):
                    bank = open_bank(("go", j))
                    for i in range(2):
                        h = 2 * j + i
                        dst = bank[:, i * S:(i + 1) * S]
                        for t in range(TT):
                            mm(dst, v_x[:, t, h * P:(h + 1) * P], st_v[:, t, h, :], start=t == 0, stop=False)
                        for d in range(2):
                            last = mm(dst, state[:, d, h * P:(h + 1) * P], qd_t[:, 4 * d + h, :], start=False, stop=d == 1)
                    close(last, ("go", j))
                pe.wait_ge(sem("go_sq"), 1)
                for j in range(2):
                    bank = open_bank(("gsum", j))
                    close(mm(bank[:, :], const("ones"), o_sq[:, 2 * j:2 * j + 2, :].rearrange("p a b -> p (a b)"), start=True, stop=True),
                          ("gsum", j))
                pe.wait_ge(sem("vv_ready"), 1)
                pe.wait_ge(sem("wsp_in"), 16)
                for j in range(2):
                    bank = open_bank(("z", j))
                    for i in range(2):
                        h = 2 * j + i
                        for t in range(TT):
                            last = mm(bank[:, i * S + t * P:i * S + (t + 1) * P], vv_x[:, t, h * P:(h + 1) * P], wsp[:, h * P:(h + 1) * P],
                                      start=True, stop=True)
                    close(last, ("z", j))
                project("mo", W_OUT, mix_t, (sem("mix2_ready"), 0))
                norm(6, buf[5])
                ffn(2, W_UP, ffn_h)
                norm(7, buf[5])

            @block.scalar
            def _(eng):
                own = Lane(eng, "act_own")
                act_ = nc.scalar.activation

                def release(ins, key):
                    ins.then_inc(free[jobs[key][0]], 1)

                def norm(n, src, sqb):
                    act_(flat(sqb), flat(src), ACT.Square).then_inc(sem("norm_sq"), 1)
                    wait_freed(eng, ("norm", n))
                    act_(rstd[:, :], rstd[:, :], ACT.Sqrt).then_inc(sem("norm_root"), 1)

                def copy_out(name, dst, n=4):
                    for j in range(n):
                        wait_full(eng, (name, j))
                        release(act_(flat(dst)[:, 512 * j:512 * (j + 1)], bank_of((name, j))[:, :], ACT.Copy), (name, j))

                def ffn(n):
                    for f in range(FT):
                        key = ("gu", n, f)
                        wait_full(eng, key)
                        if f >= 4:
                            eng.wait_ge(sem(f"act{n}"), f - 3)
                        act_(buf[4][:, f % 4, :], bank_of(key)[:, 0:S], ACT.Silu).then_inc(sem(f"gate{n}"), 1)

                eng.dma_start(resid[:, :, :], x_t).then_inc(sem("x_in"), 16)
                eng.dma_start(col[:, :], cols).then_inc(sem("col_in"), 16)
                eng.dma_start(prow("lam"), rows[0:1, 1536:NROW].partition_broadcast(P)).then_inc(sem("lam_rows_in"), 16)
                eng.wait_ge(sem("x_in"), 16)
                norm(0, resid, sq)
                eng.wait_ge(sem("col_in"), 16)
                for i, (m, f) in enumerate([(64, ACT.Tanh), (64, ACT.Copy), (128, ACT.Sigmoid), (32, ACT.Sigmoid)]):
                    wait_full(eng, ("l1", i))
                    release(act_(lora[0:m, i, :], bank_of(("l1", i))[0:m, 0:S], f), ("l1", i))
                for cb in range(KT):
                    key = ("l2", cb)
                    wait_full(eng, key)
                    own.go(act_(w_t[:, cb, :], bank_of(key)[:, 0:S], ACT.Sigmoid, bias=pcol("w0", cb)))
                    release(act_(a_t[:, cb, :], bank_of(key)[:, S:2 * S], ACT.Sigmoid, bias=pcol("a0", cb)), key)
                copy_out("k", k_t)
                copy_out("r", r_t)
                for c in range(2):
                    for t in range(TT):
                        key = ("v", 2 * c + t)
                        wait_full(eng, key)
                        release(act_(v_tokf[:, t, 512 * c:512 * (c + 1)], bank_of(key)[:, :], ACT.Copy), key)
                eng.wait_ge(sem("kk_ready"), 1)
                act_(flat(sq), flat(kk_t), ACT.Square).then_inc(sem("kk_sq"), 1)
                eng.wait_ge(sem("kk_floor"), 4)
                act_(flat(sq), flat(sq), ACT.Sqrt).then_inc(sem("kk_root"), 1)
                copy_out("bonus", a_t)
                eng.wait_ge(sem("cum_ready"), 1)
                act_(flat(w_t), flat(w_t), ACT.Exp, scale=-DECAY_SCALE).then_inc(sem("decay_a"), 1)
                act_(send, send, ACT.Exp, scale=-DECAY_SCALE).then_inc(sem("decay_s"), 1)
                act_(flat(grow_t), flat(cum_t), ACT.Exp, scale=-DECAY_SCALE).then_inc(sem("decay_r"), 1)
                eng.wait_ge(sem("kk_unit"), 1)
                act_(flat(sq), flat(cum_t), ACT.Exp, scale=DECAY_SCALE).then_inc(sem("decay_bk"), 1)
                eng.wait_ge(sem("tilde_ready"), 1)
                copy_out("vt", v_t)
                eng.wait_ge(sem("tilde_ready"), 4)
                for i, name in enumerate(("bt", "kt")):
                    for j in range(2):
                        wait_full(eng, (name, j))
                        release(act_(bk_tok[:, i * D + 512 * j:i * D + 512 * (j + 1)], bank_of((name, j))[:, :], ACT.Copy), (name, j))
                for pair in PAIRS:
                    for l in range(1, LEV):
                        for g in pair:
                            key = ("y", g, l)
                            wait_full(eng, key)
                            release(act_(work[:, g % 2, 3, :], bank_of(key)[:, :], ACT.Copy), key)
                    for what in ("q0", "sa0", "q1", "sa1", "yt"):
                        for g in pair:
                            key = (what, g)
                            wait_full(eng, key)
                            if what == "yt":
                                dst, src = y_t[:, g, :], bank_of(key)[:, 0:S]
                            else:
                                i = {"q0": 0, "sa0": 1, "q1": 3}.get(what)
                                dst = work[:, g % 2, 3, 0:P] if i is None else work[:, g % 2, 0, i * P:(i + 1) * P]
                                src = bank_of(key)[:, 0:P]
                            release(act_(dst, src, ACT.Copy), key)
                eng.wait_ge(sem("y_centered"), 4)
                act_(flat(sq), flat(y_t), ACT.Square).then_inc(sem("y_sq"), 1)
                eng.wait_ge(sem("y_var"), 4)
                act_(flat(sq), flat(sq), ACT.Sqrt).then_inc(sem("y_root"), 1)
                for j in range(4):
                    wait_freed(eng, ("o", j))
                norm(1, resid, sq)
                ffn(0)
                for cb in range(KT):
                    wait_freed(eng, ("dn", 0, cb))
                norm(2, resid, buf[5])
                copy_out("ak", ak_t)
                for c in range(2):
                    for t in range(TT):
                        key = ("av", 2 * c + t)
                        wait_full(eng, key)
                        release(act_(av_tok[:, t, 512 * c:512 * (c + 1)], bank_of(key)[:, :], ACT.Copy), key)
                for j in range(4):
                    wait_freed(eng, ("ak", j))
                act_(flat(buf[5]), flat(ak_t), ACT.Square).then_inc(sem("head_sq"), 1)
                copy_out("aq", aq_t)
                for i in range(2):
                    if i:
                        eng.wait_ge(sem("head_normed"), 1)
                        for j in range(4):
                            wait_freed(eng, ("aq", j))
                        act_(flat(buf[5]), flat(aq_t), ACT.Square).then_inc(sem("head_sq"), 1)
                    eng.wait_ge(sem("head_ms"), 4 * i + 4)
                    act_(flat(buf[5]), flat(buf[5]), ACT.Sqrt).then_inc(sem("head_root"), 1)
                eng.wait_ge(sem("lam_in"), 1)
                act_(lam_t, lam_t, ACT.Exp).then_inc(sem("lam_exp"), 1)

                def move_pt(h):
                    wait_full(eng, ("pt", h))
                    release(act_(prob_t[:, h % 2, 0:3 * P], bank_of(("pt", h))[:, 0:3 * P], ACT.Copy), ("pt", h))

                for h in range(8):
                    for qt in range(2):
                        eng.wait_ge(sem("max_ready"), 2 * h + qt + 1)
                        for i in range(2):
                            p_ = prob[:, h % 2, i, Q_COLS[qt]]
                            act_(p_, p_, ACT.Exp, bias=mx[:, h % 2, 2 * qt + i:2 * qt + i + 1],
                                 accum_out=sums[:, h % 2, 2 * qt + i:2 * qt + i + 1]).then_inc(sem("exp_done"), 1)
                    if h >= 1:
                        move_pt(h - 1)
                move_pt(7)
                for h in range(8):
                    wait_freed(eng, ("ao", h))
                act_(flat(buf[5]), flat(ao_t), ACT.Square).then_inc(sem("ao_sq"), 1)
                eng.wait_ge(sem("ao_ms"), 4)
                act_(flat(buf[5]), flat(buf[5]), ACT.Sqrt).then_inc(sem("ao_root"), 1)
                for j in range(4):
                    wait_freed(eng, ("awo", j))
                norm(3, resid, buf[5])
                ffn(1)
                for cb in range(KT):
                    wait_freed(eng, ("dn", 1, cb))
                act_(silu_c, pcol("c", 0, 16).rearrange("p (k c) -> p k c", c=2), ACT.Silu).then_inc(sem("silu_c"), 1)
                eng.dma_start(ctx_r[:, :, :], ctx_t).then_inc(sem("ctx_in"), 16)
                eng.dma_start(wsp, w_sp).then_inc(sem("wsp_in"), 16)
                eng.dma_start(work[:, 1, 1:4, :].rearrange("p a b -> p (a b)"), rows[0:1, 0:1536].partition_broadcast(P))\
                   .then_inc(sem("rows_in"), 16)
                eng.wait_ge(sem("ctx_in"), 16)
                norm(4, ctx_r, buf[10])
                eng.wait_ge(sem("hc_ready"), 8)
                norm(5, resid, buf[10])
                for d in range(7):
                    if d < 3:
                        for t in range(TT):
                            key = ("ctx", d, t)
                            wait_full(eng, key)
                            dst = v_c[:, t, :] if d == 2 else f_c[:, d, t, :]
                            release(act_(dst, bank_of(key)[:, :], ACT.Copy), key)
                    for j in range(2):
                        key = ("in", d, j)
                        wait_full(eng, key)
                        two = slice(2 * j, 2 * j + 2)
                        dst = {0: f_x[:, two, :], 1: f_x[:, 4 + 2 * j:6 + 2 * j, :], 2: v_x[:, j, :], 3: q_x[:, two, :],
                               4: gate_x[:, two, :], 5: u_x[:, two, :], 6: vv_x[:, j, :]}[d]
                        if d not in (2, 6):
                            dst = dst.rearrange("p a b -> p (a b)")
                        f = {3: ACT.Silu, 4: ACT.Silu, 5: ACT.Gelu, 6: ACT.Gelu}.get(d, ACT.Copy)
                        release(act_(dst, bank_of(key)[:, :], f), key)
                cf, ck, xf, xk = (flat(z) for z in (buf[7], buf[8], f_x, k_x))
                for n, (f, k, a) in enumerate([(cf, ck, flat(buf[9])), (xf, xk, flat(buf[10]))]):
                    for d in range(2):
                        for t in range(TT):
                            wait_freed(eng, ("ctx" if n == 0 else "in", d, t))
                    act_(k, f, ACT.Sigmoid, scale=-1.0).then_inc(sem("gate_k"), 1)
                for n, (f, k, a) in enumerate([(cf, ck, flat(buf[9])), (xf, xk, flat(buf[10]))]):
                    eng.wait_ge(sem("gate_abs"), n + 1)
                    own.step(act_(a, a, ACT.Exp, scale=-1.0))
                    act_(a, a, ACT.Ln, bias=one_col).then_inc(sem("gate_log1p"), 1)
                for d in range(2):
                    for t in range(TT):
                        wait_full(eng, ("csum", d, 1))
                        release(act_(f_c[:, d, t, :], bank_of(("csum", d, t))[:, :], ACT.Exp), ("csum", d, t))
                for d in range(2):
                    wait_full(eng, ("cstate", d))
                    release(act_(state[:, d, :], bank_of(("cstate", d))[:, :], ACT.Copy), ("cstate", d))
                for l in range(LEV + 1):
                    b = 1 << l
                    eng.wait_ge(sem("sums_ready"), l + 1)
                    if l == 0:
                        eng.wait_ge(sem("ctx_k"), 1)
                        eng.wait_ge(sem("hc_ready"), 8)
                    for t in range(TT):
                        for d in range(2):
                            if l:
                                wait_full(eng, ("lv", l - 1, d, t))
                    for i, z in enumerate((suf_t, pre_t)):
                        act_(halves_all(wgt_t, b)[i], halves_all(z, b)[i], ACT.Exp).then_inc(sem("wgt_exp"), 1)
                eng.wait_ge(sem("sums_ready"), LEV + 2)
                for t in range(TT):
                    wait_full(eng, ("diag", t))
                act_(qd_t[:, 0:4, :], pre_t[:, 0:4, :], ACT.Exp).then_inc(sem("qd_exp"), 1)
                act_(qd_t[:, 4:8, :], suf_t[:, 4:8, :], ACT.Exp).then_inc(sem("qd_exp"), 1)
                eng.wait_ge(sem("vv_var"), 1)
                act_(bna[:, :, 1:2], bna[:, :, 1:2], ACT.Sqrt).then_inc(sem("vv_root"), 1)
                for j in range(2):
                    wait_full(eng, ("go", j))
                    key = ("go", j)
                    release(act_(o_t[:, 2 * j:2 * j + 2, :].rearrange("p a b -> p (a b)"), bank_of(key)[:, :], ACT.Copy), key)
                for j in range(2):
                    wait_freed(eng, ("go", j))
                act_(o_sq, o_t, ACT.Square).then_inc(sem("go_sq"), 1)
                eng.wait_ge(sem("go_ms"), 2)
                act_(o_sq, o_sq, ACT.Sqrt).then_inc(sem("go_root"), 1)
                for j in range(4):
                    wait_freed(eng, ("mo", j))
                norm(6, resid, buf[5])
                eng.wait_ge(sem("pads_zero"), 4)
                for f in range(FT):
                    key = ("gu", 2, f)
                    wait_full(eng, key)
                    if f >= 2:
                        eng.wait_ge(sem("conv_done"), f - 1)
                    pad = buf[5 + f % 2][:, :, :].rearrange("p a b -> p (a b)")[:, 0:6 * 66].rearrange("p (r c) -> p r c", c=66)
                    act_(pad[:, 1:5, 1:65], bank_of(key)[:, S:2 * S].rearrange("p (r c) -> p r c", c=64), ACT.Copy).then_inc(sem("grid_in"), 1)
                    if f >= 1:
                        eng.wait_ge(sem("conv_done"), f)
                        act_(buf[4][:, (f - 1) % 4, :], buf[4][:, (f - 1) % 4, :], ACT.Gelu).then_inc(sem("gate2"), 1)
                eng.wait_ge(sem("conv_done"), FT)
                act_(buf[4][:, (FT - 1) % 4, :], buf[4][:, (FT - 1) % 4, :], ACT.Gelu).then_inc(sem("gate2"), 1)
                for cb in range(KT):
                    wait_freed(eng, ("dn", 2, cb))
                norm(7, resid, buf[5])

            @block.gpsimd
            def _(pool):
                pool.wait_ge(sem("con_in"), 16)
                for pair in PAIRS:
                    for l in range(LEV):
                        for g in pair:
                            nm = work[:, g % 2, 0, :].rearrange("p (j n) -> p j n", j=4)
                            if l == 0:
                                for j in range(4):
                                    wait_freed(pool, ("sc", g, j))
                                if g >= 2:
                                    wait_full(pool, ("yt", g - 2))
                            elif l == 1:
                                wait_full(pool, ("nt", g))
                                pool.wait_ge(sem("x_ready"), g + 1)
                            else:
                                wait_full(pool, ("y", g, l - 1))
                            nc.gpsimd.tensor_tensor(nm, scores[g % 2][:, :, 0:P], spread(const("right_left", l * P), [P, 4, P]),
                                                    ALU.mult).then_inc(sem(f"nm_ready{g % 2}"), 1)
                pool.wait_ge(sem("mix2_ready"), 8)
                for i in range(2):
                    pad = flat(buf[6 - i])[:, 0:6 * 66].rearrange("p (r c) -> p r c", c=66)
                    if i:
                        wait_full(pool, ("norm", 6))
                    nc.gpsimd.memset(flat(buf[6 - i])[:, 0:6 * 66], 0.0).then_inc(sem("pads_zero"), 2)

            @block.vector
            def _(eng):
                own = Lane(eng, "dve_own")
                v = nc.vector

                def release(ins, key):
                    ins.then_inc(free[jobs[key][0]], 1)

                def norm_root(n):
                    wait_full(eng, ("norm", n))
                    release(v.tensor_scalar(rstd[:, :], bank_of(("norm", n))[:, 0:S], 1.0 / D, NORM_EPS, ALU.mult, ALU.add), ("norm", n))
                    eng.wait_ge(sem("norm_root"), n + 1)
                    own.step(v.reciprocal(rstd[:, :], rstd[:, :]))

                def norm_apply(src, dst, gain_col, ready):
                    for kt in range(KT):
                        v.scalar_tensor_tensor(dst[:, kt, :], src[:, kt, :], gain_col(kt), rstd[:, :], ALU.mult, ALU.mult)\
                            .then_inc(sem(ready), 1)

                def add_resid(name):
                    for j in range(4):
                        key = (name, j)
                        wait_full(eng, key)
                        part = flat(resid)[:, 512 * j:512 * (j + 1)]
                        release(v.tensor_tensor(part, part, bank_of(key)[:, :], ALU.add), key)
                    for j in range(4):
                        wait_freed(eng, (name, j))

                def down_resid(n):
                    for cb in range(KT):
                        key = ("dn", n, cb)
                        wait_full(eng, key)
                        release(v.tensor_tensor(resid[:, cb, :], resid[:, cb, :], bank_of(key)[:, 0:S], ALU.add), key)
                    for cb in range(KT):
                        wait_freed(eng, ("dn", n, cb))

                def ffn(n, gname):
                    norm_root(2 * n + 1)
                    norm_apply(resid, ffn_h, lambda kt: pcol(gname, kt), f"ffn_h{n}")
                    for f in range(FT):
                        key = ("gu", n, f)
                        eng.wait_ge(sem(f"gate{n}"), f + 1)
                        v.tensor_tensor(act(f), buf[4][:, f % 4, :], bank_of(key)[:, S:2 * S], ALU.mult).then_inc(sem(f"act{n}"), 1)
                        eng.wait_ge(sem(f"act{n}"), f + 1)
                        eng.sem_inc(free[jobs[key][0]], 1)
                    down_resid(n)

                eng.wait_ge(sem("col_in"), 16)
                eng.wait_ge(sem("con_in"), 16)
                own.go(v.memset(one_col, 1.0))
                own.go(v.tensor_scalar(one_minus_ka, pcol("k_a", 0, 8), -1.0, 1.0, ALU.mult, ALU.add))
                norm_root(0)
                for kt in range(KT):
                    own.go(v.scalar_tensor_tensor(h_t[:, kt, :], resid[:, kt, :], pcol("g_mix0", kt), rstd[:, :], ALU.mult, ALU.mult))
                own.step(v.memset(one_col, 1.0))
                own.go(v.tensor_tensor(hh_t[:, :, 1:S], h_t[:, :, 0:S - 1], h_t[:, :, 1:S], ALU.subtract))
                own.step(v.tensor_scalar(hh_t[:, :, 0:1], h_t[:, :, 0:1], -1.0, None, ALU.mult))

                def mix(m):
                    if m >= 2:
                        wait_full(eng, last_mix[m - 2])
                    for kt in range(KT):
                        v.scalar_tensor_tensor(mixed[m % 2][:, kt, :], hh_t[:, kt, :], pcol("mu", 8 * mix_of[m] + kt), h_t[:, kt, :],
                                               ALU.mult, ALU.add).then_inc(sem("mix_ready"), 1)

                for m in range(4):
                    mix(m)
                for j in range(4):
                    key = ("l2g", j)
                    wait_full(eng, key)
                    release(v.tensor_copy(flat(g_t)[:, 512 * j:512 * (j + 1)], bank_of(key)[:, :]), key)
                mix(4)
                mix(5)
                eng.wait_ge(sem("mix_ready"), 48)
                for j in range(4):
                    wait_freed(eng, ("k", j))
                for kt in range(KT):
                    ins = v.tensor_scalar(kk_t[:, kt, :], k_t[:, kt, :], pcol("k_k", kt), None, ALU.mult)
                    own.go(ins) if kt < KT - 1 else ins.then_inc(sem("kk_ready"), 1)
                for cb in range(KT):
                    wait_freed(eng, ("l2", cb))
                wait_full(eng, ("v", 3))
                own.step(v.memset(flat(grow_t), 1.0))
                own.step(v.memset(flat(grow_t).rearrange("p (c t) -> p c t", t=P)[:, :, 0:1], 0.0))
                own.step(v.tensor_tensor_scan(flat(cum_t), flat(grow_t), flat(w_t), 0.0, ALU.mult, ALU.add))
                cum_c = flat(cum_t).rearrange("p (c t) -> p c t", t=P)
                mid3 = mid.unsqueeze(2)
                own.step(v.tensor_copy(mid3, cum_c[:, :, CH - 1:CH]))
                own.step(v.tensor_tensor(cum_c, cum_c, mid3.to_broadcast([P, 16, P]), ALU.subtract))
                cum_g = flat(cum_t).rearrange("p (g c t) -> p g c t", c=2, t=P)
                mid_g = mid.rearrange("p (g c) -> p g c", c=2)
                own.go(v.tensor_tensor(send.unsqueeze(2), cum_g[:, :, 0, P - 1:P], mid_g[:, :, 1:2], ALU.add))
                v.tensor_tensor(flat(w_t), flat(cum_t), flat(w_t), ALU.subtract).then_inc(sem("cum_ready"), 1)
                for j in range(4):
                    key = ("kksum", j)
                    wait_full(eng, key)
                    v.tensor_scalar(flat(sq)[:, 512 * j:512 * (j + 1)], bank_of(key)[:, :], 1e-24, None, ALU.max).then_inc(sem("kk_floor"), 1)
                    eng.wait_ge(sem("kk_floor"), j + 1)
                    eng.sem_inc(free[jobs[key][0]], 1)
                eng.wait_ge(sem("kk_root"), 1)
                own.step(v.reciprocal(flat(sq), flat(sq)))
                v.tensor_tensor(flat(kk_t), flat(kk_t), flat(sq), ALU.mult).then_inc(sem("kk_unit"), 1)
                eng.wait_ge(sem("kk_unit"), 1)
                own.step(v.tensor_tensor(flat(b_t), flat(kk_t), flat(a_t), ALU.mult))
                for kt in range(KT):
                    own.go(v.tensor_scalar(a_t[:, kt, :], a_t[:, kt, :], pcol("k_a", kt), one_minus_ka[:, kt:kt + 1], ALU.mult, ALU.add))
                own.step(v.memset(one_col, 1.0))
                own.step(v.tensor_tensor(flat(k_t), flat(k_t), flat(a_t), ALU.mult))
                for j in range(4):
                    wait_freed(eng, ("r", j))
                for kt in range(KT):
                    v.scalar_tensor_tensor(a_t[:, kt, :], r_t[:, kt, :], pcol("r_k", kt), k_t[:, kt, :], ALU.mult, ALU.mult)\
                        .then_inc(sem("bonus_in"), 1)
                eng.wait_ge(sem("decay_a"), 1)
                v.scalar_tensor_tensor(flat(kk_t), flat(kk_t), -1.0, flat(w_t), ALU.mult, ALU.mult).then_inc(sem("tilde_ready"), 1)
                eng.wait_ge(sem("decay_bk"), 1)
                v.tensor_tensor(flat(b_t), flat(b_t), flat(sq), ALU.mult).then_inc(sem("tilde_ready"), 1)
                v.tensor_tensor(flat(k_t), flat(k_t), flat(sq), ALU.mult).then_inc(sem("tilde_ready"), 1)
                eng.wait_ge(sem("decay_r"), 1)
                eng.wait_ge(sem("bonus_in"), 8)
                v.tensor_tensor(flat(r_t), flat(r_t), flat(grow_t), ALU.mult).then_inc(sem("tilde_ready"), 1)
                eng.wait_ge(sem("decay_s"), 1)
                for pair in PAIRS:
                    for g in pair:
                        for j in range(4):
                            key = ("sc", g, j)
                            wait_full(eng, key)
                            if g >= 2:
                                wait_full(eng, ("yt", g - 2))
                            else:
                                wait_full(eng, ("l2g", 3))
                                eng.wait_ge(sem("tilde_ready"), 3)
                            release(v.tensor_tensor(scores[g % 2][:, j, :], bank_of(key)[:, :], const("score_mask", 0, 512), ALU.mult), key)
                    for g in pair:
                        nm, x, xt, y = (work[:, g % 2, i, :].rearrange("p (j n) -> p j n", j=4) for i in range(4))
                        eng.wait_ge(sem(f"nm_ready{g % 2}"), LEV * (g // 2) + 1)
                        v.tensor_tensor(x, nm, spread(ident, [P, 4, P]), ALU.add).then_inc(sem("x_ready"), 1)
                    for g in pair:
                        xt = work[:, g % 2, 2, :].rearrange("p (j n) -> p j n", j=4)
                        key = ("nt", g)
                        wait_full(eng, key)
                        release(v.tensor_tensor(xt, bank_of(key)[:, :].rearrange("p (j n) -> p j n", j=4), spread(ident, [P, 4, P]), ALU.add), key)
                    for l in range(1, LEV):
                        for what in ("dxt", "dx"):
                            if what == "dx" and l == LEV - 1:
                                continue
                            for g in pair:
                                key = (what, g, l)
                                z = work[:, g % 2, 2 if what == "dxt" else 1, :]
                                wait_full(eng, key)
                                if l == 1:
                                    wait_freed(eng, ("nt", g)) if what == "dxt" else eng.wait_ge(sem("x_ready"), g + 1)
                                else:
                                    wait_freed(eng, (what, g, l - 1))
                                release(v.tensor_tensor(z, z, bank_of(key)[:, :], ALU.add), key)
                    for g in pair:
                        key = ("st", g)
                        wait_full(eng, key)
                        release(v.scalar_tensor_tensor(work[:, g % 2, 0, 2 * P:3 * P], bank_of(key)[:, 0:P], send[:, g:g + 1],
                                                       const("head_sum"), ALU.mult, ALU.mult), key)
                for g in range(NG):
                    wait_freed(eng, ("yt", g))
                for j in range(4):
                    key = ("ymean", j)
                    wait_full(eng, key)
                    part = flat(y_t)[:, 512 * j:512 * (j + 1)]
                    v.scalar_tensor_tensor(part, bank_of(key)[:, :], -1.0 / CH, part, ALU.mult, ALU.add).then_inc(sem("y_centered"), 1)
                    eng.wait_ge(sem("y_centered"), j + 1)
                    eng.sem_inc(free[jobs[key][0]], 1)
                for j in range(4):
                    wait_freed(eng, ("bonus", j))
                    wait_freed(eng, ("vt", j))
                own.step(v.tensor_tensor(flat(a_t), flat(a_t), flat(v_t), ALU.mult))
                for j in range(4):
                    key = ("yvar", j)
                    wait_full(eng, key)
                    v.tensor_scalar(flat(sq)[:, 512 * j:512 * (j + 1)], bank_of(key)[:, :], 1.0 / CH, LNX_EPS, ALU.mult, ALU.add).then_inc(sem("y_var"), 1)
                    eng.wait_ge(sem("y_var"), j + 1)
                    eng.sem_inc(free[jobs[key][0]], 1)
                eng.wait_ge(sem("y_root"), 1)
                own.step(v.reciprocal(flat(sq), flat(sq)))
                for kt in range(KT):
                    own.step(v.scalar_tensor_tensor(y_t[:, kt, :], y_t[:, kt, :], pcol("lnx_w", kt), sq[:, kt, :], ALU.mult, ALU.mult))
                    own.step(v.scalar_tensor_tensor(y_t[:, kt, :], y_t[:, kt, :], pcol("lnx_b", kt), a_t[:, kt, :], ALU.add, ALU.add))
                    v.tensor_tensor(y_t[:, kt, :], y_t[:, kt, :], g_t[:, kt, :], ALU.mult).then_inc(sem("y_ready"), 1)
                add_resid("o")
                ffn(0, "g_ffn0")
                norm_root(2)
                norm_apply(resid, hkv_t, lambda kt: pcol("kv_g", kt), "hkv_ready")
                norm_apply(resid, hq_t, lambda kt: pcol("g_mix1", kt), "hq_ready")
                eng.wait_ge(sem("lam_rows_in"), 16)
                lam4 = prow("lam").rearrange("p (a b n) -> p a b n", a=2, b=2)
                own.step(v.tensor_tensor(lam_tmp, lam4[:, :, 0, :], lam4[:, :, 1, :], ALU.mult))
                v.tensor_reduce(lam_t, lam_tmp, AXX, ALU.add).then_inc(sem("lam_in"), 1)
                own.go(v.tensor_scalar(sub_col, pcol("subln"), 1.0 - LAM_INIT, None, ALU.mult))
                for i, name in enumerate(("ak", "aq")):
                    z = (ak_t, aq_t)[i]
                    for j in range(4):
                        key = (name + "sum", j)
                        wait_full(eng, key)
                        v.tensor_scalar(flat(buf[5])[:, 512 * j:512 * (j + 1)], bank_of(key)[:, :], 1.0 / CH, NORM_EPS, ALU.mult, ALU.add)\
                            .then_inc(sem("head_ms"), 1)
                        eng.wait_ge(sem("head_ms"), 4 * i + j + 1)
                        eng.sem_inc(free[jobs[key][0]], 1)
                    eng.wait_ge(sem("head_root"), i + 1)
                    own.step(v.reciprocal(flat(buf[5]), flat(buf[5])))
                    v.scalar_tensor_tensor(flat(z), flat(z), pcol(("k_norm", "q_norm")[i]), flat(buf[5]), ALU.mult, ALU.mult)\
                        .then_inc(sem("head_normed"), 1)
                    eng.wait_ge(sem("head_normed"), i + 1)
                    for j in range(4):
                        key = (name + "rot", j)
                        wait_full(eng, key)
                        release(v.tensor_tensor(turn_t[:, 2 * j:2 * j + 2, :], bank_of(key)[:, :].rearrange("p (a n) -> p a n", a=2),
                                                spread(const("sin", 0, S), [P, 2, S]), ALU.mult), key)
                    own.step(v.tensor_tensor(z[:, :, :], z[:, :, :], spread(const("cos", 0, S), [P, KT, S]), ALU.mult))
                    for j in range(4):
                        wait_freed(eng, (name + "rot", j))
                    v.tensor_tensor(flat(z), flat(z), flat(turn_t), ALU.add).then_inc(sem("roped"), 1)
                eng.wait_ge(sem("lam_exp"), 1)
                own.step(v.tensor_scalar(neg_lam, lam_t[:, 1:2], lam_t[:, 0:1], -LAM_INIT, ALU.subtract, ALU.add))

                def attend_scores(h):
                    for i in range(2):
                        key = ("s", h, i)
                        wait_full(eng, key)
                        if h >= 2:
                            wait_full(eng, ("pt", h - 2))
                        release(v.scalar_tensor_tensor(prob[:, h % 2, i, 0:3 * P], bank_of(key)[:, 0:3 * P], ISS,
                                                       const("chunk_mask", 0, 3 * P), ALU.mult, ALU.add), key)
                    for i in range(2):
                        wait_freed(eng, ("s", h, i))
                    for qt in range(2):
                        p_ = prob[:, h % 2, :, Q_COLS[qt]]
                        own.step(v.tensor_reduce(mx[:, h % 2, 2 * qt:2 * qt + 2], p_, AXX, ALU.max))
                        v.tensor_scalar(mx[:, h % 2, 2 * qt:2 * qt + 2], mx[:, h % 2, 2 * qt:2 * qt + 2], -1.0, None, ALU.mult)\
                            .then_inc(sem("max_ready"), 1)

                def attend_probs(h):
                    eng.wait_ge(sem("exp_done"), 4 * h + 4)
                    own.step(v.reciprocal(sums[:, h % 2, :], sums[:, h % 2, :]))
                    odd = sums[:, h % 2, :].rearrange("p (q i) -> p q i", i=2)[:, :, 1:2]
                    own.step(v.tensor_scalar(odd, odd, neg_lam, None, ALU.mult))
                    for qt in range(2):
                        p0, p1 = (prob[:, h % 2, i, Q_COLS[qt]] for i in range(2))
                        own.step(v.tensor_scalar(p0, p0, sums[:, h % 2, 2 * qt:2 * qt + 1], None, ALU.mult))
                        v.scalar_tensor_tensor(p0, p1, sums[:, h % 2, 2 * qt + 1:2 * qt + 2], p0, ALU.mult, ALU.add)\
                            .then_inc(sem("prob_ready"), 1)

                def attend_out(h):
                    wait_full(eng, ("ao", h))
                    release(v.tensor_copy(ao_t[:, h, :], bank_of(("ao", h))[:, 0:S]), ("ao", h))

                for h in range(8):
                    attend_scores(h)
                    if h >= 1:
                        attend_probs(h - 1)
                    if h >= 2:
                        attend_out(h - 2)
                attend_probs(7)
                attend_out(6)
                attend_out(7)
                for j in range(4):
                    key = ("aosum", j)
                    wait_full(eng, key)
                    v.tensor_scalar(flat(buf[5])[:, 512 * j:512 * (j + 1)], bank_of(key)[:, :], 1.0 / P, SUBLN_EPS, ALU.mult, ALU.add)\
                        .then_inc(sem("ao_ms"), 1)
                    eng.wait_ge(sem("ao_ms"), j + 1)
                    eng.sem_inc(free[jobs[key][0]], 1)
                eng.wait_ge(sem("ao_root"), 1)
                own.step(v.reciprocal(flat(buf[5]), flat(buf[5])))
                for kt in range(KT):
                    v.scalar_tensor_tensor(ao_t[:, kt, :], ao_t[:, kt, :], sub_col, buf[5][:, kt, :], ALU.mult, ALU.mult).then_inc(sem("ao_ready"), 1)
                add_resid("awo")
                ffn(1, "g_ffn1")
                key = ("ada", 0)
                wait_full(eng, key)
                release(v.tensor_tensor(ada, bank_of(key)[:, 0:96].rearrange("p (e c) -> p e c", c=2),
                                        pcol("b_ada", 0, 48).unsqueeze(2).to_broadcast([P, 48, 2]), ALU.add), key)
                wait_freed(eng, key)
                for i, (which, part, g) in enumerate([(0, 1, "norm_mix"), (0, 4, "norm_ffn"), (1, 1, "norm_mix")]):
                    own.step(v.scalar_tensor_tensor(gain[:, 8 * i:8 * i + 8].unsqueeze(2), ada[:, 8 * part:8 * part + 8, which:which + 1], 1.0,
                                                    pcol(g, 0, 8).unsqueeze(2), ALU.add, ALU.mult))

                def modulated(src, dst, i, which, part, ready):
                    for kt in range(KT):
                        own.step(v.scalar_tensor_tensor(dst[:, kt, :], src[:, kt, :], gain[:, 8 * i + kt:8 * i + kt + 1], rstd[:, :], ALU.mult, ALU.mult))
                        v.tensor_scalar(dst[:, kt, :], dst[:, kt, :], ada[:, 8 * part + kt, which:which + 1], None, ALU.add).then_inc(sem(ready), 1)

                norm_root(4)
                modulated(ctx_r, hc_t, 2, 1, 0, "hc_ready")
                norm_root(5)
                modulated(resid, hx_t, 0, 0, 0, "hx_ready")
                cf, ck, xf, xk = (flat(z) for z in (buf[7], buf[8], f_x, k_x))
                for n, (f, a) in enumerate([(cf, flat(buf[9])), (xf, flat(buf[10]))]):
                    for d in range(2):
                        for t in range(TT):
                            wait_freed(eng, ("ctx" if n == 0 else "in", d, t))
                    v.scalar_tensor_tensor(a, f, -1.0, f, ALU.mult, ALU.max).then_inc(sem("gate_abs"), 1)
                eng.wait_ge(sem("gate_log1p"), 1)
                eng.wait_ge(sem("gate_k"), 1)
                v.scalar_tensor_tensor(cf, cf, 0.0, flat(buf[9]), ALU.min, ALU.subtract).then_inc(sem("ctx_log"), 1)
                eng.wait_ge(sem("ctx_log"), 1)
                eng.wait_ge(sem("gate_log1p"), 2)
                eng.wait_ge(sem("gate_k"), 2)
                own.step(v.scalar_tensor_tensor(xf, xf, 0.0, flat(buf[10]), ALU.min, ALU.subtract))
                own.go(v.tensor_copy(pre_t[:, 0:4, :], f_x[:, 0:4, :]))
                own.go(v.memset(pre_t[:, 4:8, :], 0.0))
                own.go(v.memset(suf_t[:, 0:4, :], 0.0))
                v.tensor_copy(suf_t[:, 4:8, :], f_x[:, 4:8, :]).then_inc(sem("sums_ready"), 1)
                eng.wait_ge(sem("sums_ready"), 1)
                for j in range(2):
                    wait_freed(eng, ("in", 3, j))
                own.step(v.tensor_scalar(q_x, q_x, HG_SCALE, None, ALU.mult))
                for j in range(2):
                    wait_full(eng, ("in", 6, j))
                v.tensor_tensor(qd_t[:, 0:4, :], k_x[:, 0:4, :], k_x[:, 4:8, :], ALU.add).then_inc(sem("diag_ready"), 1)
                for d in range(2):
                    for t in range(TT):
                        wait_freed(eng, ("csum", d, t))
                v.tensor_tensor(ck, ck, cf, ALU.mult).then_inc(sem("ctx_k"), 1)
                eng.wait_ge(sem("ctx_k"), 1)
                for t in range(TT):
                    key = ("diag", t)
                    wait_full(eng, key)
                    release(v.tensor_tensor(st_v[:, t, :, t * P:(t + 1) * P], bank_of(key)[:, :].rearrange("p (h n) -> p h n", h=HG),
                                            spread(ident, [P, HG, P]), ALU.mult), key)
                    wait_freed(eng, key)

                def take_scores(l):
                    for d in range(2):
                        for t in range(TT):
                            key = ("lv", l, d, t)
                            wait_full(eng, key)
                            mask = const("left_right" if d == 0 else "right_left", l * P)
                            dst = st_v[:, t, :, t * P:(t + 1) * P]
                            release(v.copy_predicated(dst, spread(mask, [P, HG, P]).bitcast(I32),
                                                      bank_of(key)[:, :].rearrange("p (h n) -> p h n", h=HG)), key)
                            wait_freed(eng, key)

                for l in range(LEV + 1):
                    b = 1 << l
                    eng.wait_ge(sem("wgt_exp"), 2 * l + 2)
                    for d in range(2):
                        wl, wr = halves(wgt_t, d, b)
                        kl, kr = halves(k_x, d, b)
                        ql, qr = (z for z in (lambda t_: (t_[:, :, 0, :], t_[:, :, 1, :]))(q_x.rearrange("p h (n r b) -> p (h n) r b", r=2, b=b)))
                        left, right = (kl, qr) if d == 0 else (ql, kr)
                        own.go(v.tensor_tensor(wl, wl, left, ALU.mult))
                        ins = v.tensor_tensor(wr, wr, right, ALU.mult)
                        own.go(ins) if d == 0 else ins.then_inc(sem("wgt_ready"), 1)
                    pl, pr = halves(pre_t, 0, b)
                    sl, sr = halves(suf_t, 0, b)
                    n = pl.shape[1]
                    own.step(v.tensor_tensor(sl, sl, pr[:, :, b - 1:b].to_broadcast([P, n, b]), ALU.add))
                    own.go(v.tensor_tensor(pr, pr, pl[:, :, b - 1:b].to_broadcast([P, n, b]), ALU.add))
                    pl, pr = halves(pre_t, 1, b)
                    sl, sr = halves(suf_t, 1, b)
                    own.step(v.tensor_tensor(pr, pr, sl[:, :, 0:1].to_broadcast([P, n, b]), ALU.add))
                    v.tensor_tensor(sl, sl, sr[:, :, 0:1].to_broadcast([P, n, b]), ALU.add).then_inc(sem("sums_ready"), 1)
                    eng.wait_ge(sem("sums_ready"), l + 2)
                    if l < LEV:
                        take_scores(l)
                for d in range(2):
                    key = ("cross", d)
                    wait_full(eng, key)
                    release(v.tensor_copy(st_v[:, d, :, (1 - d) * P:(2 - d) * P], bank_of(key)[:, :].rearrange("p (h n) -> p h n", h=HG)), key)
                eng.wait_ge(sem("qd_exp"), 2)
                own.go(v.tensor_tensor(qd_t[:, 0:4, :], qd_t[:, 0:4, :], q_x, ALU.mult))
                v.tensor_tensor(qd_t[:, 4:8, :], qd_t[:, 4:8, :], q_x, ALU.mult).then_inc(sem("qd_ready"), 1)
                for j in range(2):
                    wait_freed(eng, ("in", 6, j))
                vv4 = vv_x.rearrange("p t (h n) -> p t h n", h=HG)
                for i in range(8):
                    own.step(v.bn_stats(bn[:, i, :], vv4[:, i // 4, i % 4, :]))
                    own.step(v.bn_aggr(bna[:, i, :], bn[:, i, :]))
                v.tensor_scalar(bna[:, :, 1:2], bna[:, :, 1:2], NORM_EPS, None, ALU.add).then_inc(sem("vv_var"), 1)
                eng.wait_ge(sem("vv_root"), 1)
                own.step(v.reciprocal(bna[:, :, 1:2], bna[:, :, 1:2]))
                for i in range(8):
                    z = vv4[:, i // 4, i % 4, :]
                    own.go(v.tensor_scalar(z, z, bna[:, i, 0:1], bna[:, i, 1:2], ALU.subtract, ALU.mult))
                own.step(v.memset(one_col, 1.0))
                eng.wait_ge(sem("rows_in"), 16)
                own.step(v.tensor_tensor(vv_x, vv_x, spread(prow("sgu_g"), [P, TT, 512]), ALU.mult))
                v.tensor_tensor(vv_x, vv_x, spread(prow("sgu_b"), [P, TT, 512]), ALU.add).then_inc(sem("vv_ready"), 1)
                for j in range(2):
                    key = ("gsum", j)
                    wait_full(eng, key)
                    v.tensor_scalar(o_sq[:, 2 * j:2 * j + 2, :].rearrange("p a b -> p (a b)"), bank_of(key)[:, :], 1.0 / P, NORM_EPS, ALU.mult, ALU.add)\
                        .then_inc(sem("go_ms"), 1)
                    eng.wait_ge(sem("go_ms"), j + 1)
                    eng.sem_inc(free[jobs[key][0]], 1)
                eng.wait_ge(sem("go_root"), 1)
                own.step(v.reciprocal(o_sq, o_sq))
                for j in range(2):
                    wait_freed(eng, ("in", 4, j))
                    wait_freed(eng, ("in", 5, j))
                for h in range(HG):
                    own.step(v.scalar_tensor_tensor(o_t[:, h, :], o_t[:, h, :], pcol("hg_norm", h), o_sq[:, h, :], ALU.mult, ALU.mult))
                    v.tensor_tensor(mix_t[:, h, :], o_t[:, h, :], gate_x[:, h, :], ALU.mult).then_inc(sem("mix2_ready"), 1)
                for j in range(2):
                    key = ("z", j)
                    wait_full(eng, key)
                    for i in range(2):
                        h = 2 * j + i
                        dst = mix_t[:, HG + h, :].rearrange("p (t n) -> p t n", t=TT)
                        ins = v.tensor_tensor(dst, bank_of(key)[:, i * S:(i + 1) * S].rearrange("p (t n) -> p t n", t=TT),
                                              spread(prow("b_spatial")[:, h * P:(h + 1) * P], [P, TT, P]), ALU.add)
                        if i == 0:
                            own.go(ins)
                        else:
                            release(ins, key)
                    wait_freed(eng, key)
                    for i in range(2):
                        h = 2 * j + i
                        v.tensor_tensor(mix_t[:, HG + h, :], mix_t[:, HG + h, :], u_x[:, h, :], ALU.mult).then_inc(sem("mix2_ready"), 1)
                for j in range(4):
                    key = ("mo", j)
                    wait_full(eng, key)
                    for i in range(2):
                        kt = 2 * j + i
                        ins = v.scalar_tensor_tensor(resid[:, kt, :], bank_of(key)[:, i * S:(i + 1) * S], ada[:, 16 + kt, 0:1], resid[:, kt, :],
                                                     ALU.mult, ALU.add)
                        own.go(ins) if i == 0 else release(ins, key)
                for j in range(4):
                    wait_freed(eng, ("mo", j))
                norm_root(6)
                modulated(resid, ffn_h, 1, 0, 3, "ffn_h2")
                eng.wait_ge(sem("pads_zero"), 4)

                def gated(f):
                    key = ("gu", 2, f)
                    eng.wait_ge(sem("gate2"), f + 1)
                    v.tensor_tensor(act(f), buf[4][:, f % 4, :], bank_of(key)[:, 0:S], ALU.mult).then_inc(sem("act2"), 1)
                    eng.wait_ge(sem("act2"), f + 1)
                    eng.sem_inc(free[jobs[key][0]], 1)

                for f in range(FT):
                    pad = flat(buf[5 + f % 2])[:, 0:6 * 66].rearrange("p (r c) -> p r c", c=66)
                    acc = buf[4][:, f % 4, :].rearrange("p (r c) -> p r c", c=GRID)
                    eng.wait_ge(sem("grid_in"), f + 1)
                    for n, (i, j) in enumerate(TAPS):
                        view = pad[:, i:i + ROWS_X, j:j + GRID]
                        tap = pcol("conv_w", 9 * f + n)
                        if n == 0:
                            own.step(v.tensor_scalar(acc, view, tap, pcol("conv_b", f), ALU.mult, ALU.add))
                        else:
                            ins = v.scalar_tensor_tensor(acc, view, tap, acc, ALU.mult, ALU.add)
                            own.step(ins) if n < 8 else ins.then_inc(sem("conv_done"), 1)
                    if f >= 1:
                        gated(f - 1)
                gated(FT - 1)
                for cb in range(KT):
                    key = ("dn", 2, cb)
                    wait_full(eng, key)
                    release(v.scalar_tensor_tensor(resid[:, cb, :], bank_of(key)[:, 0:S], ada[:, 40 + cb, 0:1], resid[:, cb, :], ALU.mult, ALU.add), key)
                for cb in range(KT):
                    wait_freed(eng, ("dn", 2, cb))
                norm_root(7)
                norm_apply(resid, resid, lambda kt: pcol("norm_final", kt), "out_ready")


def constants():
    z = {}
    i, j = np.arange(P)[:, None], np.arange(P)[None, :]
    z["ident"] = i == j
    lv = [((i >> (l + 1)) == (j >> (l + 1))) & ((i >> l) & 1 == 1) & ((j >> l) & 1 == 0) for l in range(LEV)]
    z["right_left"] = np.concatenate(lv, 1)
    z["left_right"] = np.concatenate([m.T for m in lv], 1)
    z["score_mask"] = np.concatenate([i > j, i <= j, i < j, i <= j], 1)
    z["head_sum"] = i // CH == j // CH
    z["ones"] = np.ones((P, P))
    rope, half = CH // 4, CH // 8
    ci, cj = i % CH, j % CH
    swap = np.zeros((P, P), np.float32)
    swap[(i // CH == j // CH) & (cj < half) & (ci == cj + half)] = -1.0
    swap[(i // CH == j // CH) & (cj >= half) & (cj < rope) & (ci == cj - half)] = 1.0
    z["rope_swap"] = swap
    inv = np.power(np.float32(500000.0), -np.arange(0, rope, 2, dtype=np.float32) / np.float32(rope)).astype(np.float32)
    ang = (np.arange(S, dtype=np.float32)[:, None] * inv[None, :]).astype(np.float32)
    cos, sin = np.ones((P, S), np.float32), np.zeros((P, S), np.float32)
    for c in range(P):
        if c % CH < rope:
            cos[c], sin[c] = np.cos(ang[:, c % half]), np.sin(ang[:, c % half])
    z["cos"], z["sin"] = cos, sin
    mask = np.zeros((P, 3 * P), np.float32)
    mask[0:CH, CH:P] = mask[0:CH, 2 * P + CH:3 * P] = -1e30
    z["chunk_mask"] = mask
    return np.ascontiguousarray(np.concatenate([np.asarray(z[n], np.float32) for n, _ in CONS], 1))


def by_channel(v):
    v = np.asarray(v)
    v = v.reshape(-1, v.shape[-1] // P, P)
    return v.transpose(2, 0, 1).reshape(P, -1)


def wide_chunks(w):
    w = np.asarray(w)
    n = w.shape[1] // 512
    return w.reshape(KT, P, n, 512).transpose(2, 1, 0, 3).reshape(n, P, CHUNK)


def pair_chunks(w):
    w = np.asarray(w).reshape(KT, P, 2, FT // 2, 2 * P)
    return w.transpose(3, 1, 0, 2, 4).reshape(FT // 2, P, CHUNK)


def down_chunks(w):
    w = np.asarray(w).reshape(FT, P, KT, P)
    return w.transpose(2, 1, 0, 3).reshape(KT, P, FT * P)


def layout(x):
    g = {k: np.asarray(v) for k, v in x.items()}
    lora1 = np.zeros((1, P, CHUNK), np.float32)
    l1 = np.concatenate([g["rw_w1"][0], g["rw_a1"][0], g["rw_g1"][0]], 1)
    lora1[0, :, 0:KT * 288] = l1.reshape(KT, P, 288).transpose(1, 0, 2).reshape(P, -1)
    lora2 = np.zeros((1, P, 4, D), np.float32)
    lora2[0, 0:64, 0], lora2[0, 0:64, 1] = g["rw_w2"][0], g["rw_a2"][0]
    lora2[0, :, 2], lora2[0, 0:32, 3] = g["rw_g2"][0][0:P], g["rw_g2"][0][P:]
    wide = [lora1, lora2.reshape(1, P, CHUNK)]
    wide += [wide_chunks(g[n][0]) for n in ("rw_w_k", "rw_w_r", "rw_w_v", "rw_w_o")]
    wide += [pair_chunks(g["ffn_w_gu"][0]), wide_chunks(g["kv_w"]), wide_chunks(g["da_w_q"][0]), wide_chunks(g["da_w_o"][0])]
    wide += [pair_chunks(g["ffn_w_gu"][1]), wide_chunks(g["w_ada_2"][0]), wide_chunks(g["w_in_2"][0]), wide_chunks(g["w_out_2"][0])]
    wide += [pair_chunks(g["w_up_2"][0])]
    down = [down_chunks(g["ffn_w_down"][0]), down_chunks(g["ffn_w_down"][1]), down_chunks(g["w_down_2"][0])]
    twice = lambda v: np.concatenate([v.reshape(1, CH)] * 2, 1)
    c2 = np.stack([g["c_2"][0], g["c_ctx_2"]], 0).reshape(2, KT, P).transpose(2, 1, 0).reshape(P, 16)
    cw = g["conv_w_2"][0].reshape(9, FT, P).transpose(2, 1, 0).reshape(P, 9 * FT)
    cols = {"g_mix0": g["g_mix"][0], "g_mix1": g["g_mix"][1], "g_ffn0": g["g_ffn"][0], "g_ffn1": g["g_ffn"][1], "mu": g["rw_mu"][0],
            "w0": g["rw_w0"], "a0": g["rw_a0"], "k_k": g["rw_k_k"], "k_a": g["rw_k_a"], "r_k": g["rw_r_k"].reshape(1, D),
            "lnx_w": g["rw_lnx_w"], "lnx_b": g["rw_lnx_b"], "kv_g": g["kv_g"], "norm_mix": g["norm_mix_2"], "norm_ffn": g["norm_ffn_2"],
            "norm_final": g["norm_final_2"], "k_norm": twice(g["k_norm_g"]), "q_norm": twice(g["da_q_norm_g"]), "subln": g["da_subln_g"],
            "hg_norm": g["hg_norm_2"], "conv_b": g["conv_b_2"], "b_ada": g["b_ada_2"]}
    cols = {n: by_channel(v) for n, v in cols.items()}
    cols["conv_w"], cols["c"] = cw, c2
    rows = np.concatenate([g["sgu_norm_g_2"][0], g["sgu_norm_b_2"][0], g["b_spatial_2"][0].reshape(-1),
                           g["da_lam_q1"][0], g["da_lam_k1"][0], g["da_lam_q2"][0], g["da_lam_k2"][0]])
    tr = lambda v: v.reshape(S, KT, P).transpose(2, 1, 0)
    made = {"wide": np.concatenate(wide, 0), "down": np.concatenate(down, 0), "x_t": tr(g["x"]), "ctx_t": tr(g["ctx_2"]),
            "cols": np.concatenate([cols[n] for n, _ in COLS], 1), "cons": constants(), "rows": rows.reshape(1, NROW),
            "w_sp": g["w_spatial_2"][0].transpose(2, 0, 1).reshape(P, 512)}
    return {n: np.ascontiguousarray(v) for n, v in made.items()}


def kernel(**inputs):
    import concourse.bacc as _bacc
    from concourse.bass_utils import run_bass_kernel_spmd as _run

    nc = _bacc.Bacc("TRN2", target_bir_lowering=False, num_devices=1)
    arrays = layout(inputs)
    args = {n: nc.dram_tensor(f"in_{n}", a.shape, F32, kind="ExternalInput").ap() for n, a in arrays.items()}
    out = nc.dram_tensor("out_t", (P, KT, S), F32, kind="ExternalOutput").ap()
    build(nc, out=out, **args)
    r = _run(nc, [{f"in_{n}": a for n, a in arrays.items()}], core_ids=[0])
    y = np.asarray(r.results[0]["out_t"])
    return np.ascontiguousarray(y.transpose(2, 1, 0).reshape(1, S, D))
```

```python
import concourse.bass as bass
from concourse import mybir
from contextlib import ExitStack
import math
import numpy as np

F32 = mybir.dt.float32
F32R = mybir.dt.float32r
I32 = mybir.dt.int32
ALU = mybir.AluOpType
ACT = mybir.ActivationFunctionType
AXX = mybir.AxisListType.X

P = 128
D = 1024
KT = D // P
S = 256
TT = S // P
CH = 64
FF = 2816
FT = FF // P
LEV = 7
NG = KT
HG = 4
DECAY_SCALE = math.exp(-0.5)
LAM_INIT = 0.8 - 0.6 * math.exp(-0.3 * 1)
NORM_EPS = 1e-6
LNX_EPS = 64e-5
SUBLN_EPS = 1e-5
CHUNK = KT * 512
HALF = CHUNK // 2
RING = 5
SHARED = ("gu0", "gu2")
DVE_SHARE = 6
HIGHS = 3
NBANK = 8

COLS = [("g_mix0", 8), ("g_mix1", 8), ("g_ffn0", 8), ("g_ffn1", 8), ("mu", 48), ("w0", 8), ("a0", 8),
        ("k_k", 8), ("k_a", 8), ("r_k", 8), ("lnx_w", 8), ("lnx_b", 8), ("kv_g", 8), ("norm_mix", 8),
        ("norm_ffn", 8), ("norm_final", 8), ("k_norm", 1), ("q_norm", 1), ("subln", 1), ("hg_norm", 4),
        ("conv_b", FT), ("conv_w", 9 * FT), ("b_ada", 48), ("c", 16)]
CONS = [("ident", P), ("ones", P), ("head_sum", P), ("right_left", LEV * P), ("left_right", LEV * P), ("score_mask", 4 * P), ("rope_swap", P), ("cos", S), ("sin", S), ("chunk_mask", 3 * P)]
ROWS = [("sgu_g", 512), ("sgu_b", 512), ("b_spatial", 512), ("lam", 256)]


def offsets(table):
    at, out = 0, {}
    for name, n in table:
        out[name] = (at, n)
        at += n
    return out, at


COL_AT, NCOL = offsets(COLS)
CON_AT, NCON = offsets(CONS)
ROW_AT, NROW = offsets(ROWS)

W_AT, N_WIDE = offsets([("lora1", 1), ("lora2", 1), ("k", 2), ("r", 2), ("v", 2), ("o", 2), ("gu0", 11), ("kv", 4), ("aq", 2),
                        ("awo", 2), ("gu1", 11), ("ada", 12), ("in", 7), ("mo", 2), ("gu2", 11)])

IN_ORDER = (0, 1, 3, 2, 4, 5, 6)
IN_TOKENS = (3, 6)


def stream():
    out = []

    def wide(stage, n, name=None, first=0):
        out.extend((stage, i, half, "wide", W_AT[name or stage][0] + first + i) for i in range(n) for half in range(2))

    def down(n):
        out.extend((f"dn{n}", i, half, "down", KT * n + i) for i in range(KT) for half in range(2))

    for stage, n in (("k", 2), ("lora1", 1), ("r", 2), ("v", 2), ("o", 2), ("gu0", 11)):
        wide(stage, n)
    down(0)
    wide("ak", 2, "kv")
    wide("aq", 2)
    wide("av", 2, "kv", 2)
    wide("ctx", 3, "in")
    wide("awo", 2)
    wide("gu1", 11)
    down(1)
    out.extend(("in", i, half, "wide", W_AT["in"][0] + c) for i, c in enumerate(IN_ORDER) for half in range(2))
    wide("mo", 2)
    wide("gu2", 11)
    down(2)
    return out


UNITS = stream()
UNIT_NO = {unit[:3]: u for u, unit in enumerate(UNITS)}
N_ADA = W_AT["ada"][1]


def unit_shape(stage, i):
    if stage == "lora1":
        return KT // 2, 288
    if stage[:2] == "dn":
        return FT // 2, P
    if stage in ("v", "av", "ctx") or (stage == "in" and i in IN_TOKENS):
        return KT // 2, 512
    return KT, S


def build(nc, wide, down, x_t, ctx_t, cols, cons, rows, w_sp, out):
    with ExitStack() as ctx:
        place_of = {}
        sbuf_at = [(nc.sbuf_base + 63) // 64 * 64]

        def sb(name, shape, dt=F32):
            place_of[name] = sbuf_at[0]
            sbuf_at[0] += (math.prod(shape[1:]) * 4 + 63) // 64 * 64
            return nc.alloc_sbuf_tensor_at(name, shape, dt, offset=place_of[name])

        def rounded(name, of, shape):
            return nc.alloc_sbuf_tensor_at(name, shape, F32R, offset=place_of[of])

        sems = {}

        def sem(name):
            if name not in sems:
                sems[name] = ctx.enter_context(nc.semaphore(name))
            return sems[name]

        ring = sb("ring", [P, RING, HALF])
        high = sb("high", [P, HIGHS, HALF], F32R)
        resid = sb("resid", [P, KT, S])
        col = sb("col", [P, NCOL])
        con = sb("con", [P, NCON])
        buf = [sb(f"buf{i}", [P, KT, S]) for i in range(12)]
        rstd = sb("rstd", [P, S])
        tiny = sb("tiny", [P, 640])
        work = sb("work", [P, 2, 4, 512])
        ring_r = rounded("ring_r", "ring", [P, RING, HALF])
        part = [rounded(f"part{i}", f"buf{i}", [P, KT, S]) for i in range(12)]
        banks = [ctx.enter_context(nc.psum_tensor(f"bank{i}", [P, 512], F32)) for i in range(NBANK)]

        def pcol(name, i=0, n=1):
            return col[:, COL_AT[name][0] + i:COL_AT[name][0] + i + n]

        def const(name, i=0, n=P):
            return con[:, CON_AT[name][0] + i:CON_AT[name][0] + i + n]

        def flat(t):
            return t[:, :, :].rearrange("p a b -> p (a b)")

        def piece(t, j):
            return flat(t)[:, 512 * j:512 * (j + 1)]

        def prow(name):
            if name == "lam":
                return tiny[:, 384:640]
            return work[:, 0, 1 + ROW_AT[name][0] // 512, :]

        ident = const("ident")

        jobs = {}
        uses = [0] * NBANK
        order = []

        def place(key):
            b = len(order) % NBANK
            jobs[key] = (b, uses[b])
            uses[b] += 1
            order.append(key)

        unit_end = {}
        mids = [0]

        def unit_mid(stage, i, half):
            mids[0] += 1
            unit_end[UNIT_NO[(stage, i, half)]] = ("unit_used", mids[0])

        def unit_job(stage, i, half, key):
            unit_end[UNIT_NO[(stage, i, half)]] = key

        def plan_proj(name):
            for c in range(2):
                for j in range(2):
                    place((name, 2 * c + j))
                    unit_job(name, c, j, (name, 2 * c + j))

        def plan_tokens(stage, c, keys):
            for key in keys:
                place(key)
            unit_mid(stage, c, 0)
            unit_job(stage, c, 1, keys[-1])

        def plan_gu(n, c):
            for i in range(2):
                place(("gu", n, 2 * c + i))
                unit_job(f"gu{n}", c, i, ("gu", n, 2 * c + i))

        def plan_down(n, after_first=()):
            for cb in range(KT):
                if cb == 1:
                    for key in after_first:
                        place(key)
                place(("dn", n, cb))
                unit_mid(f"dn{n}", cb, 0)
                unit_job(f"dn{n}", cb, 1, ("dn", n, cb))

        place(("norm", 0))
        plan_proj("k")
        for i in range(4):
            place(("l1", i))
        unit_job("lora1", 0, 0, ("l1", 3))
        unit_job("lora1", 0, 1, ("l1", 3))
        for j in range(4):
            place(("l2g", j))
        for cb in range(KT):
            place(("l2", cb))
        for j in range(4):
            place(("kksum", j))
        plan_proj("r")
        for c in range(2):
            plan_tokens("v", c, [("v", 2 * c), ("v", 2 * c + 1)])
        for n in ("bt", "kt"):
            for j in range(2):
                place((n, j))
        PAIRS = [(0, 1), (2, 3), (4, 5), (6, 7)]
        for pair in PAIRS:
            for g in pair:
                for j in range(4):
                    place(("sc", g, j))
            if pair[0] == 0:
                for j in range(4):
                    place(("bonus", j))
                for j in range(4):
                    place(("vt", j))
            for g in pair:
                place(("nt", g))
            for l in range(1, LEV):
                for what in ("y", "dxt") + (("dx",) if l < LEV - 1 else ()):
                    for g in pair:
                        place((what, g, l))
            for what in ("q0", "sa0", "st", "q1", "sa1", "yt"):
                for g in pair:
                    place((what, g))
        for n in ("ymean", "yvar"):
            for j in range(4):
                place((n, j))
        plan_proj("o")
        place(("norm", 1))
        for c in range(11):
            plan_gu(0, c)
            if c >= 1:
                place(("ada", c - 1))
        plan_down(0, (("ada", 10), ("ada", 11), ("norm", 2)))
        place(("norm", 3))
        plan_proj("ak")
        plan_proj("aq")
        for n in ("aksum", "aqsum"):
            for j in range(4):
                place((n, j))
        plan_tokens("av", 0, [("av", 0), ("av", 1)])
        for n in ("akrot", "aqrot"):
            for j in range(4):
                place((n, j))
        plan_tokens("av", 1, [("av", 2), ("av", 3)])
        for h in range(8):
            place(("s", h, 0))
            place(("s", h, 1))
            if h % 2 == 0 and h < 6:
                plan_tokens("ctx", h // 2, [("ctx", h // 2, 0), ("ctx", h // 2, 1)])
            if h >= 1:
                place(("pt", h - 1))
                place(("ao", h - 1))
            if h in (4, 6):
                place(("aosum", h // 2 - 2))
        place(("pt", 7))
        place(("ao", 7))
        for j in (2, 3):
            place(("aosum", j))
        plan_proj("awo")
        place(("norm", 4))
        for c in range(11):
            plan_gu(1, c)
            if c == 4:
                for d in range(2):
                    for t in range(TT):
                        place(("csum", d, t))
            if c == 7:
                for d in range(2):
                    place(("cstate", d))
        plan_down(1)
        place(("norm", 5))

        def plan_in(d):
            if d in IN_TOKENS:
                plan_tokens("in", d, [("in", d, 0), ("in", d, 1)])
            else:
                for j in range(2):
                    place(("in", d, j))
                    unit_job("in", d, j, ("in", d, j))

        for d in range(4):
            plan_in(d)
        for t in range(TT):
            place(("diag", t))
        for d in range(3, 7):
            if d > 3:
                plan_in(d)
            for l in (2 * (d - 3), 2 * (d - 3) + 1):
                if l < LEV:
                    for t in range(TT):
                        for dr in range(2):
                            place(("lv", l, dr, t))
        for d in range(2):
            place(("cross", d))
        for name in ("go", "gsum", "z"):
            for j in range(2):
                place((name, j))
        plan_proj("mo")
        place(("norm", 6))
        for c in range(11):
            plan_gu(2, c)
        plan_down(2)
        place(("norm", 7))

        full = [sem(f"bank_full{b}") for b in range(NBANK)]
        free = [sem(f"bank_free{b}") for b in range(NBANK)]
        slot_full = [sem(f"slot_full{r}") for r in range(RING)]

        def bank_of(key):
            return banks[jobs[key][0]]

        def wait_full(eng, key):
            b, use = jobs[key]
            eng.wait_ge(full[b], use + 1)

        def wait_freed(eng, key):
            b, use = jobs[key]
            eng.wait_ge(free[b], use + 1)

        def wait_unit(eng, u):
            end = unit_end[u]
            if end[0] == "unit_used":
                eng.wait_ge(sem("unit_used"), end[1])
            else:
                wait_full(eng, end)

        def wait_slot(eng, u):
            eng.wait_ge(slot_full[u % RING], 16 * (u // RING + 1))

        def unit_views(u):
            k, n = unit_shape(*UNITS[u][:2])
            return [t[:, 0:k * n].rearrange("p (k n) -> p k n", n=n) for t in (ring[:, u % RING], ring_r[:, u % RING], high[:, u % HIGHS])]

        class Lane:

            def __init__(self, eng, name):
                self.eng, self.sem, self.n = eng, sem(name), 0

            def go(self, ins):
                self.n += 1
                ins.then_inc(self.sem, 1)

            def settle(self):
                self.eng.wait_ge(self.sem, self.n)

            def step(self, ins):
                self.go(ins)
                self.settle()

        def spread(ap, shape):
            return ap.unsqueeze(1).to_broadcast(shape)

        def halves(t, d, b):
            v = t[:, 4 * d:4 * d + 4, :].rearrange("p h (n r b) -> p (h n) r b", r=2, b=b)
            return v[:, :, 0, :], v[:, :, 1, :]

        def halves_all(t, b):
            v = t[:, :, :].rearrange("p h (n r b) -> p (h n) r b", r=2, b=b)
            return v[:, :, 0, :], v[:, :, 1, :]

        SPLITS = ["mix0", "mix1", "mix2", "mix3", "mix4", "mix5", "y", "ffn0", "hc", "hkv", "hq", "ao", "ffn1", "hx", "mix", "ffn2"]
        LOW_BUF = {"mix0": 2, "mix1": 3, "mix2": 6, "mix3": 2, "mix4": 3, "mix5": 2, "y": 3, "ffn0": 0, "hc": 11, "hkv": 0, "hq": 2,
                   "ao": 9, "ffn1": 0, "hx": 0, "mix": 3, "ffn2": 0}
        HIGH_BUF = {"mix0": 10, "mix1": 11, "mix2": 8, "mix3": 10, "mix4": 11, "mix5": 10, "y": 10, "ffn0": 1, "hc": 10, "hkv": 1, "hq": 3,
                    "ao": 2, "ffn1": 1, "hx": 1, "mix": 9, "ffn2": 1}

        def value_of(name):
            return buf[LOW_BUF[name]]

        def low_of(name):
            return part[LOW_BUF[name]]

        def high_of(name):
            return part[HIGH_BUF[name]]

        def part_value(name, j):
            return 4 * SPLITS.index(name) + j + 1

        TAPS = [(i, j) for i in range(3) for j in range(3)]
        ROWS_X, GRID = S // 64, 64
        h_t, hh_t = buf[0], buf[1]
        k_t, r_t, a_t, w_t, g_t, v_tok = buf[4], buf[5], buf[6], buf[7], buf[8], buf[9]
        lora = buf[5]
        lora_out = [buf[9], buf[7]]
        kk_t, b_t = buf[0], buf[1]
        grow_t, cum_t = (work[:, i, :, :].rearrange("p a b -> p (a b)") for i in range(2))
        bk_tok = flat(buf[2])
        v_t, y_t = buf[7], buf[3]
        v_tokf = v_tok[:, :, :].rearrange("p (t a) b -> p t (a b)", t=TT)
        scores = [buf[10][:, :, :].rearrange("p (j a) b -> p j (a b)", j=4),
                  buf[11][:, :, :].rearrange("p (j a) b -> p j (a b)", j=4)]
        y_sq = buf[11]
        mix_of = [2, 1, 4, 5, 0, 3]
        buffers_free = {3: ("k", 3), 4: ("l1", 0), 5: ("l1", 3)}
        NORM_SQ = [buf[4], buf[9], buf[9], buf[9], buf[10], buf[9], buf[10], buf[9]]
        ak_t, aq_t, ao_t = buf[4], buf[6], buf[9]
        k_sq, q_sq, ao_sq = buf[7], buf[9], buf[3]
        av_tok = buf[5][:, :, :].rearrange("p (t a) b -> p t (a b)", t=TT)
        turn_t = buf[8]
        prob = buf[7][:, :, :].rearrange("p (w i q) n -> p w i (q n)", w=2, i=2)
        Q_COLS = [slice(0, P), slice(P, 3 * P)]
        prob_t = buf[8][:, :, :].rearrange("p (w a) n -> p w (a n)", w=2)

        def act_value(f):
            return buf[2 + f // 8][:, f % 8, :]

        def act_low(f):
            return part[2 + f // 8][:, f % 8, :]

        def act_high(f):
            return part[5 + f // 8][:, f % 8, :]

        def gate_tmp(f):
            return buf[8][:, f % 4, :]

        def grid(f):
            return buf[8][:, 4 + 2 * (f % 2):6 + 2 * (f % 2), :].rearrange("p a b -> p (a b)")[:, 0:6 * 66].rearrange("p (r c) -> p r c", c=66)

        ctx_r = buf[11]
        f_c = work[:, 0, :, :].rearrange("p (d t) n -> p d t n", d=2)
        v_c = work[:, 1, 0:2, :]
        k_c = buf[10][:, :, :].rearrange("p (d t a) n -> p d t (a n)", d=2, t=TT)
        cf, ck, c_log = f_c.rearrange("p d t n -> p (d t n)"), flat(buf[10]), flat(buf[11])
        state = work[:, 1, 2:4, :]
        wsp = work[:, 0, 0, :]
        f_x, k_x = buf[2], buf[3]
        q_x, u_x = buf[4][:, 0:4, :], buf[4][:, 4:8, :]
        gate_x = buf[5][:, 0:4, :]
        v_x = buf[5][:, 4:8, :].rearrange("p (t a) n -> p t (a n)", t=TT)
        vv_x = buf[6][:, 0:4, :].rearrange("p (t a) n -> p t (a n)", t=TT)
        pre_t, suf_t, st_t, qd_t = buf[9], buf[10], buf[7], buf[8]
        wgt = [buf[11], buf[2]]
        st_v = st_t[:, :, :].rearrange("p (t h) n -> p t h n", t=TT)
        mix_t = buf[3]
        o_t, o_sq = buf[2][:, 0:4, :], buf[2][:, 4:8, :]
        ada = tiny[:, 0:96].rearrange("p (e c) -> p e c", c=2)
        silu_c = tiny[:, 96:112].rearrange("p (k c) -> p k c", c=2)
        gain = tiny[:, 112:136]
        mid = tiny[:, 136:152]
        send = tiny[:, 152:160]
        one_minus_ka = tiny[:, 160:168]
        mx = tiny[:, 168:176].rearrange("p (w n) -> p w n", w=2)
        sums = tiny[:, 176:184].rearrange("p (w n) -> p w n", w=2)
        lam_t = tiny[:, 184:186]
        neg_lam = tiny[:, 186:187]
        sub_col = tiny[:, 187:188]
        one_col, eps_norm, eps_lnx, eps_sub = (tiny[:, i:i + 1] for i in (188, 189, 190, 191))
        bn = tiny[:, 192:192 + 8 * 6].rearrange("p (a s) -> p a s", a=8)
        bna = tiny[:, 240:256].rearrange("p (a s) -> p a s", a=8)
        lam_tmp = tiny[:, 256:384].rearrange("p (a n) -> p a n", a=2)
        ISS = CH ** -0.5
        HG_SCALE = float(P) ** -0.5

        def ada_acc(c):
            return work[:, c % 2, 0:2, :]

        def ada_w(half):
            return buf[9 + half][:, :, :].rearrange("p (k a) n -> p k (a n)", k=KT // 2)

        def load_x(eng, j):
            eng.dma_start(resid[:, 2 * j:2 * j + 2, :], x_t[:, 2 * j:2 * j + 2, :]).then_inc(sem(f"x_in{j}"), 16)

        with nc.Block() as block:
            @block.sync
            def _(sp):
                for j in (2, 3):
                    load_x(sp, j)
                first = CON_AT["right_left"][0]
                sp.dma_start(con[:, 0:first], cons[:, 0:first]).then_inc(sem("con_in"), 16)
                for j in range(4):
                    sp.wait_ge(sem(f"x_in{j}"), 16)
                for u, (stage, i, half, which, at) in enumerate(UNITS):
                    if u == RING:
                        sp.dma_start(con[:, first:NCON], cons[:, first:NCON]).then_inc(sem("masks_in"), 16)
                    if u >= RING:
                        wait_unit(sp, u - RING)
                    k, n = unit_shape(stage, i)
                    if n == S:
                        src = wide[at].rearrange("p (k n) -> p k n", k=KT)[:, :, n * half:n * (half + 1)]
                    else:
                        src = (wide if which == "wide" else down)[at][:, k * n * half:k * n * (half + 1)].rearrange("p (k n) -> p k n", n=n)
                    sp.dma_start(unit_views(u)[0], src).then_inc(slot_full[u % RING], 16)
                for t in range(KT):
                    sp.wait_ge(sem("out_ready"), t + 1)
                    sp.dma_start(out[:, t, :], resid[:, t, :]).then_inc(sem("out_done"), 16)
                sp.wait_ge(sem("out_done"), 16 * KT)

            @block.tensor
            def _(pe):
                mm = nc.tensor.matmul

                def open_bank(key):
                    b, use = jobs[key]
                    if use > 0:
                        pe.wait_ge(free[b], use)
                    return banks[b]

                def close(ins, key):
                    ins.then_inc(full[jobs[key][0]], 1)

                def arrived(stage, i, half):
                    u = UNIT_NO[(stage, i, half)]
                    pe.wait_ge(sem("unit_low"), u + 1)
                    if stage in SHARED:
                        pe.wait_ge(sem("unit_low_rest"), FT * SHARED.index(stage) + 2 * i + half + 1)
                    return unit_views(u)[1:]

                def split_mm(bank, lhs, rhs, start, stop):
                    (al, ah), (bl, bh) = lhs, rhs
                    mm(bank, ah, bh, start=start, stop=False)
                    mm(bank, ah, bl, start=False, stop=False)
                    return mm(bank, al, bh, start=False, stop=stop)

                def tile_of(name, kt, tok=slice(0, S)):
                    return low_of(name)[:, kt, tok], high_of(name)[:, kt, tok]

                def wait_part(name, kt):
                    pe.wait_ge(sem("part_low"), part_value(name, kt // 2))

                def norm(n):
                    bank = open_bank(("norm", n))
                    for kt in range(KT):
                        if kt % 2 == 0:
                            pe.wait_ge(sem("norm_sq"), 4 * n + kt // 2 + 1)
                        last = mm(bank[:, 0:S], const("ones"), NORM_SQ[n][:, kt, :], start=kt == 0, stop=kt == KT - 1)
                    close(last, ("norm", n))

                def columns(bank, w, c0, x, first):
                    for kt in range(KT):
                        if first:
                            wait_part(x, kt)
                        last = split_mm(bank, [z[:, kt, c0:c0 + P] for z in w], tile_of(x, kt), kt == 0, kt == KT - 1)
                    return last

                def project(name, x):
                    for c in range(2):
                        for j in range(2):
                            w = arrived(name, c, j)
                            bank = open_bank((name, 2 * c + j))
                            for half in range(2):
                                last = columns(bank[:, half * S:(half + 1) * S], w, half * P, x, c + j + half == 0)
                            close(last, (name, 2 * c + j))

                def tokens(stage, i, keys, x, first, which=(0, 1)):
                    for half in which:
                        w = arrived(stage, i, half)
                        for t in range(TT):
                            bank = banks[jobs[keys[t]][0]] if half else open_bank(keys[t])
                            for k in range(KT // 2):
                                kt = KT // 2 * half + k
                                if first and t == 0:
                                    wait_part(x, kt)
                                last = split_mm(bank[:, :], tile_of(x, kt, slice(t * P, (t + 1) * P)), [z[:, k, :] for z in w],
                                                kt == 0, kt == KT - 1)
                            if half:
                                close(last, keys[t])
                        if not half:
                            last.then_inc(sem("unit_used"), 1)

                def sums_over(name, lhs, src, before):
                    for j in range(4):
                        before(j)
                        bank = open_bank((name, j))
                        close(mm(bank[:, :], lhs, piece(src, j), start=True, stop=True), (name, j))

                def gate_up(n, c):
                    for i in range(2):
                        w = arrived(f"gu{n}", c, i)
                        key = ("gu", n, 2 * c + i)
                        bank = open_bank(key)
                        columns(bank[:, 0:S], w, 0, f"ffn{n}", c + i == 0)
                        close(columns(bank[:, S:2 * S], w, P, f"ffn{n}", False), key)

                def down_proj(n, after_first=lambda: None):
                    for cb in range(KT):
                        if cb == 1:
                            after_first()
                        bank = open_bank(("dn", n, cb))
                        for half in range(2):
                            w = arrived(f"dn{n}", cb, half)
                            for k in range(FT // 2):
                                f = FT // 2 * half + k
                                if cb == 0:
                                    pe.wait_ge(sem("act_ready"), FT * n + f + 1)
                                last = split_mm(bank[:, 0:S], [z[:, k, :] for z in w], (act_low(f), act_high(f)), f == 0, f == FT - 1)
                            if half:
                                close(last, ("dn", n, cb))
                            else:
                                last.then_inc(sem("unit_used"), 1)

                pe.wait_ge(sem("con_in"), 16)
                norm(0)
                project("k", "mix0")
                wl0, wl1 = arrived("lora1", 0, 0), arrived("lora1", 0, 1)
                for i, (c0, m, src) in enumerate([(0, 64, 1), (64, 64, 2), (128, 128, 3), (256, 32, 3)]):
                    bank = open_bank(("l1", i))
                    for kt in range(KT):
                        wait_part(f"mix{src}", kt)
                        w = (wl0, wl1)[kt // 4]
                        last = split_mm(bank[0:m, 0:S], [z[:, kt % 4, c0:c0 + m] for z in w], tile_of(f"mix{src}", kt), kt == 0, kt == KT - 1)
                    close(last, ("l1", i))
                w = [lora_out[i // 2][:, 4 * (i % 2):4 * (i % 2) + 4, :].rearrange("p a b -> p (a b)") for i in range(4)]
                pe.wait_ge(sem("lora2_in"), 32)
                wait_freed(pe, ("l1", 2))
                wait_freed(pe, ("l1", 3))
                for j in range(4):
                    bank = open_bank(("l2g", j))
                    for half in range(2):
                        cb = 2 * j + half
                        mm(bank[:, half * S:(half + 1) * S], w[2][:, cb * P:(cb + 1) * P], lora[:, 2, :], start=True, stop=False)
                        last = mm(bank[:, half * S:(half + 1) * S], w[3][0:32, cb * P:(cb + 1) * P], lora[0:32, 3, :], start=False, stop=True)
                    close(last, ("l2g", j))
                wait_freed(pe, ("l1", 0))
                wait_freed(pe, ("l1", 1))
                for cb in range(KT):
                    bank = open_bank(("l2", cb))
                    mm(bank[:, 0:S], w[0][0:64, cb * P:(cb + 1) * P], lora[0:64, 0, :], start=True, stop=True)
                    close(mm(bank[:, S:2 * S], w[1][0:64, cb * P:(cb + 1) * P], lora[0:64, 1, :], start=True, stop=True), ("l2", cb))
                sums_over("kksum", const("head_sum"), buf[1], lambda j: pe.wait_ge(sem("kk_sq"), 1))
                project("r", "mix4")
                for c in range(2):
                    tokens("v", c, [("v", 2 * c), ("v", 2 * c + 1)], "mix5", c == 0)
                for name, src in (("bt", b_t), ("kt", k_t)):
                    pe.wait_ge(sem("tilde_ready"), 2 if name == "bt" else 3)
                    for j in range(2):
                        bank = open_bank((name, j))
                        for i in range(4):
                            last = nc.tensor.transpose(bank[:, i * P:(i + 1) * P], src[:, 4 * j + i, 0:P], ident)
                        close(last, (name, j))
                pe.wait_ge(sem("tilde_ready"), 4)
                pe.wait_ge(sem("masks_in"), 16)
                for pair in PAIRS:
                    for g in pair:
                        for c in range(2):
                            for hd in range(2):
                                key = ("sc", g, 2 * c + hd)
                                bank = open_bank(key)
                                part = slice(hd * CH, hd * CH + CH)
                                tok = slice(c * P, (c + 1) * P)
                                at_, bt_, kt_, rt_ = (z[part, g, tok] for z in (kk_t, b_t, k_t, r_t))
                                mm(bank[:, 0:P], at_, bt_, start=True, stop=True)
                                mm(bank[:, P:2 * P], bt_, rt_, start=True, stop=True)
                                mm(bank[:, 2 * P:3 * P], kt_, at_, start=True, stop=True)
                                close(mm(bank[:, 3 * P:4 * P], kt_, rt_, start=True, stop=True), key)
                    if pair[0] == 0:
                        sums_over("bonus", const("head_sum"), a_t, lambda j: pe.wait_ge(sem("bonus_in"), 2 * j + 2))
                        for j in range(4):
                            wait_freed(pe, ("v", j))
                        for j in range(4):
                            bank = open_bank(("vt", j))
                            for half in range(2):
                                for t in range(TT):
                                    last = nc.tensor.transpose(bank[:, half * S + t * P:half * S + (t + 1) * P],
                                                               v_tokf[:, t, (2 * j + half) * P:(2 * j + half + 1) * P], ident)
                            close(last, ("vt", j))
                    for g in pair:
                        nm = work[:, g % 2, 0, :]
                        pe.wait_ge(sem(f"nm_ready{g % 2}"), LEV * (g // 2) + 1)
                        bank = open_bank(("nt", g))
                        for j in range(4):
                            last = nc.tensor.transpose(bank[:, j * P:(j + 1) * P], nm[:, j * P:(j + 1) * P], ident)
                        close(last, ("nt", g))
                    for l in range(1, LEV):
                        for g in pair:
                            nm, x, xt, y = (work[:, g % 2, i, :] for i in range(4))
                            pe.wait_ge(sem(f"nm_ready{g % 2}"), LEV * (g // 2) + l + 1)
                            wait_freed(pe, ("nt", g) if l == 1 else ("dxt", g, l - 1))
                            bank = open_bank(("y", g, l))
                            for j in range(4):
                                s_ = slice(j * P, (j + 1) * P)
                                last = mm(bank[:, s_], nm[:, s_], xt[:, s_], start=True, stop=True)
                            close(last, ("y", g, l))
                        for g in pair:
                            nm, x, xt, y = (work[:, g % 2, i, :] for i in range(4))
                            wait_freed(pe, ("y", g, l))
                            if l == 1:
                                pe.wait_ge(sem("x_ready"), g + 1)
                            else:
                                wait_freed(pe, ("dx", g, l - 1))
                            bank = open_bank(("dxt", g, l))
                            for j in range(4):
                                s_ = slice(j * P, (j + 1) * P)
                                last = mm(bank[:, s_], x[:, s_], y[:, s_], start=True, stop=True)
                            close(last, ("dxt", g, l))
                        if l < LEV - 1:
                            for g in pair:
                                nm, x, xt, y = (work[:, g % 2, i, :] for i in range(4))
                                bank = open_bank(("dx", g, l))
                                for j in range(4):
                                    s_ = slice(j * P, (j + 1) * P)
                                    last = mm(bank[:, s_], y[:, s_], x[:, s_], start=True, stop=True)
                                close(last, ("dx", g, l))
                    for what in ("q0", "sa0", "st", "q1", "sa1", "yt"):
                        for g in pair:
                            key = (what, g)
                            sc = scores[g % 2]
                            xt = work[:, g % 2, 2, :]
                            q0, sa0, st, q1 = (work[:, g % 2, 0, i * P:(i + 1) * P] for i in range(4))
                            sa1 = work[:, g % 2, 3, 0:P]
                            if what == "sa0":
                                wait_freed(pe, ("q0", g))
                                wait_freed(pe, ("dxt", g, LEV - 1))
                            elif what != "q0":
                                wait_freed(pe, ({"st": "sa0", "q1": "st", "sa1": "q1", "yt": "sa1"}[what], g))
                            if what == "st" and g == 0:
                                for i in range(2):
                                    wait_freed(pe, ("bt", i))
                                    wait_freed(pe, ("kt", i))
                            bank = open_bank(key)
                            if what in ("q0", "q1"):
                                c = int(what[1])
                                if c:
                                    mm(bank[:, 0:P], kk_t[:, g, P:S], st, start=True, stop=False)
                                for hd in range(2):
                                    o = hd * CH
                                    last = mm(bank[:, o:o + CH], sc[:, 2 * c + hd, 2 * P:3 * P], v_tokf[:, c, g * P + o:g * P + o + CH],
                                              start=c == 0, stop=c == 0 or hd == 1)
                            elif what in ("sa0", "sa1"):
                                c = int(what[2])
                                for hd in range(2):
                                    o = hd * CH
                                    j = 2 * c + hd
                                    last = mm(bank[:, o:o + CH], xt[:, j * P:(j + 1) * P], (q0, q1)[c][:, o:o + CH], start=True, stop=True)
                            elif what == "st":
                                mm(bank[:, 0:P], bk_tok[:, g * P:(g + 1) * P], sa0, start=True, stop=False)
                                last = mm(bank[:, 0:P], bk_tok[:, D + g * P:D + (g + 1) * P], v_tokf[:, 0, g * P:(g + 1) * P], start=False, stop=True)
                            else:
                                for hd in range(2):
                                    o = hd * CH
                                    for c in range(2):
                                        dst = bank[o:o + CH, c * P:(c + 1) * P]
                                        mm(dst, (sa0, sa1)[c][:, o:o + CH], sc[:, 2 * c + hd, P:2 * P], start=True, stop=False)
                                        last = mm(dst, v_tokf[:, c, g * P + o:g * P + o + CH], sc[:, 2 * c + hd, 3 * P:4 * P],
                                                  start=False, stop=c == 0)
                                        if c:
                                            last = mm(dst, st[:, o:o + CH], r_t[:, g, P:S], start=False, stop=True)
                            close(last, key)
                for g in range(NG):
                    wait_freed(pe, ("yt", g))
                sums_over("ymean", const("head_sum"), y_t, lambda j: None)
                sums_over("yvar", const("head_sum"), y_sq, lambda j: pe.wait_ge(sem("y_sq"), j + 1))
                project("o", "y")
                norm(1)

                def ada_sum(c):
                    pe.wait_ge(sem("ada_read"), 2 * c + 2)
                    bank = open_bank(("ada", c))
                    for i in range(4):
                        for which in range(2 if c < 4 else 1):
                            last = mm(bank[:, 2 * i + which:2 * i + which + 1], ada_acc(c)[:, which, i * P:(i + 1) * P], one_col,
                                      start=True, stop=True)
                    close(last, ("ada", c))

                for c in range(11):
                    gate_up(0, c)
                    if c >= 1:
                        ada_sum(c - 1)

                def rest_of_context():
                    ada_sum(10)
                    ada_sum(11)
                    norm(2)

                down_proj(0, rest_of_context)
                norm(3)
                project("ak", "hkv")
                project("aq", "hq")
                for i, name in enumerate(("aksum", "aqsum")):
                    sums_over(name, const("head_sum"), (k_sq, q_sq)[i], lambda j: pe.wait_ge(sem("head_sq"), 4 * i + j + 1))
                tokens("av", 0, [("av", 0), ("av", 1)], "hkv", False)
                for i, name in enumerate(("akrot", "aqrot")):
                    sums_over(name, const("rope_swap"), (ak_t, aq_t)[i], lambda j: pe.wait_ge(sem("head_normed"), i + 1))
                tokens("av", 1, [("av", 2), ("av", 3)], "hkv", False)

                def values(h):
                    pe.wait_ge(sem("prob_ready"), 2 * h + 2)
                    bank = open_bank(("pt", h))
                    p_ = prob[:, h % 2]
                    for i in range(3):
                        last = nc.tensor.transpose(bank[:, i * P:(i + 1) * P], p_[:, 0, i * P:(i + 1) * P], ident)
                    close(last, ("pt", h))
                    wait_freed(pe, ("pt", h))
                    bank = open_bank(("ao", h))
                    t_ = prob_t[:, h % 2, :]
                    mm(bank[:, 0:S], av_tok[:, 0, h * P:(h + 1) * P], t_[:, 0:S], start=True, stop=False)
                    close(mm(bank[:, P:S], av_tok[:, 1, h * P:(h + 1) * P], t_[:, S:S + P], start=False, stop=True), ("ao", h))

                def sum_heads(j):
                    pe.wait_ge(sem("ao_sq"), j + 1)
                    bank = open_bank(("aosum", j))
                    close(mm(bank[:, :], const("ones"), piece(ao_sq, j), start=True, stop=True), ("aosum", j))

                for i in range(4):
                    wait_freed(pe, ("av", i))
                pe.wait_ge(sem("roped"), 2)
                for h in range(8):
                    for i in range(2):
                        bank = open_bank(("s", h, i))
                        o = i * CH
                        for qt in range(2):
                            last = mm(bank[:, Q_COLS[qt]], aq_t[o:o + CH, h, qt * P:(qt + 1) * P],
                                      ak_t[o:o + CH, h, 0:(qt + 1) * P], start=True, stop=True)
                        close(last, ("s", h, i))
                    if h < 6:
                        tokens("ctx", h // 2, [("ctx", h // 2, 0), ("ctx", h // 2, 1)], "hc", h < 2, (h % 2,))
                    if h >= 1:
                        values(h - 1)
                    if h in (4, 6):
                        sum_heads(h // 2 - 2)
                values(7)
                sum_heads(2)
                sum_heads(3)
                project("awo", "ao")
                norm(4)
                for c in range(11):
                    gate_up(1, c)
                    if c == 4:
                        pe.wait_ge(sem("ctx_log"), 1)
                        for d in range(2):
                            tri = const("score_mask", (0, 2)[d] * P)
                            for t in range(TT):
                                bank = open_bank(("csum", d, t))
                                other = t == d
                                last = mm(bank[:, :], tri, f_c[:, d, t, :], start=True, stop=not other)
                                if other:
                                    last = mm(bank[:, :], const("ones"), f_c[:, d, 1 - t, :], start=False, stop=True)
                                close(last, ("csum", d, t))
                    if c == 7:
                        pe.wait_ge(sem("ctx_k"), 1)
                        for d in range(2):
                            bank = open_bank(("cstate", d))
                            for h in range(HG):
                                for t in range(TT):
                                    last = mm(bank[:, h * P:(h + 1) * P], k_c[:, d, t, h * P:(h + 1) * P], v_c[:, t, h * P:(h + 1) * P],
                                              start=t == 0, stop=t == TT - 1)
                            close(last, ("cstate", d))
                down_proj(1)
                norm(5)

                def in_proj(d):
                    if d in IN_TOKENS:
                        tokens("in", d, [("in", d, 0), ("in", d, 1)], "hx", False)
                        return
                    for j in range(2):
                        w = arrived("in", d, j)
                        bank = open_bank(("in", d, j))
                        for half in range(2):
                            last = columns(bank[:, half * S:(half + 1) * S], w, half * P, "hx", d + j + half == 0)
                        close(last, ("in", d, j))

                def level(l):
                    pe.wait_ge(sem("wgt_ready"), l + 1)
                    for t in range(TT):
                        for dr in range(2):
                            bank = open_bank(("lv", l, dr, t))
                            for h in range(HG):
                                z = wgt[l % 2][:, 4 * dr + h, t * P:(t + 1) * P]
                                last = mm(bank[:, h * P:(h + 1) * P], z, z, start=True, stop=True)
                            close(last, ("lv", l, dr, t))

                for d in range(4):
                    in_proj(d)
                pe.wait_ge(sem("diag_ready"), 1)
                for t in range(TT):
                    bank = open_bank(("diag", t))
                    tok = slice(t * P, (t + 1) * P)
                    for h in range(HG):
                        last = mm(bank[:, h * P:(h + 1) * P], qd_t[:, h, tok], q_x[:, h, tok], start=True, stop=True)
                    close(last, ("diag", t))
                for d in range(3, 7):
                    if d > 3:
                        in_proj(d)
                    for l in (2 * (d - 3), 2 * (d - 3) + 1):
                        if l < LEV:
                            level(l)
                pe.wait_ge(sem("wgt_ready"), LEV + 1)
                for d in range(2):
                    bank = open_bank(("cross", d))
                    s_tok, t_tok = (slice(0, P), slice(P, S)) if d == 0 else (slice(P, S), slice(0, P))
                    for h in range(HG):
                        z = wgt[LEV % 2][:, 4 * d + h, :]
                        last = mm(bank[:, h * P:(h + 1) * P], z[:, s_tok], z[:, t_tok], start=True, stop=True)
                    close(last, ("cross", d))
                pe.wait_ge(sem("qd_ready"), 1)
                for d in range(2):
                    wait_freed(pe, ("cross", d))
                for j in range(2):
                    bank = open_bank(("go", j))
                    for i in range(2):
                        h = 2 * j + i
                        dst = bank[:, i * S:(i + 1) * S]
                        for t in range(TT):
                            mm(dst, v_x[:, t, h * P:(h + 1) * P], st_v[:, t, h, :], start=t == 0, stop=False)
                        for d in range(2):
                            last = mm(dst, state[:, d, h * P:(h + 1) * P], qd_t[:, 4 * d + h, :], start=False, stop=d == 1)
                    close(last, ("go", j))
                for j in range(2):
                    pe.wait_ge(sem("go_sq"), j + 1)
                    bank = open_bank(("gsum", j))
                    close(mm(bank[:, :], const("ones"), o_sq[:, 2 * j:2 * j + 2, :].rearrange("p a b -> p (a b)"), start=True, stop=True),
                          ("gsum", j))
                pe.wait_ge(sem("vv_ready"), 1)
                pe.wait_ge(sem("wsp_in"), 16)
                for j in range(2):
                    bank = open_bank(("z", j))
                    for i in range(2):
                        h = 2 * j + i
                        for t in range(TT):
                            last = mm(bank[:, i * S + t * P:i * S + (t + 1) * P], vv_x[:, t, h * P:(h + 1) * P], wsp[:, h * P:(h + 1) * P],
                                      start=True, stop=True)
                    close(last, ("z", j))
                project("mo", "mix")
                norm(6)
                for c in range(11):
                    gate_up(2, c)
                down_proj(2)
                norm(7)

            @block.scalar
            def _(eng):
                own = Lane(eng, "act_own")
                act_ = nc.scalar.activation
                done = [0]

                def release(ins, key):
                    ins.then_inc(free[jobs[key][0]], 1)

                def split_to(n):
                    while done[0] < min(n, len(UNITS)):
                        u = done[0]
                        wait_slot(eng, u)
                        if u >= HIGHS:
                            wait_unit(eng, u - HIGHS)
                        raw, _, hi = unit_views(u)
                        act_(hi, raw, ACT.Copy).then_inc(sem("unit_high"), 1)
                        done[0] += 1

                def ahead(stage, i, half):
                    split_to(UNIT_NO[(stage, i, half)] + HIGHS + 1)

                def part_of(name, j):
                    eng.wait_ge(sem("part_raw"), part_value(name, j))
                    act_(piece(high_of(name), j), piece(value_of(name), j), ACT.Copy).then_inc(sem("part_high"), 1)

                def parts(name):
                    for j in range(4):
                        part_of(name, j)

                def square(n, src, j):
                    act_(piece(NORM_SQ[n], j), piece(src, j), ACT.Square).then_inc(sem("norm_sq"), 1)

                def root(n):
                    wait_full(eng, ("norm", n))
                    act_(rstd[:, :], bank_of(("norm", n))[:, 0:S], ACT.Ln, scale=1.0 / D, bias=eps_norm).then_inc(free[jobs[("norm", n)][0]], 1)
                    wait_freed(eng, ("norm", n))
                    act_(rstd[:, :], rstd[:, :], ACT.Exp, scale=-0.5).then_inc(sem("norm_root"), 1)

                def norm(n, src):
                    for j in range(4):
                        square(n, src, j)
                    root(n)

                def proj_out(name, dst):
                    for j in range(4):
                        wait_full(eng, (name, j))
                        release(act_(piece(dst, j), bank_of((name, j))[:, :], ACT.Copy), (name, j))
                        ahead(name, j // 2, j % 2)

                def tokens_out(stage, c, keys, dst):
                    ahead(stage, c, 0)
                    for t in range(TT):
                        wait_full(eng, keys[t])
                        release(act_(dst(t), bank_of(keys[t])[:, :], ACT.Copy), keys[t])
                    ahead(stage, c, 1)

                def rsqrt_of(jobs_out, n, eps, signal):
                    for key, dst in jobs_out:
                        wait_full(eng, key)
                        release(act_(dst, bank_of(key)[:, :], ACT.Ln, scale=1.0 / n, bias=eps), key)
                    for key, dst in jobs_out:
                        wait_freed(eng, key)
                        act_(dst, dst, ACT.Exp, scale=-0.5).then_inc(sem(signal), 1)

                def gate_high(n, f):
                    eng.wait_ge(sem("act_raw"), FT * n + f + 1)
                    act_(act_high(f), act_value(f), ACT.Copy).then_inc(sem("act_high"), 1)

                def ffn(n, between=lambda c: None):
                    for f in range(FT):
                        key = ("gu", n, f)
                        wait_full(eng, key)
                        if f >= 4:
                            eng.wait_ge(sem("act_raw"), FT * n + f - 3)
                        act_(gate_tmp(f), bank_of(key)[:, 0:S], ACT.Silu).then_inc(sem("gate"), 1)
                        ahead(f"gu{n}", f // 2, f % 2)
                        gate_high(n, f)
                        if f % 2:
                            between(f // 2)

                def down(n, norm_no):
                    for cb in range(KT + 2):
                        if cb < KT:
                            for half in range(2):
                                ahead(f"dn{n}", cb, half)
                        if cb % 2 == 0 and cb >= 2:
                            for done_ in (cb - 2, cb - 1):
                                wait_freed(eng, ("dn", n, done_))
                            square(norm_no, resid, cb // 2 - 1)
                    root(norm_no)

                for j in (0, 1):
                    load_x(eng, j)
                eng.dma_start(col[:, :], cols).then_inc(sem("col_in"), 16)
                eng.dma_start(prow("lam"), rows[0:1, 1536:NROW].partition_broadcast(P)).then_inc(sem("lam_rows_in"), 16)
                for j in range(4):
                    eng.wait_ge(sem(f"x_in{j}"), 16)
                    square(0, resid, j)
                lora2 = [wide[W_AT["lora2"][0]][:, HALF * i:HALF * (i + 1)] for i in range(2)]
                for i in range(2):
                    eng.dma_start(flat(lora_out[i]), lora2[i]).then_inc(sem("lora2_in"), 16)
                eng.wait_ge(sem("eps_ready"), 1)
                split_to(1)
                root(0)
                split_to(HIGHS)
                parts("mix0")
                parts("mix1")

                def lora_in(i):
                    m, f = [(64, ACT.Tanh), (64, ACT.Copy), (128, ACT.Sigmoid), (32, ACT.Sigmoid)][i]
                    wait_full(eng, ("l1", i))
                    release(act_(lora[0:m, i, :], bank_of(("l1", i))[0:m, 0:S], f), ("l1", i))

                for j in range(4):
                    wait_full(eng, ("k", j))
                    release(act_(piece(k_t, j), bank_of(("k", j))[:, :], ACT.Copy), ("k", j))
                    ahead("k", j // 2, j % 2)
                    if j == 0:
                        parts("mix2")
                parts("mix3")
                lora_in(0)
                parts("mix4")
                lora_in(1)
                lora_in(2)
                lora_in(3)
                ahead("lora1", 0, 1)
                parts("mix5")
                eng.wait_ge(sem("kk_ready"), 1)
                act_(flat(buf[1]), flat(kk_t), ACT.Square).then_inc(sem("kk_sq"), 1)
                for cb in range(KT):
                    key = ("l2", cb)
                    wait_full(eng, key)
                    own.go(act_(w_t[:, cb, :], bank_of(key)[:, 0:S], ACT.Sigmoid, bias=pcol("w0", cb)))
                    release(act_(a_t[:, cb, :], bank_of(key)[:, S:2 * S], ACT.Sigmoid, bias=pcol("a0", cb)), key)
                eng.wait_ge(sem("kk_floor"), 4)
                act_(flat(buf[1]), flat(buf[1]), ACT.Sqrt).then_inc(sem("kk_root"), 1)
                proj_out("r", r_t)
                tokens_out("v", 0, [("v", 0), ("v", 1)], lambda t: v_tokf[:, t, 0:512])
                eng.wait_ge(sem("cum_ready"), 1)
                act_(flat(w_t), flat(w_t), ACT.Exp, scale=-DECAY_SCALE).then_inc(sem("decay_a"), 1)
                act_(send, send, ACT.Exp, scale=-DECAY_SCALE).then_inc(sem("decay_s"), 1)
                act_(grow_t, cum_t, ACT.Exp, scale=-DECAY_SCALE).then_inc(sem("decay_r"), 1)
                eng.wait_ge(sem("decay_r"), 1)
                act_(cum_t, cum_t, ACT.Exp, scale=DECAY_SCALE).then_inc(sem("decay_bk"), 1)
                tokens_out("v", 1, [("v", 2), ("v", 3)], lambda t: v_tokf[:, t, 512:1024])
                for i, name in enumerate(("bt", "kt")):
                    for j in range(2):
                        wait_full(eng, (name, j))
                        release(act_(bk_tok[:, i * D + 512 * j:i * D + 512 * (j + 1)], bank_of((name, j))[:, :], ACT.Copy), (name, j))
                for name, dst in (("bonus", a_t), ("vt", v_t)):
                    for j in range(4):
                        wait_full(eng, (name, j))
                        release(act_(piece(dst, j), bank_of((name, j))[:, :], ACT.Copy), (name, j))
                for pair in PAIRS:
                    for l in range(1, LEV):
                        for g in pair:
                            key = ("y", g, l)
                            wait_full(eng, key)
                            release(act_(work[:, g % 2, 3, :], bank_of(key)[:, :], ACT.Copy), key)
                    for what in ("q0", "sa0", "q1", "sa1", "yt"):
                        for g in pair:
                            key = (what, g)
                            wait_full(eng, key)
                            if what == "yt":
                                dst, src = y_t[:, g, :], bank_of(key)[:, 0:S]
                            else:
                                i = {"q0": 0, "sa0": 1, "q1": 3}.get(what)
                                dst = work[:, g % 2, 3, 0:P] if i is None else work[:, g % 2, 0, i * P:(i + 1) * P]
                                src = bank_of(key)[:, 0:P]
                            release(act_(dst, src, ACT.Copy), key)
                for j in range(4):
                    eng.wait_ge(sem("y_centered"), j + 1)
                    act_(piece(y_sq, j), piece(y_t, j), ACT.Square).then_inc(sem("y_sq"), 1)
                rsqrt_of([(("yvar", j), piece(y_sq, j)) for j in range(4)], CH, eps_lnx, "y_root")
                parts("y")

                def project_resid(name, norm_no):
                    for j in range(5):
                        if j < 4:
                            ahead(name, j // 2, j % 2)
                        if j:
                            wait_freed(eng, (name, j - 1))
                            square(norm_no, resid, j - 1)
                    root(norm_no)

                project_resid("o", 1)
                parts("ffn0")
                eng.dma_start(ctx_r[:, :, :], ctx_t).then_inc(sem("ctx_in"), 16)
                act_(silu_c, pcol("c", 0, 16).rearrange("p (k c) -> p k c", c=2), ACT.Silu).then_inc(sem("silu_c"), 1)
                ffn(0)
                eng.wait_ge(sem("ctx_in"), 16)
                eng.wait_ge(sem("ada_read"), 2 * N_ADA)
                for j in range(4):
                    square(2, ctx_r, j)
                for half in range(2):
                    ahead("dn0", 0, half)
                root(2)
                parts("hc")
                down(0, 3)
                parts("hkv")
                parts("hq")
                for name, dst, sq in (("ak", ak_t, k_sq), ("aq", aq_t, q_sq)):
                    for j in range(5):
                        if j < 4:
                            wait_full(eng, (name, j))
                            release(act_(piece(dst, j), bank_of((name, j))[:, :], ACT.Copy), (name, j))
                            ahead(name, j // 2, j % 2)
                        if j:
                            wait_freed(eng, (name, j - 1))
                            act_(piece(sq, j - 1), piece(dst, j - 1), ACT.Square).then_inc(sem("head_sq"), 1)
                rsqrt_of([((name, j), piece(sq, j)) for name, sq in (("aksum", k_sq), ("aqsum", q_sq)) for j in range(4)],
                         CH, eps_norm, "head_root")
                for c in range(2):
                    tokens_out("av", c, [("av", 2 * c), ("av", 2 * c + 1)], lambda t: av_tok[:, t, 512 * c:512 * (c + 1)])
                eng.wait_ge(sem("lam_in"), 1)
                act_(lam_t, lam_t, ACT.Exp).then_inc(sem("lam_exp"), 1)

                def square_heads(j):
                    wait_freed(eng, ("ao", 2 * j))
                    wait_freed(eng, ("ao", 2 * j + 1))
                    act_(piece(ao_sq, j), piece(ao_t, j), ACT.Square).then_inc(sem("ao_sq"), 1)

                def root_heads(j):
                    rsqrt_of([(("aosum", j), piece(ao_sq, j))], P, eps_sub, "ao_root")

                def move_pt(h):
                    wait_full(eng, ("pt", h))
                    release(act_(prob_t[:, h % 2, 0:3 * P], bank_of(("pt", h))[:, 0:3 * P], ACT.Copy), ("pt", h))

                for h in range(8):
                    for qt in range(2):
                        eng.wait_ge(sem("max_ready"), 2 * h + qt + 1)
                        for i in range(2):
                            p_ = prob[:, h % 2, i, Q_COLS[qt]]
                            act_(p_, p_, ACT.Exp, bias=mx[:, h % 2, 2 * qt + i:2 * qt + i + 1],
                                 accum_out=sums[:, h % 2, 2 * qt + i:2 * qt + i + 1]).then_inc(sem("exp_done"), 1)
                    if h < 6:
                        d = h // 2
                        ahead("ctx", d, 0) if h % 2 == 0 else \
                            tokens_out("ctx", d, [("ctx", d, 0), ("ctx", d, 1)], lambda t: v_c[:, t, :] if d == 2 else f_c[:, d, t, :])
                    if h >= 1:
                        move_pt(h - 1)
                    if h in (3, 5, 7):
                        square_heads((h - 3) // 2)
                    if h in (4, 6):
                        root_heads(h // 2 - 2)
                move_pt(7)
                root_heads(2)
                part_of("ao", 0)
                part_of("ao", 1)
                square_heads(3)
                part_of("ao", 2)
                root_heads(3)
                part_of("ao", 3)
                project_resid("awo", 4)
                parts("ffn1")

                def context_gates(c):
                    if c == 1:
                        for d in range(2):
                            for t in range(TT):
                                wait_freed(eng, ("ctx", d, t))
                        act_(ck, cf, ACT.Sigmoid, scale=-1.0).then_inc(sem("gate_k"), 1)
                        eng.wait_ge(sem("gate_abs"), 1)
                        own.step(act_(c_log, c_log, ACT.Exp, scale=-1.0))
                        act_(c_log, c_log, ACT.Ln, bias=one_col).then_inc(sem("gate_log1p"), 1)
                    if c == 5:
                        for d in range(2):
                            for t in range(TT):
                                wait_full(eng, ("csum", d, 1))
                                release(act_(f_c[:, d, t, :], bank_of(("csum", d, t))[:, :], ACT.Exp), ("csum", d, t))
                    if c == 8:
                        for d in range(2):
                            wait_full(eng, ("cstate", d))
                            release(act_(state[:, d, :], bank_of(("cstate", d))[:, :], ACT.Copy), ("cstate", d))
                        eng.dma_start(wsp, w_sp).then_inc(sem("wsp_in"), 16)
                        eng.dma_start(work[:, 0, 1:4, :].rearrange("p a b -> p (a b)"), rows[0:1, 0:1536].partition_broadcast(P))\
                           .then_inc(sem("rows_in"), 16)

                ffn(1, context_gates)
                down(1, 5)
                parts("hx")

                def in_out(d, dst):
                    for j in range(2):
                        key = ("in", d, j)
                        wait_full(eng, key)
                        release(act_(dst[:, 2 * j:2 * j + 2, :].rearrange("p a b -> p (a b)"), bank_of(key)[:, :], ACT.Copy), key)
                        ahead("in", d, j)

                xf, xk, x_log = flat(f_x), flat(k_x), flat(suf_t)
                in_out(0, f_x[:, 0:4, :])
                in_out(1, f_x[:, 4:8, :])
                for d in range(2):
                    for t in range(TT):
                        wait_freed(eng, ("in", d, t))
                eng.wait_ge(sem("gate_abs"), 2)
                own.step(act_(x_log, x_log, ACT.Exp, scale=-1.0))
                act_(x_log, x_log, ACT.Ln, bias=one_col).then_inc(sem("gate_log1p"), 1)
                act_(xk, xf, ACT.Sigmoid, scale=-1.0).then_inc(sem("gate_k"), 1)
                for j in range(2):
                    key = ("in", 2, j)
                    wait_full(eng, key)
                    release(act_(q_x[:, 2 * j:2 * j + 2, :].rearrange("p a b -> p (a b)"), bank_of(key)[:, :], ACT.Silu), key)
                    ahead("in", 2, j)

                def level_exp(l):
                    b = 1 << l
                    eng.wait_ge(sem("sums_ready"), l + 1)
                    if l >= 2:
                        for t in range(TT):
                            for d in range(2):
                                wait_full(eng, ("lv", l - 2, d, t))
                    for i, z in enumerate((suf_t, pre_t)):
                        act_(halves_all(wgt[l % 2], b)[i], halves_all(z, b)[i], ACT.Exp).then_inc(sem("wgt_exp"), 1)

                level_exp(0)
                level_exp(1)
                for d in range(3, 7):
                    if d == 3:
                        tokens_out("in", d, [("in", d, 0), ("in", d, 1)], lambda t: v_x[:, t, :])
                    elif d == 6:
                        tokens_out("in", d, [("in", d, 0), ("in", d, 1)], lambda t: vv_x[:, t, :])
                    else:
                        in_out(d, {4: gate_x, 5: u_x}[d])
                    for l in (2 * (d - 2), 2 * (d - 2) + 1):
                        if l <= LEV:
                            level_exp(l)
                for t in range(TT):
                    wait_full(eng, ("diag", t))
                eng.wait_ge(sem("sums_ready"), LEV + 2)
                act_(qd_t[:, 0:4, :], pre_t[:, 0:4, :], ACT.Exp).then_inc(sem("qd_exp"), 1)
                act_(qd_t[:, 4:8, :], suf_t[:, 4:8, :], ACT.Exp).then_inc(sem("qd_exp"), 1)
                for j in range(2):
                    wait_freed(eng, ("in", 6, j))
                    wait_freed(eng, ("in", 5, j))
                    wait_freed(eng, ("in", 4, j))
                act_(vv_x, vv_x, ACT.Gelu).then_inc(sem("gelu_done"), 1)
                act_(u_x, u_x, ACT.Gelu).then_inc(sem("gelu_done"), 1)
                act_(gate_x, gate_x, ACT.Silu).then_inc(sem("gate_x"), 1)
                for j in range(2):
                    key = ("go", j)
                    wait_full(eng, key)
                    release(act_(o_t[:, 2 * j:2 * j + 2, :].rearrange("p a b -> p (a b)"), bank_of(key)[:, :], ACT.Copy), key)
                for j in range(2):
                    wait_freed(eng, ("go", j))
                    act_(o_sq[:, 2 * j:2 * j + 2, :], o_t[:, 2 * j:2 * j + 2, :], ACT.Square).then_inc(sem("go_sq"), 1)
                eng.wait_ge(sem("vv_var"), 1)
                act_(bna[:, :, 1:2], bna[:, :, 1:2], ACT.Sqrt).then_inc(sem("vv_root"), 1)
                rsqrt_of([(("gsum", j), o_sq[:, 2 * j:2 * j + 2, :].rearrange("p a b -> p (a b)")) for j in range(2)], P, eps_norm, "go_root")
                parts("mix")
                project_resid("mo", 6)
                parts("ffn2")
                eng.wait_ge(sem("pads_zero"), 1)

                def gelu_of(f):
                    eng.wait_ge(sem("conv_done"), f + 1)
                    act_(gate_tmp(f), gate_tmp(f), ACT.Gelu).then_inc(sem("gate"), 1)

                for f in range(FT):
                    key = ("gu", 2, f)
                    wait_full(eng, key)
                    if f >= 2:
                        eng.wait_ge(sem("conv_done"), f - 1)
                    act_(grid(f)[:, 1:5, 1:65], bank_of(key)[:, S:2 * S].rearrange("p (r c) -> p r c", c=64), ACT.Copy).then_inc(sem("grid_in"), 1)
                    if f >= 4:
                        eng.wait_ge(sem("act_raw"), FT * 2 + f - 3)
                    act_(gate_tmp(f), bank_of(key)[:, S:2 * S], ACT.Identity, scale=pcol("conv_w", 9 * f + TAPS.index((1, 1))),
                         bias=pcol("conv_b", f)).then_inc(sem("tap_in"), 1)
                    ahead("gu2", f // 2, f % 2)
                    if f >= 1:
                        gelu_of(f - 1)
                    if f >= 2:
                        gate_high(2, f - 2)
                gelu_of(FT - 1)
                gate_high(2, FT - 2)
                gate_high(2, FT - 1)
                down(2, 7)

            @block.gpsimd
            def _(pool):
                own = Lane(pool, "pool_own")
                own.step(nc.gpsimd.memset(grow_t, 1.0))
                nc.gpsimd.memset(grow_t.rearrange("p (c t) -> p c t", t=P)[:, :, 0:1], 0.0).then_inc(sem("scan_mask"), 1)
                pool.wait_ge(sem("masks_in"), 16)
                pool.wait_ge(sem("tilde_ready"), 4)
                for pair in PAIRS:
                    for l in range(LEV):
                        for g in pair:
                            nm = work[:, g % 2, 0, :].rearrange("p (j n) -> p j n", j=4)
                            if l == 0:
                                for j in range(4):
                                    wait_freed(pool, ("sc", g, j))
                                if g >= 2:
                                    wait_full(pool, ("yt", g - 2))
                            elif l == 1:
                                wait_full(pool, ("nt", g))
                                pool.wait_ge(sem("x_ready"), g + 1)
                            else:
                                wait_full(pool, ("y", g, l - 1))
                            nc.gpsimd.tensor_tensor(nm, scores[g % 2][:, :, 0:P], spread(const("right_left", l * P), [P, 4, P]),
                                                    ALU.mult).then_inc(sem(f"nm_ready{g % 2}"), 1)
                def act_low_part(n, f):
                    key = ("gu", n, f)
                    pool.wait_ge(sem("act_high"), FT * n + f + 1)
                    nc.gpsimd.tensor_tensor(act_low(f), act_value(f), act_high(f).bitcast(F32), ALU.subtract).then_inc(sem("act_ready"), 1)
                    pool.sem_inc(free[jobs[key][0]], 1)

                def low_rest(stage, f):
                    u = UNIT_NO[(stage, f // 2, f % 2)]
                    pool.wait_ge(sem("unit_high"), u + 1)
                    raw, low, hi = (z[:, DVE_SHARE:KT, :] for z in unit_views(u))
                    nc.gpsimd.tensor_tensor(low, raw, hi.bitcast(F32), ALU.subtract).then_inc(sem("unit_low_rest"), 1)

                def load_ada(n):
                    c, half = n // 2, n % 2
                    if c >= 1:
                        pool.wait_ge(sem("ada_read"), n - 1)
                    pool.dma_start(ada_w(half), wide[W_AT["ada"][0] + c][:, HALF * half:HALF * (half + 1)].rearrange("p (k n) -> p k n", n=512))\
                        .then_inc(sem(f"ada_in{half}"), 16)

                wait_full(pool, ("norm", 1))
                load_ada(0)
                load_ada(1)
                for f in range(HIGHS):
                    low_rest("gu0", f)
                for f in range(FT):
                    if f + HIGHS < FT:
                        low_rest("gu0", f + HIGHS)
                    if f >= 1:
                        act_low_part(0, f - 1)
                    for n in ([f + 2] if f < 20 else [22, 23] if f == 20 else []):
                        load_ada(n)
                act_low_part(0, FT - 1)
                for f in range(FT):
                    act_low_part(1, f)
                add = nc.gpsimd.tensor_tensor
                pool.wait_ge(sem("sums_ready"), 1)
                for l in range(LEV + 1):
                    b = 1 << l
                    pool.wait_ge(sem("wgt_exp"), 2 * l + 2)
                    pl, pr = halves(pre_t, 0, b)
                    sl, sr = halves(suf_t, 0, b)
                    n = pl.shape[1]
                    own.step(add(sl, sl, pr[:, :, b - 1:b].to_broadcast([P, n, b]), ALU.add))
                    own.go(add(pr, pr, pl[:, :, b - 1:b].to_broadcast([P, n, b]), ALU.add))
                    pl, pr = halves(pre_t, 1, b)
                    sl, sr = halves(suf_t, 1, b)
                    own.step(add(pr, pr, sl[:, :, 0:1].to_broadcast([P, n, b]), ALU.add))
                    add(sl, sl, sr[:, :, 0:1].to_broadcast([P, n, b]), ALU.add).then_inc(sem("sums_ready"), 1)
                    pool.wait_ge(sem("sums_ready"), l + 2)
                for j in range(2):
                    wait_full(pool, ("go", j))
                nc.gpsimd.memset(buf[8][:, 4:8, :].rearrange("p a b -> p (a b)"), 0.0).then_inc(sem("pads_zero"), 1)

                for f in range(HIGHS):
                    low_rest("gu2", f)
                for f in range(FT):
                    if f + HIGHS < FT:
                        low_rest("gu2", f + HIGHS)
                    act_low_part(2, f)

            @block.vector
            def _(eng):
                own = Lane(eng, "dve_own")
                v = nc.vector
                done = [0]

                def release(ins, key):
                    ins.then_inc(free[jobs[key][0]], 1)

                def split_to(n):
                    while done[0] < min(n, len(UNITS)):
                        u = done[0]
                        eng.wait_ge(sem("unit_high"), u + 1)
                        raw, low, hi = unit_views(u)
                        if UNITS[u][0] in SHARED:
                            raw, low, hi = (z[:, 0:DVE_SHARE, :] for z in (raw, low, hi))
                        v.tensor_tensor(low, raw, hi.bitcast(F32), ALU.subtract).then_inc(sem("unit_low"), 1)
                        done[0] += 1

                def ahead(stage, i, half):
                    split_to(UNIT_NO[(stage, i, half)] + HIGHS + 1)

                def low_piece(name, j):
                    eng.wait_ge(sem("part_high"), part_value(name, j))
                    v.tensor_tensor(piece(low_of(name), j), piece(value_of(name), j), piece(high_of(name), j).bitcast(F32), ALU.subtract).then_inc(sem("part_low"), 1)

                def lows(name):
                    for j in range(4):
                        low_piece(name, j)

                def emit(ins, kt):
                    if kt % 2:
                        ins.then_inc(sem("part_raw"), 1)
                    else:
                        own.go(ins)

                def norm_root(n):
                    eng.wait_ge(sem("norm_root"), n + 1)

                def norm_apply(src, name, gain_col):
                    for kt in range(KT):
                        emit(v.scalar_tensor_tensor(value_of(name)[:, kt, :], src[:, kt, :], gain_col(kt), rstd[:, :], ALU.mult, ALU.mult), kt)
                        if kt % 2 and kt >= 3:
                            low_piece(name, kt // 2 - 1)
                    low_piece(name, 3)

                def add_resid(name):
                    for j in range(4):
                        key = (name, j)
                        ahead(name, j // 2, j % 2)
                        wait_full(eng, key)
                        release(v.tensor_tensor(piece(resid, j), piece(resid, j), bank_of(key)[:, :], ALU.add), key)
                    for j in range(4):
                        wait_freed(eng, (name, j))

                def down_resid(n, add):
                    for cb in range(KT):
                        key = ("dn", n, cb)
                        for half in range(2):
                            ahead(f"dn{n}", cb, half)
                        wait_full(eng, key)
                        release(add(cb, bank_of(key)[:, 0:S]), key)
                    for cb in range(KT):
                        wait_freed(eng, ("dn", n, cb))

                def plain_add(cb, bank):
                    return v.tensor_tensor(resid[:, cb, :], resid[:, cb, :], bank, ALU.add)

                def gated(n, f, cols):
                    key = ("gu", n, f)
                    eng.wait_ge(sem("gate"), FT * n + f + 1)
                    v.tensor_tensor(act_value(f), gate_tmp(f), bank_of(key)[:, cols], ALU.mult).then_inc(sem("act_raw"), 1)

                def ffn(n, gname, between=lambda c: None):
                    norm_root((1, 4)[n])
                    norm_apply(resid, f"ffn{n}", lambda kt: pcol(gname, kt))
                    for f in range(FT):
                        ahead(f"gu{n}", f // 2, f % 2)
                        gated(n, f, slice(S, 2 * S))
                        between(f)

                for ap, value in ((one_col, 1.0), (eps_lnx, LNX_EPS), (eps_sub, SUBLN_EPS)):
                    own.go(v.memset(ap, value))
                v.memset(eps_norm, NORM_EPS).then_inc(sem("eps_ready"), 1)
                eng.wait_ge(sem("col_in"), 16)
                eng.wait_ge(sem("con_in"), 16)
                own.go(v.tensor_scalar(one_minus_ka, pcol("k_a", 0, 8), -1.0, 1.0, ALU.mult, ALU.add))
                split_to(1)
                norm_root(0)
                for kt in range(KT):
                    own.go(v.scalar_tensor_tensor(h_t[:, kt, :], resid[:, kt, :], pcol("g_mix0", kt), rstd[:, :], ALU.mult, ALU.mult))
                own.settle()
                own.go(v.tensor_tensor(hh_t[:, :, 1:S], h_t[:, :, 0:S - 1], h_t[:, :, 1:S], ALU.subtract))
                own.step(v.tensor_scalar(hh_t[:, :, 0:1], h_t[:, :, 0:1], -1.0, None, ALU.mult))

                def mix(m):
                    if m in buffers_free:
                        wait_full(eng, buffers_free[m])
                    for kt in range(KT):
                        emit(v.scalar_tensor_tensor(value_of(f"mix{m}")[:, kt, :], hh_t[:, kt, :], pcol("mu", 8 * mix_of[m] + kt), h_t[:, kt, :],
                                                    ALU.mult, ALU.add), kt)

                mix(0)
                lows("mix0")
                split_to(HIGHS)
                mix(1)
                ahead("k", 0, 0)
                mix(2)
                lows("mix1")
                ahead("k", 0, 1)
                lows("mix2")
                ahead("k", 1, 0)
                ahead("k", 1, 1)
                mix(3)
                lows("mix3")
                mix(4)
                lows("mix4")
                mix(5)
                ahead("lora1", 0, 1)
                eng.wait_ge(sem("part_raw"), part_value("mix5", 3))
                own.settle()
                for j in range(4):
                    wait_freed(eng, ("k", j))
                for kt in range(KT):
                    ins = v.tensor_scalar(kk_t[:, kt, :], k_t[:, kt, :], pcol("k_k", kt), None, ALU.mult)
                    own.go(ins) if kt < KT - 1 else ins.then_inc(sem("kk_ready"), 1)
                lows("mix5")
                for j in range(4):
                    key = ("l2g", j)
                    wait_full(eng, key)
                    release(v.tensor_copy(piece(g_t, j), bank_of(key)[:, :]), key)
                for j in range(4):
                    key = ("kksum", j)
                    wait_full(eng, key)
                    if j == 0:
                        wait_full(eng, ("kksum", 3))
                    release(v.tensor_scalar(piece(buf[1], j), bank_of(key)[:, :], 1e-24, None, ALU.max), key)
                    wait_freed(eng, key)
                    eng.sem_inc(sem("kk_floor"), 1)
                for cb in range(KT):
                    wait_freed(eng, ("l2", cb))
                eng.wait_ge(sem("scan_mask"), 1)
                own.step(v.tensor_tensor_scan(cum_t, grow_t, flat(w_t), 0.0, ALU.mult, ALU.add))
                ahead("r", 0, 0)
                cum_c = cum_t.rearrange("p (c t) -> p c t", t=P)
                mid3 = mid.unsqueeze(2)
                own.step(v.tensor_copy(mid3, cum_c[:, :, CH - 1:CH]))
                own.step(v.tensor_tensor(cum_c, cum_c, mid3.to_broadcast([P, 16, P]), ALU.subtract))
                cum_g = cum_t.rearrange("p (g c t) -> p g c t", c=2, t=P)
                mid_g = mid.rearrange("p (g c) -> p g c", c=2)
                own.go(v.tensor_tensor(send.unsqueeze(2), cum_g[:, :, 0, P - 1:P], mid_g[:, :, 1:2], ALU.add))
                v.tensor_tensor(flat(w_t), cum_t, flat(w_t), ALU.subtract).then_inc(sem("cum_ready"), 1)
                ahead("r", 0, 1)
                eng.wait_ge(sem("kk_root"), 1)
                own.step(v.reciprocal(flat(buf[1]), flat(buf[1])))
                ahead("r", 1, 0)
                v.tensor_tensor(flat(kk_t), flat(kk_t), flat(buf[1]), ALU.mult).then_inc(sem("kk_unit"), 1)
                eng.wait_ge(sem("kk_unit"), 1)
                own.step(v.tensor_tensor(flat(b_t), flat(kk_t), flat(a_t), ALU.mult))
                for kt in range(KT):
                    own.go(v.tensor_scalar(a_t[:, kt, :], a_t[:, kt, :], pcol("k_a", kt), one_minus_ka[:, kt:kt + 1], ALU.mult, ALU.add))
                own.settle()
                own.step(v.tensor_tensor(flat(k_t), flat(k_t), flat(a_t), ALU.mult))
                ahead("r", 1, 1)
                for j in range(4):
                    wait_freed(eng, ("r", j))
                for kt in range(KT):
                    v.scalar_tensor_tensor(a_t[:, kt, :], r_t[:, kt, :], pcol("r_k", kt), k_t[:, kt, :], ALU.mult, ALU.mult)\
                        .then_inc(sem("bonus_in"), 1)
                ahead("v", 0, 0)
                ahead("v", 0, 1)
                eng.wait_ge(sem("decay_a"), 1)
                v.scalar_tensor_tensor(flat(kk_t), flat(kk_t), -1.0, flat(w_t), ALU.mult, ALU.mult).then_inc(sem("tilde_ready"), 1)
                eng.wait_ge(sem("decay_bk"), 1)
                v.tensor_tensor(flat(b_t), flat(b_t), cum_t, ALU.mult).then_inc(sem("tilde_ready"), 1)
                eng.wait_ge(sem("bonus_in"), 8)
                v.tensor_tensor(flat(k_t), flat(k_t), cum_t, ALU.mult).then_inc(sem("tilde_ready"), 1)
                ahead("v", 1, 0)
                eng.wait_ge(sem("decay_r"), 1)
                v.tensor_tensor(flat(r_t), flat(r_t), grow_t, ALU.mult).then_inc(sem("tilde_ready"), 1)
                eng.wait_ge(sem("decay_s"), 1)
                ahead("v", 1, 1)
                wait_full(eng, ("v", 3))
                eng.wait_ge(sem("masks_in"), 16)
                for pair in PAIRS:
                    for g in pair:
                        for j in range(4):
                            key = ("sc", g, j)
                            wait_full(eng, key)
                            if g >= 2:
                                wait_full(eng, ("yt", g - 2))
                            release(v.tensor_tensor(scores[g % 2][:, j, :], bank_of(key)[:, :], const("score_mask", 0, 512), ALU.mult), key)
                    for g in pair:
                        nm, x, xt, y = (work[:, g % 2, i, :].rearrange("p (j n) -> p j n", j=4) for i in range(4))
                        eng.wait_ge(sem(f"nm_ready{g % 2}"), LEV * (g // 2) + 1)
                        v.tensor_tensor(x, nm, spread(ident, [P, 4, P]), ALU.add).then_inc(sem("x_ready"), 1)
                    for g in pair:
                        xt = work[:, g % 2, 2, :].rearrange("p (j n) -> p j n", j=4)
                        key = ("nt", g)
                        wait_full(eng, key)
                        release(v.tensor_tensor(xt, bank_of(key)[:, :].rearrange("p (j n) -> p j n", j=4), spread(ident, [P, 4, P]), ALU.add), key)
                    for l in range(1, LEV):
                        for what in ("dxt", "dx"):
                            if what == "dx" and l == LEV - 1:
                                continue
                            for g in pair:
                                key = (what, g, l)
                                z = work[:, g % 2, 2 if what == "dxt" else 1, :]
                                wait_full(eng, key)
                                if l == 1:
                                    wait_freed(eng, ("nt", g)) if what == "dxt" else eng.wait_ge(sem("x_ready"), g + 1)
                                else:
                                    wait_freed(eng, (what, g, l - 1))
                                release(v.tensor_tensor(z, z, bank_of(key)[:, :], ALU.add), key)
                    for g in pair:
                        key = ("st", g)
                        wait_full(eng, key)
                        release(v.scalar_tensor_tensor(work[:, g % 2, 0, 2 * P:3 * P], bank_of(key)[:, 0:P], send[:, g:g + 1],
                                                       const("head_sum"), ALU.mult, ALU.mult), key)
                for j in range(4):
                    wait_freed(eng, ("bonus", j))
                    wait_freed(eng, ("vt", j))
                own.step(v.tensor_tensor(flat(a_t), flat(a_t), flat(v_t), ALU.mult))
                for g in range(NG):
                    wait_freed(eng, ("yt", g))
                for j in range(4):
                    key = ("ymean", j)
                    wait_full(eng, key)
                    v.scalar_tensor_tensor(piece(y_t, j), bank_of(key)[:, :], -1.0 / CH, piece(y_t, j), ALU.mult, ALU.add)\
                        .then_inc(sem("y_centered"), 1)
                eng.wait_ge(sem("y_centered"), 4)
                for j in range(4):
                    eng.sem_inc(free[jobs[("ymean", j)][0]], 1)
                for j in range(4):
                    eng.wait_ge(sem("y_root"), j + 1)
                    two = (2 * j, 2 * j + 1)
                    for kt in two:
                        own.go(v.scalar_tensor_tensor(y_t[:, kt, :], y_t[:, kt, :], pcol("lnx_w", kt), y_sq[:, kt, :], ALU.mult, ALU.mult))
                    own.settle()
                    for kt in two:
                        own.go(v.scalar_tensor_tensor(y_t[:, kt, :], y_t[:, kt, :], pcol("lnx_b", kt), a_t[:, kt, :], ALU.add, ALU.add))
                    own.settle()
                    v.tensor_tensor(piece(y_t, j), piece(y_t, j), piece(g_t, j), ALU.mult).then_inc(sem("part_raw"), 1)
                    if j:
                        low_piece("y", j - 1)
                low_piece("y", 3)
                add_resid("o")

                def modulation(n):
                    c, half = n // 2, n % 2
                    eng.wait_ge(sem(f"ada_in{half}"), 16 * (c + 1))
                    if n == 0:
                        eng.wait_ge(sem("silu_c"), 1)
                    if c >= 2 and not half:
                        wait_full(eng, ("ada", c - 2))
                    acc = ada_acc(c)
                    both = range(2 if c < 4 else 1)
                    for k in range(KT // 2):
                        kt = KT // 2 * half + k
                        for which in both:
                            s_ = silu_c[:, kt, which:which + 1]
                            if kt == 0:
                                ins = v.tensor_scalar(acc[:, which, :], ada_w(half)[:, k, :], s_, None, ALU.mult)
                            else:
                                ins = v.scalar_tensor_tensor(acc[:, which, :], ada_w(half)[:, k, :], s_, acc[:, which, :], ALU.mult, ALU.add)
                            if k == KT // 2 - 1 and which == both[-1]:
                                ins.then_inc(sem("ada_read"), 1)
                                eng.wait_ge(sem("ada_read"), n + 1)
                            else:
                                own.go(ins)
                        own.settle()

                def modulation_out(c):
                    key = ("ada", c)
                    wait_full(eng, key)
                    n = 2 if c < 4 else 1
                    release(v.tensor_tensor(ada[:, 4 * c:4 * c + 4, 0:n], bank_of(key)[:, 0:8].rearrange("p (e c) -> p e c", c=2)[:, :, 0:n],
                                            pcol("b_ada", 4 * c, 4).unsqueeze(2).to_broadcast([P, 4, n]), ALU.add), key)

                def gain_of(i, which, part, g):
                    own.step(v.scalar_tensor_tensor(gain[:, 8 * i:8 * i + 8].unsqueeze(2), ada[:, 8 * part:8 * part + 8, which:which + 1], 1.0,
                                                    pcol(g, 0, 8).unsqueeze(2), ALU.add, ALU.mult))

                def modulated(src, name, i, which, part):
                    for j in range(4):
                        for kt in (2 * j, 2 * j + 1):
                            own.go(v.scalar_tensor_tensor(value_of(name)[:, kt, :], src[:, kt, :], gain[:, 8 * i + kt:8 * i + kt + 1], rstd[:, :],
                                                          ALU.mult, ALU.mult))
                        if j:
                            low_piece(name, j - 1)
                        own.settle()
                        for kt in (2 * j, 2 * j + 1):
                            emit(v.tensor_scalar(value_of(name)[:, kt, :], value_of(name)[:, kt, :], ada[:, 8 * part + kt, which:which + 1], None,
                                                 ALU.add), kt)
                    low_piece(name, 3)

                def side0(f):
                    for n in ([f] if f < 20 else [2 * f - 20, 2 * f - 19]):
                        modulation(n)
                    if f % 2 and f >= 5:
                        modulation_out(f // 2 - 2)

                ffn(0, "g_ffn0", side0)
                modulation_out(9)
                for half in range(2):
                    ahead("dn0", 0, half)
                modulation_out(10)
                modulation_out(11)
                gain_of(2, 1, 1, "norm_mix")
                norm_root(2)
                modulated(ctx_r, "hc", 2, 1, 0)
                down_resid(0, plain_add)
                wait_freed(eng, ("ada", 11))
                gain_of(0, 0, 1, "norm_mix")
                gain_of(1, 0, 4, "norm_ffn")
                norm_root(3)
                norm_apply(resid, "hkv", lambda kt: pcol("kv_g", kt))
                norm_apply(resid, "hq", lambda kt: pcol("g_mix1", kt))
                eng.wait_ge(sem("lam_rows_in"), 16)
                lam4 = prow("lam").rearrange("p (a b n) -> p a b n", a=2, b=2)
                own.step(v.tensor_tensor(lam_tmp, lam4[:, :, 0, :], lam4[:, :, 1, :], ALU.mult))
                v.tensor_reduce(lam_t, lam_tmp, AXX, ALU.add).then_inc(sem("lam_in"), 1)
                own.go(v.tensor_scalar(sub_col, pcol("subln"), 1.0 - LAM_INIT, None, ALU.mult))
                for name in ("ak", "aq"):
                    for j in range(4):
                        ahead(name, j // 2, j % 2)

                def head_norm(i):
                    z, rs = (ak_t, aq_t)[i], (k_sq, q_sq)[i]
                    eng.wait_ge(sem("head_root"), 4 * i + 4)
                    v.scalar_tensor_tensor(flat(z), flat(z), pcol(("k_norm", "q_norm")[i]), flat(rs), ALU.mult, ALU.mult)\
                        .then_inc(sem("head_normed"), 1)
                    eng.wait_ge(sem("head_normed"), i + 1)

                def rope(i):
                    z, name = (ak_t, aq_t)[i], ("akrot", "aqrot")[i]
                    for j in range(4):
                        key = (name, j)
                        wait_full(eng, key)
                        release(v.tensor_tensor(turn_t[:, 2 * j:2 * j + 2, :], bank_of(key)[:, :].rearrange("p (a n) -> p a n", a=2),
                                                spread(const("sin", 0, S), [P, 2, S]), ALU.mult), key)
                    own.step(v.tensor_tensor(z[:, :, :], z[:, :, :], spread(const("cos", 0, S), [P, KT, S]), ALU.mult))
                    for j in range(4):
                        wait_freed(eng, (name, j))
                    v.tensor_tensor(flat(z), flat(z), flat(turn_t), ALU.add).then_inc(sem("roped"), 1)
                    eng.wait_ge(sem("roped"), i + 1)

                head_norm(0)
                head_norm(1)
                ahead("av", 0, 0)
                ahead("av", 0, 1)
                rope(0)
                ahead("av", 1, 0)
                rope(1)
                ahead("av", 1, 1)
                eng.wait_ge(sem("lam_exp"), 1)
                own.step(v.tensor_scalar(neg_lam, lam_t[:, 1:2], lam_t[:, 0:1], -LAM_INIT, ALU.subtract, ALU.add))

                def attend_scores(h):
                    for i in range(2):
                        key = ("s", h, i)
                        wait_full(eng, key)
                        if h >= 2:
                            wait_full(eng, ("pt", h - 2))
                        release(v.scalar_tensor_tensor(prob[:, h % 2, i, 0:3 * P], bank_of(key)[:, 0:3 * P], ISS,
                                                       const("chunk_mask", 0, 3 * P), ALU.mult, ALU.add), key)
                    for i in range(2):
                        wait_freed(eng, ("s", h, i))
                    for qt in range(2):
                        own.go(v.tensor_reduce(mx[:, h % 2, 2 * qt:2 * qt + 2], prob[:, h % 2, :, Q_COLS[qt]], AXX, ALU.max))
                    own.settle()
                    v.tensor_scalar(mx[:, h % 2, :], mx[:, h % 2, :], -1.0, None, ALU.mult).then_inc(sem("max_ready"), 2)

                def attend_probs(h):
                    eng.wait_ge(sem("exp_done"), 4 * h + 4)
                    own.step(v.reciprocal(sums[:, h % 2, :], sums[:, h % 2, :]))
                    odd = sums[:, h % 2, :].rearrange("p (q i) -> p q i", i=2)[:, :, 1:2]
                    own.step(v.tensor_scalar(odd, odd, neg_lam, None, ALU.mult))
                    for qt in range(2):
                        p0 = prob[:, h % 2, 0, Q_COLS[qt]]
                        own.go(v.tensor_scalar(p0, p0, sums[:, h % 2, 2 * qt:2 * qt + 1], None, ALU.mult))
                    own.settle()
                    for qt in range(2):
                        p0, p1 = (prob[:, h % 2, i, Q_COLS[qt]] for i in range(2))
                        v.scalar_tensor_tensor(p0, p1, sums[:, h % 2, 2 * qt + 1:2 * qt + 2], p0, ALU.mult, ALU.add)\
                            .then_inc(sem("prob_ready"), 1)

                def attend_out(h):
                    wait_full(eng, ("ao", h))
                    release(v.tensor_copy(ao_t[:, h, :], bank_of(("ao", h))[:, 0:S]), ("ao", h))

                for h in range(8):
                    attend_scores(h)
                    if h >= 1:
                        attend_probs(h - 1)
                    if h < 6:
                        ahead("ctx", h // 2, h % 2)
                    if h >= 2:
                        attend_out(h - 2)

                def scale_heads(j):
                    eng.wait_ge(sem("ao_root"), j + 1)
                    for kt in (2 * j, 2 * j + 1):
                        emit(v.scalar_tensor_tensor(ao_t[:, kt, :], ao_t[:, kt, :], sub_col, ao_sq[:, kt, :], ALU.mult, ALU.mult), kt)

                attend_probs(7)
                attend_out(6)
                scale_heads(0)
                scale_heads(1)
                attend_out(7)
                low_piece("ao", 0)
                scale_heads(2)
                low_piece("ao", 1)
                scale_heads(3)
                low_piece("ao", 2)
                low_piece("ao", 3)
                add_resid("awo")

                def side1(f):
                    c = f // 2 if f % 2 else -1
                    if c == 0:
                        for d in range(2):
                            for t in range(TT):
                                wait_freed(eng, ("ctx", d, t))
                                wait_full(eng, ("ctx", 2, t))
                        v.scalar_tensor_tensor(c_log, cf, -1.0, cf, ALU.mult, ALU.max).then_inc(sem("gate_abs"), 1)
                    if c == 2:
                        eng.wait_ge(sem("gate_log1p"), 1)
                        eng.wait_ge(sem("gate_k"), 1)
                        v.scalar_tensor_tensor(cf, cf, 0.0, c_log, ALU.min, ALU.subtract).then_inc(sem("ctx_log"), 1)
                    if c == 6:
                        for d in range(2):
                            for t in range(TT):
                                wait_freed(eng, ("csum", d, t))
                        v.tensor_tensor(ck, ck, cf, ALU.mult).then_inc(sem("ctx_k"), 1)

                ffn(1, "g_ffn1", side1)
                down_resid(1, plain_add)
                norm_root(5)
                modulated(resid, "hx", 0, 0, 0)
                for d in range(2):
                    for j in range(2):
                        ahead("in", d, j)
                for d in range(2):
                    for t in range(TT):
                        wait_freed(eng, ("in", d, t))
                xf, x_log = flat(f_x), flat(suf_t)
                v.scalar_tensor_tensor(x_log, xf, -1.0, xf, ALU.mult, ALU.max).then_inc(sem("gate_abs"), 1)
                eng.wait_ge(sem("gate_log1p"), 2)
                eng.wait_ge(sem("gate_k"), 2)
                own.step(v.scalar_tensor_tensor(xf, xf, 0.0, x_log, ALU.min, ALU.subtract))
                own.go(v.tensor_copy(pre_t[:, 0:4, :], f_x[:, 0:4, :]))
                own.go(v.memset(pre_t[:, 4:8, :], 0.0))
                own.go(v.memset(suf_t[:, 0:4, :], 0.0))
                v.tensor_copy(suf_t[:, 4:8, :], f_x[:, 4:8, :]).then_inc(sem("sums_ready"), 1)
                eng.wait_ge(sem("sums_ready"), 1)
                for j in range(2):
                    ahead("in", 2, j)
                for j in range(2):
                    wait_freed(eng, ("in", 2, j))
                own.step(v.tensor_scalar(q_x, q_x, HG_SCALE, None, ALU.mult))
                v.tensor_tensor(qd_t[:, 0:4, :], k_x[:, 0:4, :], k_x[:, 4:8, :], ALU.add).then_inc(sem("diag_ready"), 1)
                q_v = lambda b: q_x.rearrange("p h (n r b) -> p (h n) r b", r=2, b=b)

                def level_weights(l):
                    b = 1 << l
                    eng.wait_ge(sem("wgt_exp"), 2 * l + 2)
                    for d in range(2):
                        wl, wr = halves(wgt[l % 2], d, b)
                        kl, kr = halves(k_x, d, b)
                        left, right = (kl, q_v(b)[:, :, 1, :]) if d == 0 else (q_v(b)[:, :, 0, :], kr)
                        own.go(v.tensor_tensor(wl, wl, left, ALU.mult))
                        ins = v.tensor_tensor(wr, wr, right, ALU.mult)
                        own.go(ins) if d == 0 else ins.then_inc(sem("wgt_ready"), 1)

                def take_scores(l):
                    for t in range(TT):
                        for d in range(2):
                            key = ("lv", l, d, t)
                            wait_full(eng, key)
                            if d:
                                wait_freed(eng, ("lv", l, 0, t))
                            mask = const("left_right" if d == 0 else "right_left", l * P)
                            release(v.copy_predicated(st_v[:, t, :, t * P:(t + 1) * P], spread(mask, [P, HG, P]).bitcast(I32),
                                                      bank_of(key)[:, :].rearrange("p (h n) -> p h n", h=HG)), key)
                    for t in range(TT):
                        wait_freed(eng, ("lv", l, 1, t))

                level_weights(0)
                for t in range(TT):
                    key = ("diag", t)
                    wait_full(eng, key)
                    release(v.tensor_tensor(st_v[:, t, :, t * P:(t + 1) * P], bank_of(key)[:, :].rearrange("p (h n) -> p h n", h=HG),
                                            spread(ident, [P, HG, P]), ALU.mult), key)
                    wait_freed(eng, key)
                level_weights(1)
                for d in range(3, 7):
                    for half in range(2):
                        ahead("in", d, half)
                        l = 2 * (d - 3) + half
                        if l < LEV:
                            take_scores(l)
                        if l + 2 <= LEV:
                            level_weights(l + 2)
                for d in range(2):
                    key = ("cross", d)
                    wait_full(eng, key)
                    release(v.tensor_copy(st_v[:, d, :, (1 - d) * P:(2 - d) * P], bank_of(key)[:, :].rearrange("p (h n) -> p h n", h=HG)), key)
                eng.wait_ge(sem("qd_exp"), 2)
                own.go(v.tensor_tensor(qd_t[:, 0:4, :], qd_t[:, 0:4, :], q_x, ALU.mult))
                v.tensor_tensor(qd_t[:, 4:8, :], qd_t[:, 4:8, :], q_x, ALU.mult).then_inc(sem("qd_ready"), 1)
                eng.wait_ge(sem("gelu_done"), 1)
                vv4 = vv_x.rearrange("p t (h n) -> p t h n", h=HG)
                for i in range(8):
                    own.go(v.bn_stats(bn[:, i, :], vv4[:, i // 4, i % 4, :]))
                own.settle()
                for i in range(8):
                    own.go(v.bn_aggr(bna[:, i, :], bn[:, i, :]))
                own.settle()
                v.tensor_scalar(bna[:, :, 1:2], bna[:, :, 1:2], NORM_EPS, None, ALU.add).then_inc(sem("vv_var"), 1)
                eng.wait_ge(sem("vv_root"), 1)
                own.step(v.reciprocal(bna[:, :, 1:2], bna[:, :, 1:2]))
                for i in range(8):
                    z = vv4[:, i // 4, i % 4, :]
                    own.go(v.tensor_scalar(z, z, bna[:, i, 0:1], bna[:, i, 1:2], ALU.subtract, ALU.mult))
                own.settle()
                eng.wait_ge(sem("rows_in"), 16)
                own.step(v.tensor_tensor(vv_x, vv_x, spread(prow("sgu_g"), [P, TT, 512]), ALU.mult))
                v.tensor_tensor(vv_x, vv_x, spread(prow("sgu_b"), [P, TT, 512]), ALU.add).then_inc(sem("vv_ready"), 1)
                eng.wait_ge(sem("gate_x"), 1)
                for j in range(2):
                    eng.wait_ge(sem("go_root"), j + 1)
                    for h in (2 * j, 2 * j + 1):
                        own.go(v.scalar_tensor_tensor(o_t[:, h, :], o_t[:, h, :], pcol("hg_norm", h), o_sq[:, h, :], ALU.mult, ALU.mult))
                    own.settle()
                    two = slice(2 * j, 2 * j + 2)
                    v.tensor_tensor(mix_t[:, two, :], o_t[:, two, :], gate_x[:, two, :], ALU.mult).then_inc(sem("part_raw"), 1)
                for j in range(2):
                    key = ("z", j)
                    wait_full(eng, key)
                    for i in range(2):
                        h = 2 * j + i
                        dst = mix_t[:, HG + h, :].rearrange("p (t n) -> p t n", t=TT)
                        ins = v.tensor_tensor(dst, bank_of(key)[:, i * S:(i + 1) * S].rearrange("p (t n) -> p t n", t=TT),
                                              spread(prow("b_spatial")[:, h * P:(h + 1) * P], [P, TT, P]), ALU.add)
                        own.go(ins) if i == 0 else release(ins, key)
                for j in range(2):
                    wait_freed(eng, ("z", j))
                    v.tensor_tensor(mix_t[:, HG + 2 * j:HG + 2 * j + 2, :], mix_t[:, HG + 2 * j:HG + 2 * j + 2, :], u_x[:, 2 * j:2 * j + 2, :],
                                    ALU.mult).then_inc(sem("part_raw"), 1)
                lows("mix")
                for j in range(4):
                    key = ("mo", j)
                    ahead("mo", j // 2, j % 2)
                    wait_full(eng, key)
                    for i in range(2):
                        kt = 2 * j + i
                        ins = v.scalar_tensor_tensor(resid[:, kt, :], bank_of(key)[:, i * S:(i + 1) * S], ada[:, 16 + kt, 0:1], resid[:, kt, :],
                                                     ALU.mult, ALU.add)
                        own.go(ins) if i == 0 else release(ins, key)
                for j in range(4):
                    wait_freed(eng, ("mo", j))
                norm_root(6)
                modulated(resid, "ffn2", 1, 0, 3)
                eng.wait_ge(sem("pads_zero"), 1)
                for f in range(FT):
                    ahead("gu2", f // 2, f % 2)
                    acc = gate_tmp(f).rearrange("p (r c) -> p r c", c=GRID)
                    eng.wait_ge(sem("grid_in"), f + 1)
                    eng.wait_ge(sem("tap_in"), f + 1)
                    for n, (i, j) in enumerate(TAPS):
                        if (i, j) == (1, 1):
                            continue
                        view = grid(f)[:, i:i + ROWS_X, j:j + GRID]
                        ins = v.scalar_tensor_tensor(acc, view, pcol("conv_w", 9 * f + n), acc, ALU.mult, ALU.add)
                        own.step(ins) if n < 8 else ins.then_inc(sem("conv_done"), 1)
                    if f >= 1:
                        gated(2, f - 1, slice(0, S))
                gated(2, FT - 1, slice(0, S))
                down_resid(2, lambda cb, bank: v.scalar_tensor_tensor(resid[:, cb, :], bank, ada[:, 40 + cb, 0:1], resid[:, cb, :],
                                                                     ALU.mult, ALU.add))
                norm_root(7)
                for kt in range(KT):
                    v.scalar_tensor_tensor(resid[:, kt, :], resid[:, kt, :], pcol("norm_final", kt), rstd[:, :], ALU.mult, ALU.mult)\
                        .then_inc(sem("out_ready"), 1)


def constants():
    z = {}
    i, j = np.arange(P)[:, None], np.arange(P)[None, :]
    z["ident"] = i == j
    lv = [((i >> (l + 1)) == (j >> (l + 1))) & ((i >> l) & 1 == 1) & ((j >> l) & 1 == 0) for l in range(LEV)]
    z["right_left"] = np.concatenate(lv, 1)
    z["left_right"] = np.concatenate([m.T for m in lv], 1)
    z["score_mask"] = np.concatenate([i > j, i <= j, i < j, i <= j], 1)
    z["head_sum"] = i // CH == j // CH
    z["ones"] = np.ones((P, P))
    rope, half = CH // 4, CH // 8
    ci, cj = i % CH, j % CH
    swap = np.zeros((P, P), np.float32)
    swap[(i // CH == j // CH) & (cj < half) & (ci == cj + half)] = -1.0
    swap[(i // CH == j // CH) & (cj >= half) & (cj < rope) & (ci == cj - half)] = 1.0
    z["rope_swap"] = swap
    inv = np.power(np.float32(500000.0), -np.arange(0, rope, 2, dtype=np.float32) / np.float32(rope)).astype(np.float32)
    ang = (np.arange(S, dtype=np.float32)[:, None] * inv[None, :]).astype(np.float32)
    cos, sin = np.ones((P, S), np.float32), np.zeros((P, S), np.float32)
    for c in range(P):
        if c % CH < rope:
            cos[c], sin[c] = np.cos(ang[:, c % half]), np.sin(ang[:, c % half])
    z["cos"], z["sin"] = cos, sin
    mask = np.zeros((P, 3 * P), np.float32)
    mask[0:CH, CH:P] = mask[0:CH, 2 * P + CH:3 * P] = -1e30
    z["chunk_mask"] = mask
    return np.ascontiguousarray(np.concatenate([np.asarray(z[n], np.float32) for n, _ in CONS], 1))


def by_channel(v):
    v = np.asarray(v)
    v = v.reshape(-1, v.shape[-1] // P, P)
    return v.transpose(2, 0, 1).reshape(P, -1)


def wide_chunks(w):
    w = np.asarray(w)
    n = w.shape[1] // 512
    return w.reshape(KT, P, n, 512).transpose(2, 1, 0, 3).reshape(n, P, CHUNK)


def pair_chunks(w):
    w = np.asarray(w).reshape(KT, P, 2, FT // 2, 2, P)
    return w.transpose(3, 1, 0, 4, 2, 5).reshape(FT // 2, P, CHUNK)


def down_chunks(w):
    w = np.asarray(w).reshape(FT, P, KT, P)
    return w.transpose(2, 1, 0, 3).reshape(KT, P, FT * P)


def layout(x):
    g = {k: np.asarray(v) for k, v in x.items()}
    lora1 = np.zeros((1, P, CHUNK), np.float32)
    l1 = np.concatenate([g["rw_w1"][0], g["rw_a1"][0], g["rw_g1"][0]], 1)
    lora1[0, :, 0:KT * 288] = l1.reshape(KT, P, 288).transpose(1, 0, 2).reshape(P, -1)
    lora2 = np.zeros((1, P, 4, D), np.float32)
    lora2[0, 0:64, 0], lora2[0, 0:64, 1] = g["rw_w2"][0], g["rw_a2"][0]
    lora2[0, :, 2], lora2[0, 0:32, 3] = g["rw_g2"][0][0:P], g["rw_g2"][0][P:]
    wide = [lora1, lora2.reshape(1, P, CHUNK)]
    wide += [wide_chunks(g[n][0]) for n in ("rw_w_k", "rw_w_r", "rw_w_v", "rw_w_o")]
    wide += [pair_chunks(g["ffn_w_gu"][0]), wide_chunks(g["kv_w"]), wide_chunks(g["da_w_q"][0]), wide_chunks(g["da_w_o"][0])]
    wide += [pair_chunks(g["ffn_w_gu"][1]), wide_chunks(g["w_ada_2"][0]), wide_chunks(g["w_in_2"][0]), wide_chunks(g["w_out_2"][0])]
    wide += [pair_chunks(g["w_up_2"][0])]
    down = [down_chunks(g["ffn_w_down"][0]), down_chunks(g["ffn_w_down"][1]), down_chunks(g["w_down_2"][0])]
    twice = lambda v: np.concatenate([v.reshape(1, CH)] * 2, 1)
    c2 = np.stack([g["c_2"][0], g["c_ctx_2"]], 0).reshape(2, KT, P).transpose(2, 1, 0).reshape(P, 16)
    cw = g["conv_w_2"][0].reshape(9, FT, P).transpose(2, 1, 0).reshape(P, 9 * FT)
    cols = {"g_mix0": g["g_mix"][0], "g_mix1": g["g_mix"][1], "g_ffn0": g["g_ffn"][0], "g_ffn1": g["g_ffn"][1], "mu": g["rw_mu"][0],
            "w0": g["rw_w0"], "a0": g["rw_a0"], "k_k": g["rw_k_k"], "k_a": g["rw_k_a"], "r_k": g["rw_r_k"].reshape(1, D),
            "lnx_w": g["rw_lnx_w"], "lnx_b": g["rw_lnx_b"], "kv_g": g["kv_g"], "norm_mix": g["norm_mix_2"], "norm_ffn": g["norm_ffn_2"],
            "norm_final": g["norm_final_2"], "k_norm": twice(g["k_norm_g"]), "q_norm": twice(g["da_q_norm_g"]), "subln": g["da_subln_g"],
            "hg_norm": g["hg_norm_2"], "conv_b": g["conv_b_2"], "b_ada": g["b_ada_2"]}
    cols = {n: by_channel(v) for n, v in cols.items()}
    cols["conv_w"], cols["c"] = cw, c2
    rows = np.concatenate([g["sgu_norm_g_2"][0], g["sgu_norm_b_2"][0], g["b_spatial_2"][0].reshape(-1),
                           g["da_lam_q1"][0], g["da_lam_k1"][0], g["da_lam_q2"][0], g["da_lam_k2"][0]])
    tr = lambda v: v.reshape(S, KT, P).transpose(2, 1, 0)
    made = {"wide": np.concatenate(wide, 0), "down": np.concatenate(down, 0), "x_t": tr(g["x"]), "ctx_t": tr(g["ctx_2"]),
            "cols": np.concatenate([cols[n] for n, _ in COLS], 1), "cons": constants(), "rows": rows.reshape(1, NROW),
            "w_sp": g["w_spatial_2"][0].transpose(2, 0, 1).reshape(P, 512)}
    return {n: np.ascontiguousarray(v) for n, v in made.items()}


def kernel(**inputs):
    import concourse.bacc as _bacc
    from concourse.bass_utils import run_bass_kernel_spmd as _run

    nc = _bacc.Bacc("TRN2", target_bir_lowering=False, num_devices=1)
    arrays = layout(inputs)
    args = {n: nc.dram_tensor(f"in_{n}", a.shape, F32, kind="ExternalInput").ap() for n, a in arrays.items()}
    out = nc.dram_tensor("out_t", (P, KT, S), F32, kind="ExternalOutput").ap()
    build(nc, out=out, **args)
    r = _run(nc, [{f"in_{n}": a for n, a in arrays.items()}], core_ids=[0])
    y = np.asarray(r.results[0]["out_t"])
    return np.ascontiguousarray(y.transpose(2, 1, 0).reshape(1, S, D))
```
